# Optimizing a Trainium2 kernel written in Bass

```python
import math
import jax, jax.numpy as jnp
from jax import lax
import numpy as np

D_MODEL = 1024
BATCH = 1
SEQ = 1024
DEPTH = 1

CTX_LEN = 256
GRID_W = 64
HEAD_DIM = 64
HY_WIDTH = D_MODEL // 4
GQA_HEADS = (D_MODEL // 2) // HEAD_DIM
GQA_KV_HEADS = 2
NA_HEADS = (D_MODEL // 4) // HEAD_DIM
NA_KH = 8
NA_KW = 16
Q_BLOCK = 128
ROPE_THETA = 10000.0
HY_EMB_DIM = 33
HY_FILTER_WIDTH = 64
HY_SHORT = 3
HY_DECAY_TARGET = 1e-2
HY_FAST_DECAY = 0.3
HY_SLOW_DECAY = 1.5
FFN_HIDDEN = int(math.ceil(8 * D_MODEL / 3 / 256)) * 256
NORM_EPS = 1e-6
ATTN_SCALE = HEAD_DIM ** -0.5

HY_COLS = 3 * HY_WIDTH
GQA_Q_COLS = GQA_HEADS * HEAD_DIM
GQA_KV_COLS = GQA_KV_HEADS * HEAD_DIM
NA_COLS = NA_HEADS * HEAD_DIM
IN_COLS = HY_COLS + GQA_Q_COLS + 2 * GQA_KV_COLS + 3 * NA_COLS
MIX_WIDTH = HY_WIDTH + GQA_Q_COLS + NA_COLS
SPLIT_POINTS = [int(v) for v in np.cumsum([HY_COLS, GQA_Q_COLS, GQA_KV_COLS, GQA_KV_COLS, NA_COLS, NA_COLS])]

kernel_name = 'hybrid_hyena_gqa_natten_dit'

def rms_norm(x, g):
    xf = x.astype(jnp.float32)
    y = xf * lax.rsqrt(jnp.mean(xf * xf, axis=-1, keepdims=True) + NORM_EPS)
    return (y * g.astype(jnp.float32)).astype(x.dtype)

def modulate(h, shift, scale):
    return h * (1 + scale) + shift

def axial_rope_tables(L):
    pos = jnp.arange(L)
    row = (pos // GRID_W).astype(jnp.float32)
    col = (pos % GRID_W).astype(jnp.float32)
    n_f = HEAD_DIM // 4
    inv = ROPE_THETA ** (-jnp.arange(n_f, dtype=jnp.float32) / n_f)
    ang = jnp.concatenate([row[:, None] * inv, col[:, None] * inv], axis=-1)
    return jnp.cos(ang), jnp.sin(ang)

def apply_rope(x, cos, sin):
    x1, x2 = jnp.split(x, 2, axis=-1)
    c = cos[None, :, None, :]
    s = sin[None, :, None, :]
    return jnp.concatenate([x1 * c - x2 * s, x1 * s + x2 * c], axis=-1).astype(x.dtype)

def split_proj(p):
    B, L, _ = p.shape
    hy, q, k, v, nq, nk, nv = jnp.split(p, SPLIT_POINTS, axis=-1)
    return (hy,
            q.reshape(B, L, GQA_HEADS, HEAD_DIM),
            k.reshape(B, L, GQA_KV_HEADS, HEAD_DIM),
            v.reshape(B, L, GQA_KV_HEADS, HEAD_DIM),
            nq.reshape(B, L, NA_HEADS, HEAD_DIM),
            nk.reshape(B, L, NA_HEADS, HEAD_DIM),
            nv.reshape(B, L, NA_HEADS, HEAD_DIM))

def attend(q, k, v):
    B, Lq, H, hd = q.shape
    kvh = k.shape[2]
    qg = q.reshape(B, Lq, kvh, H // kvh, hd)
    s = jnp.einsum('bqkgd,bskd->bkgqs', qg, k).astype(jnp.float32) * ATTN_SCALE
    p = jax.nn.softmax(s, axis=-1).astype(v.dtype)
    o = jnp.einsum('bkgqs,bskd->bqkgd', p, v)
    return o.reshape(B, Lq, H * hd)

def gqa_latent(q, k, v):
    B, S, H, hd = q.shape
    nb = S // Q_BLOCK
    qb = jnp.moveaxis(q.reshape(B, nb, Q_BLOCK, H, hd), 1, 0)
    o = lax.map(lambda qi: attend(qi, k, v), qb)
    return jnp.moveaxis(o, 0, 1).reshape(B, S, H * hd)

def natten_latent(q, k, v, kc, vc, rpb):
    B, S, H, hd = q.shape
    rows = S // GRID_W
    kh = min(NA_KH, rows)
    kw = NA_KW
    qg = q.reshape(B, rows, GRID_W, H, hd)
    kg = k.reshape(B, rows, GRID_W, H, hd)
    vg = v.reshape(B, rows, GRID_W, H, hd)
    cols = jnp.arange(GRID_W)
    cs = jnp.clip(cols - kw // 2, 0, GRID_W - kw)
    key_cols = cs[:, None] + jnp.arange(kw)[None, :]
    dcol = key_cols - cols[:, None] + (NA_KW - 1)

    def row_block(r):
        rs = jnp.clip(r - kh // 2, 0, rows - kh)
        kr = lax.dynamic_slice_in_dim(kg, rs, kh, axis=1)
        vr = lax.dynamic_slice_in_dim(vg, rs, kh, axis=1)
        kwin = kr[:, :, key_cols]
        vwin = vr[:, :, key_cols]
        qr = lax.dynamic_index_in_dim(qg, r, axis=1, keepdims=False)
        drow = rs + jnp.arange(kh) - r + (NA_KH - 1)
        bias = rpb[:, drow[None, :, None], dcol[:, None, :]]
        s_loc = jnp.einsum('bwhd,biwjhd->bhwij', qr, kwin).astype(jnp.float32) * ATTN_SCALE
        s_loc = (s_loc + bias.astype(jnp.float32)).reshape(B, H, GRID_W, kh * kw)
        s_ctx = jnp.einsum('bwhd,bchd->bhwc', qr, kc).astype(jnp.float32) * ATTN_SCALE
        p = jax.nn.softmax(jnp.concatenate([s_loc, s_ctx], axis=-1), axis=-1).astype(v.dtype)
        p_loc = p[..., :kh * kw].reshape(B, H, GRID_W, kh, kw)
        p_ctx = p[..., kh * kw:]
        return (jnp.einsum('bhwij,biwjhd->bwhd', p_loc, vwin)
                + jnp.einsum('bhwc,bchd->bwhd', p_ctx, vc))

    o = lax.map(row_block, jnp.arange(rows))
    return jnp.moveaxis(o, 0, 1).reshape(B, S, H * hd)

def hyena_filter(L, w1, b1, w2, b2, w3, b3, w_out, freq):
    f32 = jnp.float32
    t = jnp.linspace(0.0, 1.0, L, dtype=f32)[:, None]
    bands = (HY_EMB_DIM - 1) // 2
    w = 2.0 * math.pi * jnp.arange(L, dtype=f32)[:, None] / L
    fr = jnp.linspace(1e-4, bands - 1, bands, dtype=f32)[None, :]
    z = jnp.concatenate([t, jnp.cos(fr * w), -jnp.sin(fr * w)], axis=-1)
    om = freq.astype(f32)
    h = jnp.sin(om * (z @ w1.astype(f32) + b1.astype(f32)))
    h = jnp.sin(om * (h @ w2.astype(f32) + b2.astype(f32)))
    h = jnp.sin(om * (h @ w3.astype(f32) + b3.astype(f32)))
    h = h @ w_out.astype(f32)
    deltas = jnp.linspace(math.log(HY_DECAY_TARGET) / HY_SLOW_DECAY,
                          math.log(HY_DECAY_TARGET) / HY_FAST_DECAY, HY_WIDTH, dtype=f32)
    decay = jnp.exp(-t * jnp.abs(deltas))
    h_fwd = h[:, :HY_WIDTH] * decay
    h_bwd = h[:, HY_WIDTH:] * decay
    return jnp.concatenate([h_fwd, jnp.zeros((1, HY_WIDTH), f32), h_bwd[:0:-1]], axis=0)

def fft_long_conv(u, filt2):
    L = u.shape[1]
    uf = jnp.fft.rfft(u.astype(jnp.float32), n=2 * L, axis=1)
    ff = jnp.fft.rfft(filt2, n=2 * L, axis=0)
    y = jnp.fft.irfft(uf * ff[None], n=2 * L, axis=1)[:, :L]
    return y.astype(u.dtype)

def short_conv(u, w, b):
    L = u.shape[1]
    pad = HY_SHORT // 2
    up = jnp.pad(u, ((0, 0), (pad, HY_SHORT - 1 - pad), (0, 0)))
    return sum(up[:, i:i + L] * w[i] for i in range(HY_SHORT)) + b

def hyena_mixer(u, filt2, conv_w, conv_b, skip):
    u = short_conv(u, conv_w, conv_b)
    v, x1, x2 = jnp.split(u, 3, axis=-1)
    v = v * x1
    return x2 * (fft_long_conv(v, filt2) + v * skip)

def swiglu(h, w_in_ffn, w_out_ffn):
    g, u = jnp.split(h @ w_in_ffn, 2, axis=-1)
    return (jax.nn.silu(g) * u) @ w_out_ffn

def setup_inputs(seed: int = 0) -> dict:
    key = jax.random.key(seed)
    ks = iter(jax.random.split(key, 32))

    def nrm(shape, s):
        return jax.random.normal(next(ks), shape, jnp.float32) * s

    D = D_MODEL
    L = DEPTH
    F = HY_FILTER_WIDTH
    return {
        'x': nrm((BATCH, SEQ, D), 1.0),
        'c': nrm((BATCH, D), 1.0),
        'ctx': nrm((BATCH, CTX_LEN, D), 1.0),
        'c_ctx': nrm((D,), 1.0),
        'w_mod': nrm((L, D, 6 * D), 0.5 * D ** -0.5),
        'b_mod': nrm((L, 6 * D), 0.02),
        'g_mix': 1.0 + nrm((L, D), 0.05),
        'g_ffn': 1.0 + nrm((L, D), 0.05),
        'w_in': nrm((L, D, IN_COLS), D ** -0.5),
        'w_out': nrm((L, MIX_WIDTH, D), MIX_WIDTH ** -0.5),
        'hy_conv_w': nrm((L, HY_SHORT, HY_COLS), 0.5),
        'hy_conv_b': nrm((L, HY_COLS), 0.02),
        'hy_f_w1': nrm((L, HY_EMB_DIM, F), HY_EMB_DIM ** -0.5),
        'hy_f_b1': nrm((L, F), 0.1),
        'hy_f_w2': nrm((L, F, F), F ** -0.5),
        'hy_f_b2': nrm((L, F), 0.1),
        'hy_f_w3': nrm((L, F, F), F ** -0.5),
        'hy_f_b3': nrm((L, F), 0.1),
        'hy_f_wout': nrm((L, F, 2 * HY_WIDTH), 0.05 * F ** -0.5),
        'hy_f_freq': 1.0 + nrm((L, F), 0.05),
        'hy_skip': nrm((L, HY_WIDTH), 0.5),
        'qk_g_q': 1.0 + nrm((L, HEAD_DIM), 0.05),
        'qk_g_k': 1.0 + nrm((L, HEAD_DIM), 0.05),
        'na_rpb': nrm((L, NA_HEADS, 2 * NA_KH - 1, 2 * NA_KW - 1), 0.1),
        'w_ffn_in': nrm((L, D, 2 * FFN_HIDDEN), D ** -0.5),
        'w_ffn_out': nrm((L, FFN_HIDDEN, D), FFN_HIDDEN ** -0.5),
        'g_final': 1.0 + nrm((D,), 0.05),
    }

def reference(x, c, ctx, c_ctx, w_mod, b_mod, g_mix, g_ffn, w_in, w_out, hy_conv_w, hy_conv_b,
              hy_f_w1, hy_f_b1, hy_f_w2, hy_f_b2, hy_f_w3, hy_f_b3, hy_f_wout, hy_f_freq, hy_skip,
              qk_g_q, qk_g_k, na_rpb, w_ffn_in, w_ffn_out, g_final):
    S = x.shape[1]
    Lc = ctx.shape[1]
    cos, sin = axial_rope_tables(S)
    silu_c = jax.nn.silu(c)
    silu_cc = jax.nn.silu(c_ctx)
    xl, xc = x, ctx
    for l in range(DEPTH):
        last = l == DEPTH - 1
        mod_l = (silu_c @ w_mod[l] + b_mod[l])[:, None, :]
        mod_c = silu_cc @ w_mod[l] + b_mod[l]
        sh1, sc1, gt1, sh2, sc2, gt2 = jnp.split(mod_l, 6, axis=-1)
        csh1, csc1, cgt1, csh2, csc2, cgt2 = jnp.split(mod_c, 6, axis=-1)

        pl = modulate(rms_norm(xl, g_mix[l]), sh1, sc1) @ w_in[l]
        pc = modulate(rms_norm(xc, g_mix[l]), csh1, csc1) @ w_in[l]
        hy_l, q_l, k_l, v_l, nq_l, nk_l, nv_l = split_proj(pl)
        hy_c, q_c, k_c, v_c, nq_c, nk_c, nv_c = split_proj(pc)

        q_l = apply_rope(rms_norm(q_l, qk_g_q[l]), cos, sin)
        k_l = apply_rope(rms_norm(k_l, qk_g_k[l]), cos, sin)
        k_c = rms_norm(k_c, qk_g_k[l])
        gqa_l = gqa_latent(q_l, jnp.concatenate([k_c, k_l], axis=1),
                           jnp.concatenate([v_c, v_l], axis=1))
        na_l = natten_latent(nq_l, nk_l, nv_l, nk_c, nv_c, na_rpb[l])
        filt_l = hyena_filter(S, hy_f_w1[l], hy_f_b1[l], hy_f_w2[l], hy_f_b2[l], hy_f_w3[l],
                              hy_f_b3[l], hy_f_wout[l], hy_f_freq[l])
        hyo_l = hyena_mixer(hy_l, filt_l, hy_conv_w[l], hy_conv_b[l], hy_skip[l])

        mix_l = jnp.concatenate([hyo_l, gqa_l, na_l], axis=-1) @ w_out[l]
        xl = xl + gt1 * mix_l
        xl = xl + gt2 * swiglu(modulate(rms_norm(xl, g_ffn[l]), sh2, sc2), w_ffn_in[l], w_ffn_out[l])

        if not last:
            q_c = rms_norm(q_c, qk_g_q[l])
            gqa_c = attend(q_c, k_c, v_c)
            na_c = attend(nq_c, nk_c, nv_c)
            filt_c = hyena_filter(Lc, hy_f_w1[l], hy_f_b1[l], hy_f_w2[l], hy_f_b2[l], hy_f_w3[l],
                                  hy_f_b3[l], hy_f_wout[l], hy_f_freq[l])
            hyo_c = hyena_mixer(hy_c, filt_c, hy_conv_w[l], hy_conv_b[l], hy_skip[l])
            mix_c = jnp.concatenate([hyo_c, gqa_c, na_c], axis=-1) @ w_out[l]
            xc = xc + cgt1 * mix_c
            xc = xc + cgt2 * swiglu(modulate(rms_norm(xc, g_ffn[l]), csh2, csc2),
                                    w_ffn_in[l], w_ffn_out[l])
    return rms_norm(xl, g_final)


_drawn_inputs = setup_inputs


def setup_inputs(seed=0):
    import zlib

    import numpy as np

    out = dict(_drawn_inputs(seed))
    spreads = {}
    factors = {'ctx': 3.983,
     'b_mod': 2.923,
     'g_mix': 8.0,
     'g_ffn': 28.336,
     'hy_conv_b': 8.0,
     'hy_f_b1': 8.0,
     'hy_f_b2': 6.84,
     'hy_f_b3': 4.65,
     'hy_f_freq': 8.0,
     'qk_g_q': 32.461,
     'qk_g_k': 31.427,
     'na_rpb': 200.0}
    for name, (base, spread) in spreads.items():
        noise = np.random.default_rng([zlib.crc32(name.encode()), seed]).standard_normal(out[name].shape)
        drawn = base * np.exp(spread * noise) if base else spread * noise
        out[name] = __import__('jax').numpy.asarray(drawn.astype(out[name].dtype))
    for name, factor in factors.items():
        out[name] = (out[name] * factor).astype(out[name].dtype)
    return out
```

```python
import math
from contextlib import ExitStack

import numpy as np

import concourse.bass as bass
import concourse.mybir as mybir

F32 = mybir.dt.float32
F16 = mybir.dt.float16
ACT = mybir.ActivationFunctionType
ALU = mybir.AluOpType
AX = mybir.AxisListType.X

P = 128
S, C, D = 1024, 256, 1024
NT, NC, KD = S // P, C // P, D // P
HD = 64
HQ, HKV, HN = 8, 2, 4
HYW = 256
GRID_W, ROWS, KH, KW = 64, 16, 8, 16
FH = 2816
KF = FH // P
QKV0 = 3 * HYW
FW, EMB = 64, 33
EPS = 1e-6
NEG = -1e30
HALF = S // 2

WS = 2.0 ** 8
HS = 2.0 ** -6
GS = 2.0 ** -8
MAGIC = 1.5 * 2.0 ** 23
TWO_PI_1 = 6.28125
TWO_PI_2 = float(np.float32(np.round((2 * math.pi - TWO_PI_1) * 2 ** 21) / 2 ** 21))
TWO_PI_3 = float(np.float32(2 * math.pi - TWO_PI_1 - TWO_PI_2))
PI_IN = 3.1415925

V_BMOD, V_GMIX, V_GFFN, V_C, V_CC, V_CW, V_CB, V_SKIP = 0, 48, 56, 64, 72, 80, 98, 104
N_ROWS = 106

CHUNKS = (["ff"] * 4 + ["mod"] * 8
          + ["hy", "hy"] + ["mod"] * 5 + ["hy"] + ["mod"] * 11
          + ["fwd", "fwd", "inv", "fwd", "inv", "fwd", "inv", "inv"]
          + ["qkv"] * 6 + ["wo"] * 4 + ["fi"] * KF + ["fo"] * KF)
N_EARLY = CHUNKS.index("wo")
BY_PE = ("ff", "mod", "fwd", "inv")


def chunk_slot(c):
    return c % 4 if c < N_EARLY else (c - N_EARLY) % 2


def chunk_arrivals(c):
    return sum(1 + (CHUNKS[i] == "fi") for i in range(c + 1) if chunk_slot(i) == chunk_slot(c))


def chunk_before(c):
    return next((i for i in range(c - 1, -1, -1) if chunk_slot(i) == chunk_slot(c)), None)


def n_of_kind(c, *kinds):
    return sum(k in kinds for k in CHUNKS[:c + 1])


def n_split(c):
    return sum(k not in BY_PE and k != "wo" for k in CHUNKS[:c + 1])


def chunk_index(kind, n):
    return [i for i, k in enumerate(CHUNKS) if k == kind][n]


def flat(v):
    names = "abcd"[:len(v.shape) - 1]
    return v if len(names) == 1 else v.rearrange(f"p {' '.join(names)} -> p ({' '.join(names)})")


def constants():
    pos = np.arange(S)
    inv = (10000.0 ** (-np.arange(HD // 4, dtype=np.float32) / (HD // 4))).astype(np.float32)
    ang = np.concatenate([(pos // GRID_W).astype(np.float32)[:, None] * inv,
                          (pos % GRID_W).astype(np.float32)[:, None] * inv], -1).astype(np.float32)
    cos, sin = np.cos(ang.astype(np.float64)), np.sin(ang.astype(np.float64))
    rope = np.stack([np.concatenate([cos, cos], 1), np.concatenate([-sin, sin], 1)], 1)
    rope = rope.reshape(NT, P, 2, HD).transpose(1, 0, 2, 3)

    perm = np.concatenate([np.arange(0, S, 2), np.arange(1, S, 2)])
    t = np.linspace(0.0, 1.0, S, dtype=np.float32)[:, None]
    bands = (EMB - 1) // 2
    w = (np.float32(2.0 * math.pi) * np.arange(S, dtype=np.float32)[:, None] / np.float32(S)).astype(np.float32)
    fr = np.linspace(1e-4, bands - 1, bands, dtype=np.float32)[None, :]
    arg = (fr * w).astype(np.float32).astype(np.float64)
    z = np.concatenate([t, np.cos(arg), -np.sin(arg)], -1)[perm].T
    deltas = np.linspace(math.log(1e-2) / 1.5, math.log(1e-2) / 0.3, HYW, dtype=np.float32)
    decay = np.exp((-t * np.abs(deltas)).astype(np.float64))
    decay = np.concatenate([decay, decay], 1)
    decay[0, HYW:] = 0.0
    decay = decay[perm].reshape(NT, P, 2 * HYW).transpose(1, 0, 2)

    n = np.arange(S)[:, None]
    k = np.arange(HALF)[None, :]
    theta = np.pi * ((n * (2 * k + 1)) % 4096) / 2048.0
    cs = np.stack([np.cos(theta), np.sin(theta)], 1)[perm]
    fwd = cs.reshape(NT, P, 2, 4, P).transpose(3, 1, 0, 2, 4)
    inv_t = cs.transpose(2, 1, 0).reshape(4, P, 2, S)

    w_ = np.arange(P) % GRID_W
    wk = np.arange(GRID_W)
    first = np.clip(w_ - KW // 2, 0, GRID_W - KW)[:, None]
    cmask = np.where((wk >= first) & (wk < first + KW), 0.0, NEG)
    rmask = np.zeros((P, 5, 10))
    for n_, tile in enumerate([0, 1, 3, 6, 7]):
        for p in range(P):
            r = 2 * tile + p // GRID_W
            rs = min(max(r - KH // 2, 0), ROWS - KH)
            for i in range(10):
                kr = 2 * window(tile) + i
                rmask[p, n_, i] = 0.0 if rs <= kr < rs + KH else NEG
    out = dict(ident=np.eye(P), rope=rope, zt=z, decay=decay, fwd=fwd, inv=inv_t, cmask=cmask, rmask=rmask)
    return {"cst_" + n_: np.ascontiguousarray(a, np.float32) for n_, a in out.items()}


def window(t):
    return min(max(t - 2, 0), 3)


def bias_kind(t):
    return {0: 0, 1: 1, 6: 3, 7: 4}.get(t, 2)


def bias_shift(kind):
    return [8, 6, 4, 2, 0][kind]


class Unit:

    def __init__(self, v, it=0):
        self.v, self.it, self.par, self.na = v, it, v % 2, v < HN * NT
        self.n = v + 8 * it
        w = v if self.na else v - HN * NT
        self.blk, self.j = w // 8 + it, w % 8
        self.kv = None if self.na else self.j // (HQ // HKV)
        self.n_gqa = self.n - HN * NT

    def ahead(self, d):
        return Unit(self.v + d, self.it)


class Chain:

    def __init__(self, eng, sem):
        self.eng, self.sem, self.n = eng, sem, 0

    def step(self, ins):
        ins.then_inc(self.sem, 1)
        self.n = self.n + 1

    def wait(self):
        self.eng.wait_ge(self.sem, self.n)

    def enter(self, it, per):
        self.base = self.n
        self.per = per
        self.n = it * per + self.base

    def leave(self, count):
        self.n = self.base + count * self.per


def build(nc, io, cst, out):
    ctx = ExitStack()
    with ctx:
        sem = lambda name: ctx.enter_context(nc.semaphore(name))
        arena = ctx.enter_context(nc.sbuf_tensor("arena", [P, 207 * 256], F32))
        PS = ctx.enter_context(nc.psum_tensor("PS", [P, 8, 512], F32))
        skew = nc.dram_tensor("skewed_bias_rows", (HN, 19, 64, P), F32, kind="Internal")

        def f32(kb, *shape):
            n = int(np.prod(shape))
            o = int(kb * 256)
            v = arena[:, o:o + n]
            names = "abcd"[:len(shape)]
            if len(shape) > 1:
                v = v.rearrange(f"p ({' '.join(names)}) -> p {' '.join(names)}",
                                **{c: s for c, s in zip(names, shape)})
            return v

        def f16(kb, *shape):
            n = int(np.prod(shape))
            o = int(kb * 256)
            v = arena[:, o:o + n // 2].bitcast(F16)
            names = "abcd"[:len(shape)]
            if len(shape) > 1:
                v = v.rearrange(f"p ({' '.join(names)}) -> p {' '.join(names)}",
                                **{c: s for c, s in zip(names, shape)})
            return v

        ident = f32(0, P)
        ident16 = f16(0.5, P)
        cols = f32(0.75, P)
        mod = f32(1.25, 48, 2)
        am = f32(1.625, 8, 2)
        af = f32(1.6875, 8, 2)
        silu_c = f32(1.75, 8, 2)
        cwb = f32(1.8125, 18)
        fvec = f32(1.9, 4)
        ss = f32(2.0, 16)
        rs = f32(2.0625, 16)
        neghalf = f32(2.125, 16)
        ssq = f32(2.25, 2, 8)
        rsq = f32(2.3125, 2, 8)
        nmax = f32(2.375, 2)
        esum = f32(2.40625, 4)
        rcp = f32(2.4375, 2)
        gq = f32(2.5, 2, HD)
        rmask = f32(3.0, 5, 10)
        cmask = f32(3.25, GRID_W)
        gkc = f32(3.5, HD)

        PSf = PS[:, :, :].rearrange("p a b -> p (a b)")
        RAW = lambda s: 4 + 8 * s
        Z = 108

        def raw(c, *shape):
            return f32(RAW(chunk_slot(c)), *shape)

        def spl(slot, *shape):
            return f16(36 + 8 * slot, 2, *shape)

        hT = f16(68, 2, KD, S)
        hcT = f16(100, 2, KD, C)
        yT = f16(Z, 2, 2, S)
        x2T = f32(Z + 8, 2, S)
        uvT = f32(Z + 16, 2, S)
        vtok = f32(Z + 24, NT, HYW)
        Fc = f32(Z + 32, 4, 2 * HYW)
        Fs = f32(Z + 40, 4, 2 * HYW)
        zt = f32(Z + 8, S)
        fu = f32(Z + 12, S)
        fk = f32(Z + 16, S)
        fh = f32(Z + 20, S)
        decay = f32(Z + 24, NT, 2 * HYW)
        fw = f32(Z + 40, 4, P)
        fwo = f32(Z + 42, 2 * HYW)
        fbd = f32(Z + 44, 2, 2, HYW)
        filt_a = f32(52, NT, HYW)
        filt_b = f32(60, NT, HYW)
        rows = f32(Z + 48, P)
        accx = f32(Z + 48, 2, S)
        htmp = f32(Z + 48, 2, 512)
        tE = f32(Z + 56, 2, 2, HYW)
        tE0 = f32(Z + 48, 2, 2, HYW)
        xs = f32(Z + 59, 10, D)
        V2c = f32(Z + 60, 512)
        V2s = f32(Z + 62, 512)
        t1 = f32(Z + 64, 512)
        t2 = f32(Z + 66, 512)
        Yc = f32(Z + 68, 512)
        Ys = f32(Z + 70, 512)
        G = f32(Z + 72, 2, 4, HYW)
        yo = f32(Z + 80, 2, 512)
        t3 = f32(Z + 84, 512)
        t4 = f32(Z + 48, 512)
        qT = f16(Z + 8, HQ, S)
        kT = f16(Z + 24, HKV, 2, S + C)
        V = f32(Z + 34, NT + NC, 6, HD)
        nqT = f16(Z + 59, HN, S)
        nkT = f16(Z + 67, HN, 2, S + C)
        nT = [f32(Z + 49, 512), f32(Z + 51, 512)]
        bT = [f32(Z + 53, 512), f32(Z + 55, 512)]
        stk = [f16(Z + 57, 1024), f16(Z + 95, 1024)]
        skrow = f32(Z + 97, P)
        gc = f32(Z + 87, NT, 2, HD)
        gk = f32(Z + 91, NT, 2, HD)
        Pb = f32(Z + 49, 2, 10, P)
        J = f32(20, 2, 18, GRID_W)
        bias = f32(36, 2, 5, 10, GRID_W)
        mixtok = f32(68, NT, 768)
        PT = f32(92, 2, 10, P)
        woS = [f16(Z + 59 + 8 * i, 2, 4, 512) for i in range(4)]
        mixT = f16(Z + 8, 2, 6, S)
        gate1 = f32(Z + 95, D)
        gate2 = f32(Z + 91, D)
        x1 = f32(20, NT, D)
        ones = f32(Z + 32, P)
        diag = f32(Z + 33, 8, P)
        xn1 = f32(Z + 32, 4, D)
        wtmp = f32(Z + 49, 2, D)
        h2tmp = f32(100, 2, 512)
        fiS = [f16(52, 2, 8, 256), f16(60, 2, 8, 256)]
        foS = [f16(52, 2, 2, 1024), f16(60, 2, 2, 1024)]
        prodT = f16(Z, 2, KF, S)
        sg = f32(100, S)
        pr = f32(104, S)
        gfin = f32(68, D)
        otmp = f32(72, 4, D)
        osq = f32(88, D)

        small_in = sem("small_in")
        x_in = [sem(f"x_in{i}") for i in range(3)]
        raw_in = [sem(f"raw_in{i}") for i in range(4)]
        split_hi = sem("split_hi")
        split_lo = sem("split_lo")
        wo_split = sem("w_out_split")
        id16_rdy = sem("ident16_ready")
        cols_rdy = sem("columns_ready")
        silu_rdy = sem("silu_of_c_ready")
        mlp_mm = sem("filter_layer_product")
        mlp_arg = sem("filter_layer_argument")
        mlp_h = sem("filter_layer_value")
        taps_mm = sem("filter_taps_product")
        taps_rdy = sem("filter_taps_ready")
        spec_mm = sem("spectrum_product")
        even_part = sem("even_part_copied")
        spec_rdy = sem("spectrum_ready")
        cols_mm = sem("columns_transposed")
        mod_used = sem("modulation_chunk_used")
        mod_rdy = sem("modulation_ready")
        sq_done = sem("squares_summed")
        ms_rdy = sem("mean_square_ready")
        rs_rdy = sem("inverse_root_ready")
        xn_rdy = sem("x_normalised")
        hT_mm = sem("h_transposed")
        hT_f = sem("h_modulated")
        hT_rdy = sem("h_split")
        hy_mm = sem("hyena_projection")
        hy_mid = sem("middle_tap")
        hy_rdy = sem("short_convolution")
        vt_mm = sem("v_transposed")
        vt_rdy = sem("v_by_token")
        G_rdy = sem("folded_spectrum")
        inv_mm = sem("inverse_products")
        y_f = sem("hyena_output")
        y_hi = sem("hyena_output_hi")
        y_rdy = sem("hyena_output_split")
        gn_in = sem("gains_in")
        gt_rdy = sem("rope_tables_ready")
        pr_mm = sem("qkv_projection")
        pr_sq = sem("qk_squares")
        pr_n = sem("qk_scaled")
        pr_ms = sem("qk_mean_square")
        pr_rs = sem("qk_inverse_root")
        pr_r = sem("qk_rotated")
        pr_hi = sem("qk_hi")
        pr_lo = sem("qk_lo")
        pr_v = sem("values_copied")
        pr_tm = sem("qk_transposed")
        pr_tc = sem("qk_transposed_copied")
        skew_rows = sem("bias_rows_in")
        skew_set = sem("bias_rows_cleared")
        skew_out = sem("bias_rows_out")
        J_in = [sem("bias_table_in0"), sem("bias_table_in1")]
        bias_add = sem("bias_added")
        bias_rdy = sem("bias_ready")
        s_mm = sem("scores")
        s_max = sem("score_maximum")
        s_exp = sem("exponentials")
        pt_mm = sem("probabilities_transposed")
        pt_d = sem("probabilities_copied_by_vector")
        pt_a = sem("probabilities_copied_by_scalar")
        o_mm = sem("values_weighted")
        o_rdy = sem("attention_output")
        gate_d = sem("gate_diagonal")
        gate_mm = sem("gate_spread")
        gate_rdy = sem("gate_ready")
        mx_mm = sem("mix_transposed")
        mx_hi = sem("mix_hi")
        mx_lo = sem("mix_lo")
        wo_mm = sem("output_projection")
        x1_rdy = sem("x1_ready")
        x1_sum = sem("x1_summed")
        x1_in = sem("x_again_in")
        sq1 = sem("x1_squares")
        ms1 = sem("x1_mean_square")
        rs1 = sem("x1_inverse_root")
        xn1_rdy = sem("x1_normalised")
        fi_mm = sem("ffn_in_product")
        fi_s = sem("silu_done")
        fi_p = sem("gated")
        fi_hi = sem("gated_hi")
        fi_lo = sem("gated_lo")
        fo_used = sem("ffn_out_chunk_used")
        fo_x = sem("x2_summed")
        fo_mm = sem("ffn_out_product")
        fo_r = sem("x2_ready")
        fo_sq = sem("x2_squares")
        fo_ms = sem("x2_mean_square")
        fo_rs = sem("x2_inverse_root")
        fo_y = sem("output_row_ready")
        gf_in = sem("g_final_in")
        out_done = sem("output_stored")
        dve_own = sem("vector_steps")
        pool_own = sem("pool_steps")

        block = ctx.enter_context(nc.Block())
        x_rows = io["x"].rearrange("b (t p) d -> p (b t) d", p=P)
        ctx_rows = io["ctx"].rearrange("b (t p) d -> p (b t) d", p=P)
        out_rows = out.rearrange("b (t p) d -> p (b t) d", p=P)
        w_mod = io["w_mod"][0].rearrange("(k p) n -> p k n", p=P)
        w_in = io["w_in"][0].rearrange("(k p) n -> p k n", p=P)
        w_out = io["w_out"][0].rearrange("(k p) n -> p k n", p=P)
        w_fi = io["w_ffn_in"][0].rearrange("(k p) n -> p k n", p=P)
        w_fo = io["w_ffn_out"][0].rearrange("(k p) n -> p k n", p=P)
        small = [
            (ident, cst["ident"]),
            (zt[0:EMB], cst["zt"]),
            (fw[0:EMB, 0, 0:FW], io["hy_f_w1"][0]),
            (fw[0:FW, 1, 0:FW], io["hy_f_w2"][0]),
            (fw[0:FW, 2, 0:FW], io["hy_f_w3"][0]),
            (fwo[0:FW], io["hy_f_wout"][0]),
            (fvec[0:FW, 0:1], io["hy_f_b1"].rearrange("a f -> f a")),
            (fvec[0:FW, 1:2], io["hy_f_b2"].rearrange("a f -> f a")),
            (fvec[0:FW, 2:3], io["hy_f_b3"].rearrange("a f -> f a")),
            (fvec[0:FW, 3:4], io["hy_f_freq"].rearrange("a f -> f a")),
            (decay, cst["decay"]),
            (rows[V_BMOD:V_BMOD + 48], io["b_mod"][0].rearrange("(t p) -> t p", p=P)),
            (rows[V_GMIX:V_GMIX + 8], io["g_mix"][0].rearrange("(t p) -> t p", p=P)),
            (rows[V_GFFN:V_GFFN + 8], io["g_ffn"][0].rearrange("(t p) -> t p", p=P)),
            (rows[V_C:V_C + 8], io["c"][0].rearrange("(t p) -> t p", p=P)),
            (rows[V_CC:V_CC + 8], io["c_ctx"].rearrange("(t p) -> t p", p=P)),
            (rows[V_CW:V_CW + 18], io["hy_conv_w"][0].rearrange("i (t p) -> (i t) p", p=P)),
            (rows[V_CB:V_CB + 6], io["hy_conv_b"][0].rearrange("(t p) -> t p", p=P)),
            (rows[V_SKIP:V_SKIP + 2], io["hy_skip"][0].rearrange("(t p) -> t p", p=P)),
            (rmask, cst["rmask"]),
            (cmask, cst["cmask"]),
            (gq[:, 0], io["qk_g_q"][0].partition_broadcast(P)),
            (gq[:, 1], io["qk_g_k"][0].partition_broadcast(P)),
        ]
        N_SMALL = len(small) * 16

        UNITS = [(g, t) for g in (1, 2, 0) for t in range(NT + (NC if g else 0))]
        NU = len(UNITS)
        GROUP0 = {1: 0, 2: NT + NC, 0: 2 * (NT + NC)}

        def n_normed(u):
            return sum(g != 2 for g, _ in UNITS[:u + 1])

        NV = HN * NT + HQ * NT
        NNA = HN * NT

        def arrived(eng, c, more=0):
            eng.wait_ge(raw_in[chunk_slot(c)], more * 16 + 16 * chunk_arrivals(c))

        def stacks(g, t, par):
            out = []
            n_k = {1: HKV, 2: HN, 0: 0}[g]
            if n_k:
                v = stk[par][:, 0:n_k * 256].rearrange("p (h a r d) -> p h a r d", h=n_k, a=2, r=2)
                src = nT[par][:, 0:n_k * HD].rearrange("p (h d) -> p h d", d=HD).unsqueeze(2)\
                    .broadcast_to((P, n_k, 2, HD))
                out.append((v[:, :, 0], v[:, :, 1], src))
            if g == 0 or (g == 1 and t < NT):
                n_q, o, s = (HQ, 0, 0) if g == 0 else (HN, 512, 128)
                v = stk[par][:, o:o + n_q * 128].rearrange("p (h a d) -> p h a d", h=n_q, a=2)
                out.append((v[:, :, 0], v[:, :, 1], nT[par][:, s:s + n_q * HD].rearrange("p (h d) -> p h d", d=HD)))
            return out

        def tok(t):
            return bass.ds(t * P, P)

        @block.sync
        def _(sp):
            def load(c, src, shape):
                before = chunk_before(c)
                if before is not None:
                    kind = CHUNKS[before]
                    if kind in ("ff", "fwd"):
                        sp.wait_ge(spec_mm, n_of_kind(before, "ff", "fwd"))
                    elif kind == "inv":
                        sp.wait_ge(inv_mm, n_of_kind(before, "inv"))
                    elif kind == "mod":
                        sp.wait_ge(mod_used, n_of_kind(before, "mod"))
                    elif kind == "wo":
                        sp.wait_ge(wo_split, n_of_kind(before, "wo"))
                    else:
                        sp.wait_ge(split_lo, n_split(before))
                sp.dma_start(raw(c, *shape), src).then_inc(raw_in[chunk_slot(c)], 16)

            for n in range(4):
                load(n, cst["fwd"][n].rearrange("p a b k -> p (a b) k"), (16, P))
            for i in range(2):
                sp.dma_start(xs[:, 4 * i:4 * i + 4], x_rows[:, 4 * i:4 * i + 4]).then_inc(x_in[i], 16)
            sp.dma_start(xs[:, 8:10], ctx_rows).then_inc(x_in[2], 16)
            n_of = dict.fromkeys(CHUNKS, 0)
            for c in range(4, N_EARLY):
                kind = CHUNKS[c]
                n = n_of[kind]
                n_of[kind] += 1
                if kind == "mod":
                    load(c, w_mod[:, :, 256 * n:256 * n + 256], (8, 256))
                elif kind == "hy":
                    load(c, w_in[:, :, 256 * n:256 * n + 256], (8, 256))
                elif kind == "fwd":
                    load(c, cst["fwd"][n].rearrange("p a b k -> p (a b) k"), (16, P))
                elif kind == "inv":
                    load(c, cst["inv"][n], (2, S))
                else:
                    col, kh = QKV0 + 512 * (1, 2, 0)[n // 2], 4 * (n % 2)
                    load(c, w_in[:, kh:kh + 4, col:col + 512], (4, 512))
                if kind == "hy" and n == 0:
                    sp.wait_ge(hT_mm, 20)
                    for tab in (gc, gk):
                        sp.dma_start(tab, cst["rope"]).then_inc(gn_in, 16)
            sp.wait_ge(skew_out, 16)
            sp.wait_ge(split_lo, n_split(chunk_index("qkv", 5) - 1))
            for h in range(HN):
                if h >= 2:
                    sp.wait_ge(bias_rdy, 5 * (h - 1))
                for a in range(2):
                    src = bass.AP(tensor=skew, offset=(h * 19 + 1 - a) * 64 * P + 63,
                                  ap=[[P - 1, 64], [64 * P, 18], [1, GRID_W]])
                    sp.dma_start(J[64 * a:64 * a + 64, h % 2], src).then_inc(J_in[h % 2], 16)
                if h == 1:
                    for n in range(2):
                        load(chunk_index("wo", n), w_out[:, 0:4, 512 * n:512 * n + 512], (4, 512))
            for n in range(2, 4):
                load(chunk_index("wo", n), w_out[:, 4:8, 512 * (n % 2):512 * (n % 2) + 512], (4, 512))
            sp.wait_ge(bias_add, NNA)
            for i in range(4):
                sp.dma_start(x1[:, 2 * i:2 * i + 2], x_rows[:, 2 * i:2 * i + 2]).then_inc(x1_in, 16)
            c0 = chunk_index("fi", 0)

            def load_fi(j, b):
                for g in range(2):
                    sp.dma_start(f32(RAW(b), KD, 2, P)[:, :, g], w_fi[:, :, bass.ds(j * P + g * FH, P)])\
                        .then_inc(raw_in[b], 16)

            for b in range(2):
                sp.wait_ge(wo_split, 3 + b)
                load_fi(b, b)
            with sp.Fori(0, KF // 2 - 1) as it:
                for b in range(2):
                    sp.wait_ge(split_lo, it * 2 + n_split(c0 + b))
                    load_fi(it * 2 + 2 + b, b)
            c1 = chunk_index("fo", 0)
            for grp in range(2):
                with sp.Fori(0, 5) as it:
                    for b in range(2):
                        s = (grp + b) % 2
                        sp.wait_ge(split_lo, it * 2 + n_split(c1 + grp * 11 + b - 2))
                        sp.dma_start(f32(RAW(s), 2, D), w_fo[:, bass.ds(it * 4 + 2 * b, 2), :]).then_inc(raw_in[s], 16)
                sp.wait_ge(split_lo, n_split(c1 + grp * 11 + 8))
                sp.dma_start(f32(RAW(grp), 2, D), w_fo[:, 20:22, :]).then_inc(raw_in[grp], 16)
            for t in range(NT):
                sp.wait_ge(fo_y, t + 1)
                sp.dma_start(out_rows[:, t], x1[:, t]).then_inc(out_done, 16)
            sp.wait_ge(out_done, 16 * NT)

        @block.gpsimd
        def _(pool):
            own = Chain(pool, pool_own)
            own.step(pool.memset(neghalf, -0.5))
            own.wait()
            pool.wait_ge(ms_rdy, 1)
            pool.tensor_tensor(rs[:, 0:10], ss[:, 0:10], neghalf[:, 0:10], ALU.pow).then_inc(rs_rdy, 1)
            pool.wait_ge(hT_mm, 20)
            pool.memset(skrow[0:HN * 19], NEG).then_inc(skew_set, 1)
            for u, (g, t) in enumerate(UNITS):
                if g == 2:
                    continue
                n, w = n_normed(u), HQ if g == 0 else HKV
                pool.wait_ge(pr_ms, n)
                pool.tensor_tensor(rsq[:, u % 2, 0:w], ssq[:, u % 2, 0:w], neghalf[:, 0:w], ALU.pow)\
                    .then_inc(pr_rs, 1)
            for h in range(HN):
                pool.wait_ge(J_in[h % 2], 32 * (h // 2 + 1))
                own.step(pool.tensor_tensor(J[:, h % 2], J[:, h % 2],
                                            cmask.unsqueeze(1).broadcast_to((P, 18, GRID_W)), ALU.add))
                own.wait()
                if h < 2:
                    pool.wait_ge(pr_mm, (GROUP0[0], NU)[h])
                else:
                    pool.wait_ge(bias_add, NT * (h - 1))
                for kind in range(5):
                    o = bias_shift(kind)
                    last = pool.tensor_tensor(bias[:, h % 2, kind], J[:, h % 2, o:o + 10],
                                              rmask[:, kind, :].unsqueeze(2).broadcast_to((P, 10, GRID_W)), ALU.add)
                    last.then_inc(bias_rdy, 1)
            for n in range(4):
                c = chunk_index("wo", n)
                arrived(pool, c)
                if n == 0:
                    pool.wait_ge(s_mm, NNA)
                r, (k0, hy) = raw(c, 4, 512), (4 * (n // 2), 2 if n < 2 else 0)
                if hy:
                    own.step(pool.tensor_scalar(r[:, 0:2], r[:, 0:2], WS / HS, None, ALU.mult))
                own.step(pool.tensor_scalar(r[:, hy:4], r[:, hy:4], WS, None, ALU.mult))
                own.wait()
                own.step(pool.tensor_copy(woS[n][:, 0], r))
                own.wait()
                pool.tensor_tensor(woS[n][:, 1], r, woS[n][:, 0], ALU.subtract).then_inc(wo_split, 1)
            for half in range(2):
                pool.wait_ge(ms1, half + 1)
                pool.tensor_tensor(rs[:, 4 * half:4 * half + 4], ss[:, 4 * half:4 * half + 4],
                                   neghalf[:, 0:4], ALU.pow).then_inc(rs1, 1)
            for t in range(NT):
                pool.wait_ge(fo_ms, t + 1)
                pool.tensor_tensor(rs[:, t:t + 1], ss[:, t:t + 1], neghalf[:, 0:1], ALU.pow).then_inc(fo_rs, 1)

        @block.tensor
        def _(pe):
            def mm(out, lhsT, rhs, start, stop):
                return pe.matmul(out, lhsT, rhs, start=start, stop=stop, skip_group_check=True)

            pe.wait_ge(small_in, N_SMALL)
            pe.transpose(PS[:, 4, 0:N_ROWS], rows[0:N_ROWS], ident[0:N_ROWS, 0:N_ROWS]).then_inc(cols_mm, 1)
            for layer in range(3):
                k = EMB if layer == 0 else FW
                src = zt if layer == 0 else fh
                if layer:
                    pe.wait_ge(mlp_h, layer)
                for half in range(2):
                    ins = mm(PS[0:FW, half, :], fw[0:k, layer, 0:FW], src[0:k, half * 512:half * 512 + 512], True, True)
                ins.then_inc(mlp_mm, 1)
            pe.wait_ge(mlp_h, 3)
            for nt in range(NT):
                if nt >= 2:
                    pe.wait_ge(taps_rdy, nt - 1)
                mm(PS[:, 2 + nt % 2, :], fh[0:FW, nt * P:nt * P + P], fwo[0:FW], True, True).then_inc(taps_mm, 1)

            def spectrum(c, par, cos_of, sin_of):
                w = raw(c, NT, 2, P)
                arrived(pe, c)
                for trig, table in ((0, cos_of), (1, sin_of)):
                    for odd in range(2):
                        for i in range(4):
                            nt = 4 * odd + i
                            ins = mm(PS[:, 2 * par + trig, 256 * odd:256 * odd + 256], w[:, nt, trig], table[:, nt],
                                     i == 0, i == 3)
                ins.then_inc(spec_mm, 1)

            def modulation(c, tile):
                w = raw(c, KD, 256)
                arrived(pe, c)
                for i in range(2):
                    o = 2 * (tile + i)
                    for k in range(KD):
                        ins = mm(PS[:, 7, o:o + 2], w[:, k, i * P:i * P + P], silu_c[:, k], k == 0, k == KD - 1)
                ins.then_inc(mod_used, 1)

            pe.wait_ge(taps_rdy, NT)
            for kt in range(4):
                if kt >= 2:
                    pe.wait_ge(spec_rdy, kt - 1)
                spectrum(kt, kt % 2, filt_a, filt_b)
            pe.wait_ge(silu_rdy, 1)
            n_mod = 0
            for c in range(4, 12):
                modulation(c, 2 * n_mod)
                n_mod += 1

            def turn_x(src, tiles, bank, f):
                for i, t in enumerate(tiles):
                    ins = pe.transpose(PS[:, bank, i * P:i * P + P], src[:, t, f * P:f * P + P], ident)
                ins.then_inc(hT_mm, 1)

            pe.wait_ge(spec_rdy, 4)
            pe.wait_ge(xn_rdy, 10)
            for n in range(20):
                if n >= 4:
                    pe.wait_ge(hT_f, n - 3)
                if n < 16:
                    turn_x(xs, range(4 * (n // KD), 4 * (n // KD) + 4), n % 4, n % KD)
                else:
                    for i in range(4):
                        f, t = 2 * (n - 16) + i // 2, NT + i % 2
                        ins = pe.transpose(PS[:, n % 4, i * P:i * P + P], xs[:, t, f * P:f * P + P], ident)
                    ins.then_inc(hT_mm, 1)

            pe.wait_ge(hT_rdy, 16)
            pe.wait_ge(mod_rdy, 1)
            for i in range(3):
                slot = i % 2
                w = spl(slot, KD, 256)
                pe.wait_ge(split_lo, i + 1)
                for b in range(2):
                    ct = 2 * i + b
                    if ct >= 2:
                        pe.wait_ge(hy_rdy, ct - 1)
                    else:
                        pe.wait_ge(hT_f, 18 + 2 * ct)
                    for k in range(KD):
                        for part, others in ((0, (0, 1)), (1, (0,))):
                            for o in others:
                                for half in range(2):
                                    ins = mm(PS[:, 2 * b + half, :], w[:, part, k, b * P:b * P + P],
                                             hT[:, o, k, half * 512:half * 512 + 512],
                                             k == 0 and part + o == 0, k == KD - 1 and part == 1)
                    ins.then_inc(hy_mm, 1)
                for _ in range((5, 5, 6)[i]):
                    modulation(chunk_index("mod", n_mod), 2 * n_mod)
                    n_mod += 1

            pe.wait_ge(hy_rdy, 4)
            for q in range(4):
                if q >= 2:
                    pe.wait_ge(vt_rdy, q - 1)
                for i in range(2):
                    nt = 2 * q + i
                    o = nt * 256 if nt < 4 else (nt - 4) * 256 + 1
                    for c2 in range(2):
                        ins = pe.transpose(PS[:, 4 + q % 2, 256 * i + P * c2:256 * i + P * c2 + P],
                                           uvT[:, c2, o:o + 255:2], ident)
                ins.then_inc(vt_mm, 1)
            pe.wait_ge(vt_rdy, 4)
            pe.wait_ge(hy_rdy, 6)
            pe.wait_ge(mod_rdy, 2)

            def inverse(c, kt):
                w = raw(c, 2, S)
                arrived(pe, c)
                pe.wait_ge(G_rdy, kt + 1)
                for trig in range(2):
                    for odd in range(2):
                        for c2 in range(2):
                            ins = mm(PS[:, 4 + 2 * c2 + odd, :], G[:, kt % 2, 2 * odd + trig, c2 * P:c2 * P + P],
                                     w[:, trig, 512 * odd:512 * odd + 512], kt == 0 and trig == 0,
                                     kt == 3 and trig == 1)
                ins.then_inc(inv_mm, 1)

            for kt in range(5):
                if kt < 4:
                    if kt >= 2:
                        pe.wait_ge(spec_rdy, 4 + kt - 1)
                    spectrum(chunk_index("fwd", kt), kt % 2, vtok, vtok)
                if kt:
                    inverse(chunk_index("inv", kt - 1), kt - 1)

            def project(u, par, g, t, is_ctx, it=None):
                more = 0 if it is None else it * 2
                if u >= 2:
                    if UNITS[u - 2][0] != 0:
                        pe.wait_ge(pr_v, more + u - 1)
                    if UNITS[u - 2][0] != 2:
                        pe.wait_ge(pr_n, more + n_normed(u - 2))
                pair = 2 if g != 2 else 0
                width = 256 if (is_ctx and g == 1) else 512
                for k in range(KD):
                    w = spl(pair + k // 4, 4, 512)
                    src = hcT if is_ctx else hT
                    for part, others in ((0, (0, 1)), (1, (0,))):
                        for o in others:
                            ins = mm(PS[:, par, 0:width], src[:, part, k, tok(t)], w[:, o, k % 4, 0:width],
                                     k == 0 and part + o == 0, k == KD - 1 and part == 1)
                ins.then_inc(pr_mm, 1)

            def turn_qk(u, par, n, it=None):
                more = 0 if it is None else it * 2
                pe.wait_ge(pr_lo, more + u + 1)
                if u >= 2:
                    pe.wait_ge(pr_tc, more + u - 1)
                out16 = PS[:, 2 + par, :].bitcast(F16)
                for j in range(n):
                    ins = pe.transpose(out16[:, j * P:j * P + P], stk[par][:, j * P:j * P + P], ident16)
                ins.then_inc(pr_tm, 1)

            for gi, g in enumerate((1, 2, 0)):
                u0 = GROUP0[g]
                pe.wait_ge(split_lo, 3 + 2 * gi + 2)
                for b in range(2):
                    project(u0 + b, b, g, b, False)
                    if gi:
                        turn_qk(u0 + b - 2, b, 4 if g == 2 else 8)
                with pe.Fori(0, 3) as it:
                    for b in range(2):
                        project(u0 + 2 + b, b, g, it * 2 + 2 + b, False, it)
                        turn_qk(u0 + b, b, 8, it)
                if g:
                    for b in range(2):
                        project(u0 + 8 + b, b, g, b, True)
                        turn_qk(u0 + 6 + b, b, 8)
            for b in range(2):
                turn_qk(NU - 2 + b, b, 8)

            def copied(u):
                pe.wait_ge(pt_a, u.n + 1)
                if not u.na:
                    pe.wait_ge(pt_d, u.n_gqa + 1)

            def scores(u):
                if u.v >= 2:
                    copied(u.ahead(-2))
                if u.na:
                    q = nqT[:, u.blk, u.j * P:u.j * P + P]
                    k0 = window(u.j) * P
                    for o, w, s0 in ((0, 512, k0), (512, 128, k0 + 512), (640, 256, S)):
                        for part in range(2):
                            ins = mm(PSf[:, 1536 * u.par + o:1536 * u.par + o + w], q,
                                     nkT[:, u.blk, part, s0:s0 + w], part == 0, part == 1)
                else:
                    q = qT[:, u.j, tok(u.blk)]
                    for o, w in ((0, 512), (512, 512), (1024, 256)):
                        for part in range(2):
                            ins = mm(PSf[:, 1536 * u.par + o:1536 * u.par + o + w], q,
                                     kT[:, u.kv, part, o:o + w], part == 0, part == 1)
                ins.then_inc(s_mm, 1)

            def turn_p(u):
                pe.wait_ge(s_exp, u.n + 1)
                for i in range(7 if u.na else 10):
                    o = 1536 * u.par + i * P
                    ins = pe.transpose(PSf[:, o:o + P], Pb[:, u.par, i], ident)
                ins.then_inc(pt_mm, 1)

            def weigh(u):
                copied(u)
                if u.v >= 2:
                    pe.wait_ge(o_rdy, u.n - 1)
                tiles = [window(u.j) + i for i in range(5)] + [NT, NT + 1] if u.na else range(10)
                for i, kt in enumerate(tiles):
                    ins = mm(PS[:, 6 + u.par, 0:HD], PT[:, u.par, i], V[:, kt, HKV + u.blk if u.na else u.kv],
                             i == 0, i == len(tiles) - 1)
                ins.then_inc(o_mm, 1)

            def attend(u):
                if u.v < NV - 1:
                    scores(u.ahead(1))
                turn_p(u)
                if u.v:
                    weigh(u.ahead(-1))

            pe.wait_ge(pr_tc, NU)
            scores(Unit(0))
            for v in range(3):
                attend(Unit(v))
            with pe.Fori(0, HN - 1) as it:
                for v in range(3, 11):
                    attend(Unit(v, it))
            for v in range(27, 33):
                attend(Unit(v))
            with pe.Fori(0, NT - 1) as it:
                for v in range(33, 41):
                    attend(Unit(v, it))
            for v in range(89, NV):
                attend(Unit(v))
            weigh(Unit(NV - 1))

            for n in range(2):
                pe.wait_ge(gate_d, n + 1)
                for i in range(2):
                    ins = mm(PS[:, 2 * n + i, :], ones, diag[:, 4 * i:4 * i + 4].rearrange("p a b -> p (a b)"),
                             True, True)
                ins.then_inc(gate_mm, 1)
            pe.wait_ge(o_rdy, NV)
            for t in range(NT):
                if t >= 2:
                    pe.wait_ge(mx_lo, t - 1)
                for f in range(6):
                    ins = pe.transpose(PS[:, 4 + 2 * (t % 2) + f // 4, (f % 4) * P:(f % 4) * P + P],
                                       mixtok[:, t, f * P:f * P + P], ident)
                ins.then_inc(mx_mm, 1)

            def project_out(t, b):
                for k in range(KD):
                    for part, others in ((0, (0, 1)), (1, (0,))):
                        lhs = yT[:, part, k, tok(t)] if k < 2 else mixT[:, part, k - 2, tok(t)]
                        for o in others:
                            for half in range(2):
                                ins = mm(PS[:, 2 * b + half, :], lhs, woS[2 * (k // 4) + half][:, o, k % 4, :],
                                         k == 0 and part + o == 0, k == KD - 1 and part == 1)
                ins.then_inc(wo_mm, 1)

            pe.wait_ge(mx_lo, NT)
            pe.wait_ge(gate_rdy, 2)
            pe.wait_ge(wo_split, 4)
            pe.wait_ge(y_rdy, 4)
            for b in range(2):
                project_out(b, b)
            with pe.Fori(0, 3) as it:
                for b in range(2):
                    pe.wait_ge(x1_rdy, it * 2 + b + 1)
                    project_out(it * 2 + 2 + b, b)
            for half in range(2):
                pe.wait_ge(xn1_rdy, half + 1)
                for f in range(KD):
                    n = 8 * half + f
                    if n >= 4:
                        pe.wait_ge(hT_f, 20 + n - 3)
                    turn_x(xn1, range(4), 4 + n % 4, f)

            def hidden(b):
                w = fiS[b]
                for gu in range(2):
                    for k in range(KD):
                        for part, others in ((0, (0, 1)), (1, (0,))):
                            for o in others:
                                for half in range(2):
                                    ins = mm(PS[:, 4 * b + 2 * gu + half, :], w[:, part, k, gu * P:gu * P + P],
                                             hT[:, o, k, half * 512:half * 512 + 512],
                                             k == 0 and part + o == 0, k == KD - 1 and part == 1)
                ins.then_inc(fi_mm, 1)

            pe.wait_ge(hT_rdy, 20 + 16)
            base = n_split(chunk_index("fi", 0))
            for b in range(2):
                pe.wait_ge(split_lo, base + b)
                hidden(b)
            with pe.Fori(0, KF // 2 - 1) as it:
                for b in range(2):
                    pe.wait_ge(split_lo, it * 2 + base + 2 + b)
                    pe.wait_ge(fi_p, it * 2 + b + 1)
                    hidden(b)

            def down(k0, s, grp, start, stop):
                for t in range(4):
                    if start and grp:
                        pe.wait_ge(fo_r, t + 1)
                    for kk in range(2):
                        for part, others in ((0, (0, 1)), (1, (0,))):
                            for o in others:
                                for half in range(2):
                                    ins = mm(PS[:, 2 * t + half, :], prodT[:, part, k0 + kk, tok(4 * grp + t)],
                                             foS[s][:, o, kk, half * 512:half * 512 + 512],
                                             start and kk == 0 and part + o == 0, stop and kk == 1 and part == 1)
                    if stop:
                        ins.then_inc(fo_mm, 1)
                if not stop:
                    ins.then_inc(fo_used, 1)

            pe.wait_ge(fi_lo, KF)
            base = n_split(chunk_index("fo", 0))
            for grp in range(2):
                n0 = base + 11 * grp
                pe.wait_ge(split_lo, n0)
                down(0, grp % 2, grp, True, False)
                with pe.Fori(0, 4) as it:
                    for b in range(2):
                        pe.wait_ge(split_lo, it * 2 + n0 + 1 + b)
                        down(it * 4 + 2 + 2 * b, (grp + 1 + b) % 2, grp, False, False)
                for b in range(2):
                    pe.wait_ge(split_lo, n0 + 9 + b)
                    down(18 + 2 * b, (grp + 1 + b) % 2, grp, False, b == 1)

        @block.scalar
        def _(act):
            for dst, src in small:
                act.dma_start(dst, src).then_inc(small_in, 16)

            def hi_of(c, dst):
                arrived(act, c)
                n = int(np.prod(dst.shape[2:]))
                src = f32(RAW(chunk_slot(c)), n)
                act.activation(flat(dst[:, 0]), src, ACT.Copy, scale=WS).then_inc(split_hi, 1)

            for layer in range(3):
                act.wait_ge(mlp_arg, layer + 1)
                act.activation(fh[0:FW], fu[0:FW], ACT.Sin).then_inc(mlp_h, 1)
            act.wait_ge(cols_rdy, 1)
            act.activation(silu_c.rearrange("p k n -> p n k"),
                           cols[:, V_C:V_C + 16].rearrange("p (n k) -> p n k", n=2), ACT.Silu).then_inc(silu_rdy, 1)
            for kt in range(4):
                act.wait_ge(spec_mm, kt + 1)
                if kt >= 2:
                    act.wait_ge(spec_rdy, kt - 1)
                act.activation(tE0[:, kt % 2], PS[:, 2 * (kt % 2):2 * (kt % 2) + 2, 0:256], ACT.Copy,
                               scale=1.0 / 1024).then_inc(even_part, 1)
                if kt == 0:
                    for t in range(10):
                        act.wait_ge(x_in[t // 4], 16)
                        act.activation(f32(68 + 4 * t, D), xs[:, t], ACT.Square, accum_out=ss[:, t:t + 1])\
                            .then_inc(sq_done, 1)

            hi_of(chunk_index("hy", 0), spl(0, KD, 256))
            act.wait_ge(mod_rdy, 1)
            for n in range(20):
                act.wait_ge(hT_mm, n + 1)
                if n >= 2:
                    act.wait_ge(hT_rdy, n - 1)
                if n < 16:
                    f = n % KD
                    act.activation(htmp[:, n % 2], PS[:, n % 4], ACT.Identity, scale=am[:, f, 0:1],
                                   bias=mod[:, f, 0:1]).then_inc(hT_f, 1)
                else:
                    for i in range(2):
                        f = 2 * (n - 16) + i
                        ins = act.activation(htmp[:, n % 2, 256 * i:256 * i + 256], PS[:, n % 4, 256 * i:256 * i + 256],
                                             ACT.Identity, scale=am[:, f, 1:2], bias=mod[:, f, 1:2])
                    ins.then_inc(hT_f, 1)
            hi_of(chunk_index("hy", 1), spl(1, KD, 256))
            for ct in range(6):
                act.wait_ge(hy_mm, ct + 1)
                if ct == 2:
                    act.wait_ge(hT_rdy, 20)
                dst = (uvT, accx, x2T)[ct // 2][:, ct % 2]
                act.activation(dst, PSf[:, 1024 * (ct % 2):1024 * (ct % 2) + 1024], ACT.Identity,
                               scale=cwb[:, 6 + ct:7 + ct], bias=cols[:, V_CB + ct:V_CB + ct + 1]).then_inc(hy_mid, 1)
                if ct == 1:
                    hi_of(chunk_index("hy", 2), spl(0, KD, 256))
            for q in range(4):
                act.wait_ge(vt_mm, q + 1)
                act.copy(flat(vtok[:, 2 * q:2 * q + 2]), PS[:, 4 + q % 2]).then_inc(vt_rdy, 1)
            for kt in range(4):
                act.wait_ge(spec_mm, 4 + kt + 1)
                if kt >= 2:
                    act.wait_ge(spec_rdy, 4 + kt - 1)
                act.copy(tE[:, kt % 2], PS[:, 2 * (kt % 2):2 * (kt % 2) + 2, 0:256]).then_inc(even_part, 1)
            for i in range(2):
                hi_of(chunk_index("qkv", i), spl(2 + i, 4, 512))
            for n in range(4):
                c2, odd = n // 2, n % 2
                act.wait_ge(y_f, n + 1)
                act.copy(yT[:, 0, c2, odd::2], yo[:, n % 2]).then_inc(y_hi, 1)
            for i in range(2, 4):
                hi_of(chunk_index("qkv", i), spl(i - 2, 4, 512))

            def from_psum(u, it=0):
                (g, t), par, m = UNITS[u], u % 2, it * 2
                act.wait_ge(pr_mm, m + u + 1)
                if u >= 2:
                    act.wait_ge(pr_lo, m + u - 1)
                    if UNITS[u - 2][0] != 2:
                        act.wait_ge(pr_r, m + n_normed(u - 2))
                ps, tt = PS[:, par], t + m
                if g == 0:
                    act.activation(bT[par], ps, ACT.Square).then_inc(pr_sq, 1)
                elif g == 1:
                    act.activation(bT[par][:, 0:128], ps[:, 0:128], ACT.Square).then_inc(pr_sq, 1)
                    if t < NT:
                        act.activation(nT[par][:, 128:384], ps[:, 256:512], ACT.Copy, scale=0.125 / WS)
                    act.activation(V[:, tt, 0:2], ps[:, 128:256].rearrange("p (h d) -> p h d", h=2), ACT.Copy,
                                   scale=1 / WS).then_inc(pr_v, 1)
                else:
                    act.activation(nT[par][:, 0:256], ps[:, 0:256], ACT.Copy, scale=1 / WS)
                    act.activation(V[:, tt, 2:6], ps[:, 256:512].rearrange("p (h d) -> p h d", h=4), ACT.Copy,
                                   scale=1 / WS).then_inc(pr_v, 1)

            def hi_parts(u, it=0):
                (g, t), par, m = UNITS[u], u % 2, it * 2
                if g != 2:
                    act.wait_ge(pr_r, m + n_normed(u))
                if g != 0:
                    act.wait_ge(pr_v, m + u + 1)
                if u >= 2:
                    act.wait_ge(pr_tm, m + u - 1)
                for out, _, src in stacks(g, t, par):
                    ins = act.copy(out, src)
                ins.then_inc(pr_hi, 1)

            def turned(u, it=0):
                (g, t), par, m = UNITS[u], u % 2, it * 2
                act.wait_ge(pr_tm, m + u + 1)
                ps = PS[:, 2 + par, :].bitcast(F16).rearrange("p (j t) -> p j t", t=P)
                if g == 0:
                    ins = act.copy(qT[:, :, tok(t + m)], ps)
                elif g == 2:
                    ins = act.copy(nkT.rearrange("p h a s -> p (h a) s")[:, :, tok(t + m)], ps)
                else:
                    ins = act.copy(kT.rearrange("p h a s -> p (h a) s")[:, :, tok(t + m)], ps[:, 0:4])
                    if t < NT:
                        ins = act.copy(nqT[:, :, tok(t + m)], ps[:, 4:8])
                ins.then_inc(pr_tc, 1)

            def slot(u, it=0):
                if u < NU:
                    from_psum(u, it)
                if 1 <= u <= NU:
                    hi_parts(u - 1, it)
                if u >= 2:
                    turned(u - 2, it)

            for g in (1, 2, 0):
                u0 = GROUP0[g]
                slot(u0)
                if g == 2:
                    for i in range(4, 6):
                        hi_of(chunk_index("qkv", i), spl(i - 2, 4, 512))
                slot(u0 + 1)
                with act.Fori(0, 3) as it:
                    for b in range(2):
                        slot(u0 + 2 + b, it)
                if g:
                    slot(u0 + 8)
                    slot(u0 + 9)
                if g == 1:
                    act.wait_ge(skew_set, 1)
                    for h in range(HN):
                        act.dma_start(skrow[19 * h + 2:19 * h + 17, 48:79], io["na_rpb"][0, h])\
                            .then_inc(skew_rows, 16)
                    act.wait_ge(skew_rows, 16 * HN)
                    act.dma_start(skew.ap().rearrange("h r c x -> (h r) c x"),
                                  skrow[0:19 * HN].unsqueeze(1).broadcast_to((19 * HN, 64, P))).then_inc(skew_out, 16)
            slot(NU)
            slot(NU + 1)

            def exponentials(u):
                act.wait_ge(s_max, u.n + 1)
                w = 7 if u.na else 10
                act.activation(flat(Pb[:, u.par, 0:w]), PSf[:, 1536 * u.par:1536 * u.par + w * P], ACT.Exp,
                               bias=nmax[:, u.par:u.par + 1], accum_out=esum[:, u.v % 4:u.v % 4 + 1]).then_inc(s_exp, 1)

            def copy_p(u):
                act.wait_ge(pt_mm, u.n + 1)
                if u.v >= 2:
                    act.wait_ge(o_mm, u.n - 1)
                lo, hi = (0, 7) if u.na else (4, 10)
                o = 1536 * u.par
                act.copy(flat(PT[:, u.par, lo:hi]), PSf[:, o + lo * P:o + hi * P]).then_inc(pt_a, 1)

            def attend(u):
                copy_p(u)
                if u.v < NV - 1:
                    exponentials(u.ahead(1))

            act.wait_ge(pr_mm, NU)
            exponentials(Unit(0))
            for v in range(3):
                attend(Unit(v))
            with act.Fori(0, HN - 1) as it:
                for v in range(3, 11):
                    attend(Unit(v, it))
            for v in range(27, 33):
                attend(Unit(v))
            with act.Fori(0, NT - 1) as it:
                for v in range(33, 41):
                    attend(Unit(v, it))
            for v in range(89, NV):
                attend(Unit(v))

            for n in range(2):
                act.wait_ge(gate_mm, n + 1)
                act.copy((gate1, gate2)[n], PSf[:, 1024 * n:1024 * n + 1024]).then_inc(gate_rdy, 1)
            for t in range(NT):
                act.wait_ge(mx_mm, t + 1)
                o = 2048 + 1024 * (t % 2)
                act.copy(mixT[:, 0, :, t * P:t * P + P], PSf[:, o:o + 768].rearrange("p (f t) -> p f t", f=6))\
                    .then_inc(mx_hi, 1)
            act.wait_ge(bias_add, NNA)
            for b in range(2):
                hi_of(chunk_index("fi", b), fiS[b])
            for t in range(NT):
                act.wait_ge(x1_sum, t + 1)
                if t:
                    act.wait_ge(sq1, t)
                act.activation(f32(104, D), x1[:, t], ACT.Square, accum_out=ss[:, t:t + 1]).then_inc(sq1, 1)
            for n in range(16):
                act.wait_ge(hT_mm, 20 + n + 1)
                if n >= 2:
                    act.wait_ge(hT_rdy, 20 + n - 1)
                f = n % KD
                act.activation(h2tmp[:, n % 2], PS[:, 4 + n % 4], ACT.Identity, scale=af[:, f, 0:1],
                               bias=mod[:, 24 + f, 0:1]).then_inc(hT_f, 1)

            def silu(b, j, first=False):
                act.wait_ge(fi_mm, j + 1)
                if not first:
                    act.wait_ge(fi_p, j)
                act.activation(sg, PSf[:, 2048 * b:2048 * b + 1024], ACT.Silu, scale=1 / WS).then_inc(fi_s, 1)

            def gated_hi(j):
                act.wait_ge(fi_p, j + 1)
                act.copy(prodT[:, 0, j, :], pr).then_inc(fi_hi, 1)

            act.wait_ge(hT_rdy, 36)
            c0 = chunk_index("fi", 0)
            for b in range(2):
                silu(b, b, b == 0)
                hi_of(c0 + 2 + b, fiS[b])
                gated_hi(b)
            with act.Fori(0, KF // 2 - 2) as it:
                for b in range(2):
                    silu(b, it * 2 + 2 + b)
                    act.wait_ge(raw_in[b], it * 32 + 16 * chunk_arrivals(c0 + 4 + b))
                    act.activation(flat(fiS[b][:, 0]), f32(RAW(b), 2048), ACT.Copy, scale=WS).then_inc(split_hi, 1)
                    gated_hi(it * 2 + 2 + b)
            for b in range(2):
                silu(b, KF - 2 + b)
                hi_of(chunk_index("fo", b), foS[b])
                gated_hi(KF - 2 + b)
            act.wait_ge(fi_mm, KF)
            act.dma_start(gfin, io["g_final"].partition_broadcast(P)).then_inc(gf_in, 16)

            c1 = chunk_index("fo", 0)

            def fo_hi(s, base_c, it=0):
                act.wait_ge(raw_in[s], it * 16 + 16 * chunk_arrivals(base_c))
                act.activation(flat(foS[s][:, 0]), f32(RAW(s), 2048), ACT.Copy, scale=WS).then_inc(split_hi, 1)

            def x2_square(t):
                act.wait_ge(fo_x, t + 1)
                if t:
                    act.wait_ge(fo_sq, t)
                act.activation(osq, x1[:, t], ACT.Square, accum_out=ss[:, t:t + 1]).then_inc(fo_sq, 1)

            with act.Fori(0, 4) as it:
                for b in range(2):
                    act.wait_ge(fo_used, it * 2 + b + 1)
                    fo_hi(b, c1 + 2 + b, it)
            for m in (10, 11):
                act.wait_ge(fo_used, m - 1)
                fo_hi(m % 2, c1 + m)
            act.wait_ge(fo_mm, 4)
            fo_hi(0, c1 + 12)
            for t in range(4):
                x2_square(t)
            with act.Fori(0, 4) as it:
                for b in range(2):
                    act.wait_ge(fo_used, it * 2 + b + 11)
                    fo_hi(1 - b, c1 + 13 + b, it)
            act.wait_ge(fo_used, 19)
            fo_hi(1, c1 + 21)
            for t in range(4, NT):
                x2_square(t)

        @block.vector
        def _(dve):
            own = Chain(dve, dve_own)

            def lo_of(c, dst):
                n = int(np.prod(dst.shape[2:]))
                dve.wait_ge(split_hi, n_split(c))
                dve.scalar_tensor_tensor(flat(dst[:, 1]), f32(RAW(chunk_slot(c)), n), WS, flat(dst[:, 0]),
                                         ALU.mult, ALU.subtract).then_inc(split_lo, 1)

            dve.wait_ge(small_in, N_SMALL)
            dve.tensor_copy(ident16, ident).then_inc(id16_rdy, 1)
            dve.wait_ge(cols_mm, 1)
            dve.tensor_copy(cols[:, 0:N_ROWS], PS[:, 4, 0:N_ROWS]).then_inc(cols_rdy, 1)
            dve.wait_ge(cols_rdy, 1)
            own.step(dve.tensor_scalar(cwb, cols[:, V_CW:V_CW + 18], 1 / WS, None, ALU.mult))
            own.step(dve.tensor_scalar(gkc, gq[:, 1], 1 / WS, None, ALU.mult))
            u, k = fu[0:FW], fk[0:FW]
            for layer in range(3):
                dve.wait_ge(mlp_mm, layer + 1)
                own.step(dve.tensor_scalar(u, PSf[0:FW, 0:S], fvec[0:FW, layer:layer + 1], fvec[0:FW, 3:4],
                                           ALU.add, ALU.mult))
                own.wait()
                own.step(dve.tensor_scalar(k, u, 1 / (2 * math.pi), MAGIC, ALU.mult, ALU.add))
                own.wait()
                own.step(dve.tensor_scalar(k, k, MAGIC, None, ALU.subtract))
                own.wait()
                for part in (TWO_PI_1, TWO_PI_2, TWO_PI_3):
                    own.step(dve.scalar_tensor_tensor(u, k, -part, u, ALU.mult, ALU.add))
                    own.wait()
                dve.tensor_scalar(u, u, PI_IN, -PI_IN, ALU.min, ALU.max).then_inc(mlp_arg, 1)
            for nt in range(NT):
                dve.wait_ge(taps_mm, nt + 1)
                own.step(dve.tensor_tensor(flat(fbd[:, nt % 2]), PS[:, 2 + nt % 2], decay[:, nt], ALU.mult))
                own.wait()
                own.step(dve.tensor_tensor(filt_a[:, nt], fbd[:, nt % 2, 0], fbd[:, nt % 2, 1], ALU.add))
                dve.tensor_tensor(filt_b[:, nt], fbd[:, nt % 2, 0], fbd[:, nt % 2, 1], ALU.subtract)\
                    .then_inc(taps_rdy, 1)
            for kt in range(4):
                par = kt % 2
                dve.wait_ge(even_part, kt + 1)
                oc, os = PS[:, 2 * par, 256:512], PS[:, 2 * par + 1, 256:512]
                ec, es = tE0[:, par, 0], tE0[:, par, 1]
                a = 1.0 / 1024
                dve.scalar_tensor_tensor(Fc[:, kt, 0:256], oc, a, ec, ALU.mult, ALU.add)
                dve.scalar_tensor_tensor(Fc[:, kt, 256:512], oc, -a, ec, ALU.mult, ALU.add)
                dve.scalar_tensor_tensor(Fs[:, kt, 0:256], os, a, es, ALU.mult, ALU.add)
                dve.scalar_tensor_tensor(Fs[:, kt, 256:512], os, a, es, ALU.mult, ALU.subtract).then_inc(spec_rdy, 1)
            dve.wait_ge(sq_done, 10)
            dve.tensor_scalar(ss[:, 0:10], ss[:, 0:10], 1.0 / D, EPS, ALU.mult, ALU.add).then_inc(ms_rdy, 1)
            dve.wait_ge(rs_rdy, 1)
            for t in range(10):
                dve.tensor_scalar(xs[:, t], xs[:, t], rs[:, t:t + 1], None, ALU.mult).then_inc(xn_rdy, 1)

            def modulation(t0, t1, a, scale0, gain0):
                n = t1 - t0
                own.step(dve.tensor_tensor(mod[:, t0:t1], PS[:, 7, 2 * t0:2 * t1].rearrange("p (t n) -> p t n", n=2),
                                           cols[:, V_BMOD + t0:V_BMOD + t1].unsqueeze(2).broadcast_to((P, n, 2)),
                                           ALU.add))
                own.wait()
                dve.scalar_tensor_tensor(a, mod[:, scale0:scale0 + 8], 1.0,
                                         cols[:, gain0:gain0 + 8].unsqueeze(2).broadcast_to((P, 8, 2)),
                                         ALU.add, ALU.mult).then_inc(mod_rdy, 1)

            dve.wait_ge(mod_used, 8)
            modulation(0, 16, am, 8, V_GMIX)
            lo_of(chunk_index("hy", 0), spl(0, KD, 256))

            def split_h(n, f, hi, lo):
                dve.wait_ge(hT_f, n + 1)
                own.step(dve.tensor_copy(hi, f))
                own.wait()
                dve.tensor_tensor(lo, f, hi, ALU.subtract).then_inc(hT_rdy, 1)

            for n in range(20):
                if n < 16:
                    f, o = n % KD, 512 * (n // KD)
                    split_h(n, htmp[:, n % 2], hT[:, 0, f, o:o + 512], hT[:, 1, f, o:o + 512])
                else:
                    f = 2 * (n - 16)
                    split_h(n, htmp[:, n % 2].rearrange("p (f t) -> p f t", f=2), hcT[:, 0, f:f + 2], hcT[:, 1, f:f + 2])
            lo_of(chunk_index("hy", 1), spl(1, KD, 256))
            for ct in range(6):
                dst = (uvT, accx, x2T)[ct // 2][:, ct % 2]
                ps = PSf[:, 1024 * (ct % 2):1024 * (ct % 2) + 1024]
                dve.wait_ge(hy_mid, ct + 1)
                own.step(dve.scalar_tensor_tensor(dst[:, 1:S], ps[:, 0:S - 1], cwb[:, ct:ct + 1], dst[:, 1:S],
                                                  ALU.mult, ALU.add))
                own.wait()
                ins = dve.scalar_tensor_tensor(dst[:, 0:S - 1], ps[:, 1:S], cwb[:, 12 + ct:13 + ct], dst[:, 0:S - 1],
                                               ALU.mult, ALU.add)
                if ct // 2 == 1:
                    own.step(ins)
                    own.wait()
                    ins = dve.tensor_tensor(uvT[:, ct % 2], uvT[:, ct % 2], dst, ALU.mult)
                ins.then_inc(hy_rdy, 1)
                if ct == 1:
                    lo_of(chunk_index("hy", 2), spl(0, KD, 256))
            dve.wait_ge(mod_used, 24)
            modulation(16, 48, af, 32, V_GFFN)
            for kt in range(4):
                par = kt % 2
                dve.wait_ge(even_part, 4 + kt + 1)
                oc, os = PS[:, 2 * par, 256:512], PS[:, 2 * par + 1, 256:512]
                ec, es = tE[:, par, 0], tE[:, par, 1]
                own.step(dve.tensor_tensor(V2c[:, 0:256], oc, ec, ALU.add))
                own.step(dve.tensor_tensor(V2c[:, 256:512], ec, oc, ALU.subtract))
                own.step(dve.tensor_tensor(V2s[:, 0:256], os, es, ALU.add))
                dve.tensor_tensor(V2s[:, 256:512], os, es, ALU.subtract).then_inc(spec_rdy, 1)
                dve.wait_ge(spec_rdy, 4 + kt + 1)
                own.step(dve.tensor_tensor(t1, V2c, Fc[:, kt], ALU.mult))
                own.step(dve.tensor_tensor(t2, V2s, Fs[:, kt], ALU.mult))
                own.step(dve.tensor_tensor(t3, V2c, Fs[:, kt], ALU.mult))
                own.step(dve.tensor_tensor(t4, V2s, Fc[:, kt], ALU.mult))
                own.wait()
                own.step(dve.tensor_tensor(Yc, t1, t2, ALU.subtract))
                own.step(dve.tensor_tensor(Ys, t3, t4, ALU.add))
                own.wait()
                if kt >= 2:
                    dve.wait_ge(inv_mm, kt - 1)
                dve.tensor_tensor(G[:, par, 0], Yc[:, 0:256], Yc[:, 256:512], ALU.add)
                dve.tensor_tensor(G[:, par, 1], Ys[:, 0:256], Ys[:, 256:512], ALU.subtract)
                dve.tensor_tensor(G[:, par, 2], Yc[:, 0:256], Yc[:, 256:512], ALU.subtract)
                dve.tensor_tensor(G[:, par, 3], Ys[:, 0:256], Ys[:, 256:512], ALU.add).then_inc(G_rdy, 1)
            for i in range(2):
                lo_of(chunk_index("qkv", i), spl(2 + i, 4, 512))
            dve.wait_ge(inv_mm, 4)
            for n in range(4):
                c2, odd = n // 2, n % 2
                if n >= 2:
                    dve.wait_ge(y_rdy, n - 1)
                own.step(dve.scalar_tensor_tensor(yo[:, n % 2], uvT[:, c2, odd::2], cols[:, V_SKIP + c2:V_SKIP + c2 + 1],
                                                  PS[:, 4 + n], ALU.mult, ALU.add))
                own.wait()
                dve.scalar_tensor_tensor(yo[:, n % 2], yo[:, n % 2], HS, x2T[:, c2, odd::2], ALU.mult, ALU.mult)\
                    .then_inc(y_f, 1)
                dve.wait_ge(y_hi, n + 1)
                dve.tensor_tensor(yT[:, 1, c2, odd::2], yo[:, n % 2], yT[:, 0, c2, odd::2], ALU.subtract)\
                    .then_inc(y_rdy, 1)
            for i in range(2, 4):
                lo_of(chunk_index("qkv", i), spl(i - 2, 4, 512))
            dve.wait_ge(gn_in, 32)
            for n, tab in enumerate((gc, gk)):
                s = (0.125 / WS, 1 / WS)[n]
                for o, w, g0 in ((0, 64, 0), (64, 32, 32), (96, 32, 0)):
                    v = tab.rearrange("p t a d -> p t (a d)")[:, :, o:o + w]
                    own.step(dve.scalar_tensor_tensor(v, v, s, gq[:, n, g0:g0 + w].unsqueeze(1).broadcast_to((P, NT, w)),
                                                      ALU.mult, ALU.mult))
            own.wait()

            def mean_square(u, it=0):
                (g, t), par, m = UNITS[u], u % 2, it * 2
                if g == 2:
                    return
                w = HQ if g == 0 else HKV
                dve.wait_ge(pr_sq, m + n_normed(u))
                own.step(dve.tensor_reduce(ssq[:, par, 0:w], bT[par][:, 0:w * HD].rearrange("p (h d) -> p h d", d=HD),
                                           AX, ALU.add))
                own.wait()
                dve.tensor_scalar(ssq[:, par, 0:w], ssq[:, par, 0:w], 1.0 / (HD * WS * WS), EPS, ALU.mult, ALU.add)\
                    .then_inc(pr_ms, 1)

            def rotate(u, it=0):
                (g, t), par, m = UNITS[u], u % 2, it * 2
                if g == 2:
                    return
                w = HQ if g == 0 else HKV
                dve.wait_ge(pr_rs, m + n_normed(u))
                if g == 1:
                    dve.wait_ge(pr_v, m + u + 1)
                if u >= 2:
                    dve.wait_ge(pr_hi, m + u - 1)
                n = nT[par][:, 0:w * HD].rearrange("p (h d) -> p h d", d=HD)
                b = bT[par][:, 0:w * HD].rearrange("p (h d) -> p h d", d=HD)
                dve.tensor_tensor(n, PS[:, par, 0:w * HD].rearrange("p (h d) -> p h d", d=HD),
                                  rsq[:, par, 0:w].unsqueeze(2).broadcast_to((P, w, HD)), ALU.mult).then_inc(pr_n, 1)
                dve.wait_ge(pr_n, m + n_normed(u))
                if t >= NT:
                    dve.tensor_tensor(n, n, gkc.unsqueeze(1).broadcast_to((P, w, HD)), ALU.mult).then_inc(pr_r, 1)
                    return
                tab = (gc if g == 0 else gk)[:, t + m]

                def of(a, o, k):
                    return tab[:, a, o:o + k].unsqueeze(1).broadcast_to((P, w, k))

                own.step(dve.tensor_tensor(b[:, :, 0:32], n[:, :, 32:64], of(1, 0, 32), ALU.mult))
                own.step(dve.tensor_tensor(b[:, :, 32:64], n[:, :, 0:32], of(1, 32, 32), ALU.mult))
                own.wait()
                own.step(dve.tensor_tensor(n, n, of(0, 0, 64), ALU.mult))
                own.wait()
                dve.tensor_tensor(n, n, b, ALU.add).then_inc(pr_r, 1)

            def lo_parts(u, it=0):
                (g, t), par, m = UNITS[u], u % 2, it * 2
                dve.wait_ge(pr_hi, m + u + 1)
                for hi, lo, src in stacks(g, t, par):
                    ins = dve.tensor_tensor(lo, src, hi, ALU.subtract)
                ins.then_inc(pr_lo, 1)

            def slot(u, it=0):
                if u < NU:
                    mean_square(u, it)
                if 1 <= u <= NU:
                    lo_parts(u - 1, it)
                if u < NU:
                    rotate(u, it)

            for g in (1, 2, 0):
                u0 = GROUP0[g]
                slot(u0)
                if g == 2:
                    for i in range(4, 6):
                        lo_of(chunk_index("qkv", i), spl(i - 2, 4, 512))
                slot(u0 + 1)
                with dve.Fori(0, 3) as it:
                    own.enter(it, {1: 8, 2: 0, 0: 8}[g])
                    for b in range(2):
                        slot(u0 + 2 + b, it)
                    own.leave(3)
                if g:
                    slot(u0 + 8)
                    slot(u0 + 9)
            slot(NU)

            def maximum(u):
                dve.wait_ge(s_mm, u.n + 1)
                o, w = 1536 * u.par, (7 if u.na else 10) * P
                if u.na:
                    dve.wait_ge(bias_rdy, u.blk * 5 + 5)
                    b = bias[:, u.blk % 2, bias_kind(u.j)].rearrange("p i w -> p (i w)")
                    dve.tensor_tensor(PSf[:, o:o + 640], PSf[:, o:o + 640], b, ALU.add).then_inc(bias_add, 1)
                    dve.wait_ge(bias_add, u.n + 1)
                dve.tensor_reduce(nmax[:, u.par:u.par + 1], PSf[:, o:o + w], AX, ALU.max, negate=True)\
                    .then_inc(s_max, 1)

            def copy_p(u):
                if u.na:
                    return
                dve.wait_ge(pt_mm, u.n + 1)
                dve.wait_ge(o_mm, u.n - 1)
                dve.tensor_copy(flat(PT[:, u.par, 0:4]), PSf[:, 1536 * u.par:1536 * u.par + 512]).then_inc(pt_d, 1)

            def normalise(u):
                dve.wait_ge(o_mm, u.n + 1)
                own.step(dve.reciprocal(rcp[:, u.par:u.par + 1], esum[:, u.v % 4:u.v % 4 + 1]))
                own.wait()
                if u.na:
                    dst = mixtok[:, u.j, bass.ds(u.blk * HD + HQ * HD, HD)]
                else:
                    dst = mixtok[:, u.blk, u.j * HD:u.j * HD + HD]
                dve.tensor_scalar(dst, PS[:, 6 + u.par, 0:HD], rcp[:, u.par:u.par + 1], None, ALU.mult)\
                    .then_inc(o_rdy, 1)

            def attend(u):
                if u.v < NV - 1:
                    maximum(u.ahead(1))
                copy_p(u)
                if u.v:
                    normalise(u.ahead(-1))

            maximum(Unit(0))
            for v in range(3):
                attend(Unit(v))
            with dve.Fori(0, HN - 1) as it:
                own.enter(it, 8)
                for v in range(3, 11):
                    attend(Unit(v, it))
                own.leave(HN - 1)
            for v in range(27, 33):
                attend(Unit(v))
            with dve.Fori(0, NT - 1) as it:
                own.enter(it, 8)
                for v in range(33, 41):
                    attend(Unit(v, it))
                own.leave(NT - 1)
            for v in range(89, NV):
                attend(Unit(v))
            normalise(Unit(NV - 1))

            own.step(dve.memset(ones, 1.0))
            own.wait()
            for n in range(2):
                if n:
                    dve.wait_ge(gate_mm, 1)
                g0 = (16, 40)[n]
                dve.tensor_tensor(diag, ident.unsqueeze(1).broadcast_to((P, 8, P)),
                                  mod[:, g0:g0 + 8, 0:1].broadcast_to((P, 8, P)), ALU.mult).then_inc(gate_d, 1)
            for t in range(NT):
                dve.wait_ge(mx_hi, t + 1)
                o, cut = 2048 + 1024 * (t % 2), slice(t * P, t * P + P)
                dve.tensor_tensor(mixT[:, 1, :, cut], PSf[:, o:o + 768].rearrange("p (f t) -> p f t", f=6),
                                  mixT[:, 0, :, cut], ALU.subtract).then_inc(mx_lo, 1)
            for b in range(2):
                lo_of(chunk_index("fi", b), fiS[b])

            def residual(t):
                dve.wait_ge(wo_mm, t + 1)
                dve.scalar_tensor_tensor(wtmp[:, t % 2], PSf[:, 1024 * (t % 2):1024 * (t % 2) + 1024], 1 / WS, gate1,
                                         ALU.mult, ALU.mult).then_inc(x1_rdy, 1)
                dve.wait_ge(x1_rdy, t + 1)
                dve.tensor_tensor(x1[:, t], x1[:, t], wtmp[:, t % 2], ALU.add).then_inc(x1_sum, 1)

            def mean1(half):
                dve.wait_ge(sq1, 4 * half + 4)
                dve.tensor_scalar(ss[:, 4 * half:4 * half + 4], ss[:, 4 * half:4 * half + 4], 1.0 / D, EPS,
                                  ALU.mult, ALU.add).then_inc(ms1, 1)

            def normalise1(half):
                dve.wait_ge(rs1, half + 1)
                if half:
                    dve.wait_ge(hT_mm, 20 + KD)
                for i in range(4):
                    ins = dve.tensor_scalar(xn1[:, i], x1[:, 4 * half + i], rs[:, 4 * half + i:4 * half + i + 1], None,
                                            ALU.mult)
                ins.then_inc(xn1_rdy, 1)

            dve.wait_ge(gate_rdy, 2)
            dve.wait_ge(x1_in, 64)
            for t in range(NT):
                residual(t)
                if t == 4:
                    mean1(0)
                if t == 6:
                    normalise1(0)
            mean1(1)

            for n in range(16):
                if n == 8:
                    normalise1(1)
                f, o = n % KD, 512 * (n // KD)
                split_h(20 + n, h2tmp[:, n % 2], hT[:, 0, f, o:o + 512], hT[:, 1, f, o:o + 512])

            def gated(b, j, first=False):
                dve.wait_ge(fi_s, j + 1)
                if not first:
                    dve.wait_ge(fi_lo, j)
                dve.scalar_tensor_tensor(pr, PSf[:, 2048 * b + 1024:2048 * b + 2048], GS / WS, sg, ALU.mult, ALU.mult)\
                    .then_inc(fi_p, 1)

            def gated_lo(j):
                dve.wait_ge(fi_hi, j + 1)
                dve.tensor_tensor(prodT[:, 1, j, :], pr, prodT[:, 0, j, :], ALU.subtract).then_inc(fi_lo, 1)

            c0 = chunk_index("fi", 0)
            for b in range(2):
                gated(b, b, b == 0)
                lo_of(c0 + 2 + b, fiS[b])
                gated_lo(b)
            with dve.Fori(0, KF // 2 - 2) as it:
                for b in range(2):
                    gated(b, it * 2 + 2 + b)
                    dve.wait_ge(split_hi, it * 2 + n_split(c0 + 4 + b))
                    dve.scalar_tensor_tensor(flat(fiS[b][:, 1]), f32(RAW(b), 2048), WS, flat(fiS[b][:, 0]),
                                             ALU.mult, ALU.subtract).then_inc(split_lo, 1)
                    gated_lo(it * 2 + 2 + b)
            for b in range(2):
                gated(b, KF - 2 + b)
                lo_of(chunk_index("fo", b), foS[b])
                gated_lo(KF - 2 + b)

            c1 = chunk_index("fo", 0)

            def fo_lo(s, base_c, it=0):
                dve.wait_ge(split_hi, it + n_split(base_c))
                dve.scalar_tensor_tensor(flat(foS[s][:, 1]), f32(RAW(s), 2048), WS, flat(foS[s][:, 0]),
                                         ALU.mult, ALU.subtract).then_inc(split_lo, 1)

            def gate_out(t):
                dve.wait_ge(fo_mm, t + 1)
                dve.tensor_tensor(otmp[:, t % 4], PSf[:, 1024 * (t % 4):1024 * (t % 4) + 1024], gate2, ALU.mult)\
                    .then_inc(fo_r, 1)
                dve.wait_ge(fo_r, t + 1)
                dve.tensor_tensor(x1[:, t], x1[:, t], otmp[:, t % 4], ALU.add).then_inc(fo_x, 1)

            def mean_out(t):
                dve.wait_ge(fo_sq, t + 1)
                dve.tensor_scalar(ss[:, t:t + 1], ss[:, t:t + 1], 1.0 / D, EPS, ALU.mult, ALU.add).then_inc(fo_ms, 1)

            def norm_out(t):
                dve.wait_ge(fo_rs, t + 1)
                dve.scalar_tensor_tensor(x1[:, t], x1[:, t], rs[:, t:t + 1], gfin, ALU.mult, ALU.mult).then_inc(fo_y, 1)

            with dve.Fori(0, 4) as it:
                for b in range(2):
                    fo_lo(b, c1 + 2 + b, it * 2)
            for m in (10, 11):
                fo_lo(m % 2, c1 + m)
            gate_out(0)
            gate_out(1)
            fo_lo(0, c1 + 12)
            gate_out(2)
            gate_out(3)
            dve.wait_ge(gf_in, 16)
            for t in range(4):
                mean_out(t)
                if t:
                    norm_out(t - 1)
            norm_out(3)
            with dve.Fori(0, 4) as it:
                for b in range(2):
                    fo_lo(1 - b, c1 + 13 + b, it * 2)
            fo_lo(1, c1 + 21)
            for t in range(4, NT):
                gate_out(t)
                if t > 4:
                    mean_out(t - 1)
                if t > 5:
                    norm_out(t - 2)
            mean_out(NT - 1)
            norm_out(NT - 2)
            norm_out(NT - 1)


INPUTS = ["x", "c", "ctx", "c_ctx", "w_mod", "b_mod", "g_mix", "g_ffn", "w_in", "w_out", "hy_conv_w", "hy_conv_b",
          "hy_f_w1", "hy_f_b1", "hy_f_w2", "hy_f_b2", "hy_f_w3", "hy_f_b3", "hy_f_wout", "hy_f_freq", "hy_skip",
          "qk_g_q", "qk_g_k", "na_rpb", "w_ffn_in", "w_ffn_out", "g_final"]


def kernel(**inputs):
    import concourse.bacc as bacc
    from concourse.bass_utils import run_bass_kernel_spmd

    nc = bacc.Bacc("TRN2", target_bir_lowering=False, num_devices=1)
    tables = constants()
    arrays = {"in_" + n: np.ascontiguousarray(inputs[n]) for n in INPUTS} | tables
    dram = {n: nc.dram_tensor(n, a.shape, mybir.dt.from_np(a.dtype), kind="ExternalInput").ap()
            for n, a in arrays.items()}
    out = nc.dram_tensor("out", (1, S, D), F32, kind="ExternalOutput").ap()
    build(nc, {n: dram["in_" + n] for n in INPUTS}, {n[4:]: dram[n] for n in tables}, out)
    return run_bass_kernel_spmd(nc, [arrays], core_ids=[0]).results[0]["out"]
```

```python
import math
from contextlib import ExitStack

import numpy as np

import concourse.bass as bass
import concourse.mybir as mybir

F32 = mybir.dt.float32
F16 = mybir.dt.float16
ACT = mybir.ActivationFunctionType
ALU = mybir.AluOpType
AX = mybir.AxisListType.X

P = 128
S, C, D = 1024, 256, 1024
NT, NC, KD = S // P, C // P, D // P
HD = 64
HQ, HKV, HN = 8, 2, 4
HYW = 256
GRID_W, ROWS, KH, KW = 64, 16, 8, 16
FH = 2816
KF = FH // P
QKV0 = 3 * HYW
FW, EMB = 64, 33
EPS = 1e-6
NEG = -1e30
HALF = S // 2

WS = 2.0 ** 8
HS = 2.0 ** -6
GS = 2.0 ** -8
MAGIC = 1.5 * 2.0 ** 23
TWO_PI_1 = 6.28125
TWO_PI_2 = float(np.float32(np.round((2 * math.pi - TWO_PI_1) * 2 ** 21) / 2 ** 21))
TWO_PI_3 = float(np.float32(2 * math.pi - TWO_PI_1 - TWO_PI_2))
PI_IN = 3.1415925

V_BMOD, V_GMIX, V_GFFN, V_C, V_CC, V_CW, V_CB, V_SKIP = 0, 48, 56, 64, 72, 80, 98, 104
N_ROWS = 106

CHUNKS = (["mod"] * 8 + ["ff", "ff", "hy", "ff", "ff", "hy"] + ["late"] * 3 + ["hy"] + ["late"] * 9
          + ["fwd", "fwd", "late", "inv", "fwd", "late", "inv", "fwd", "late", "inv", "late", "inv"]
          + ["qkv"] * 6 + ["wo"] * 4 + ["fi"] * KF + ["fo"] * KF)
N_EARLY = CHUNKS.index("wo")
AS_IS = ("ff", "mod", "late", "fwd", "inv")
GW = 1024


def chunk_slot(c):
    return c % 4 if c < N_EARLY else (c - N_EARLY) % 2


def chunk_arrivals(c):
    return sum(1 + (CHUNKS[i] == "fi") for i in range(c + 1) if chunk_slot(i) == chunk_slot(c))


def chunk_before(c):
    return next((i for i in range(c - 1, -1, -1) if chunk_slot(i) == chunk_slot(c)), None)


def n_of_kind(c, *kinds):
    return sum(k in kinds for k in CHUNKS[:c + 1])


def n_split(c):
    return sum(k not in AS_IS and k != "wo" for k in CHUNKS[:c + 1])


def chunk_index(kind, n):
    return [i for i, k in enumerate(CHUNKS) if k == kind][n]


def flat(v):
    names = "abcd"[:len(v.shape) - 1]
    return v if len(names) == 1 else v.rearrange(f"p {' '.join(names)} -> p ({' '.join(names)})")


def constants():
    pos = np.arange(S)
    inv = (10000.0 ** (-np.arange(HD // 4, dtype=np.float32) / (HD // 4))).astype(np.float32)
    ang = np.concatenate([(pos // GRID_W).astype(np.float32)[:, None] * inv,
                          (pos % GRID_W).astype(np.float32)[:, None] * inv], -1).astype(np.float32)
    cos, sin = np.cos(ang.astype(np.float64)), np.sin(ang.astype(np.float64))
    rope = np.stack([np.concatenate([cos, cos], 1), np.concatenate([-sin, sin], 1)], 1)
    rope = rope.reshape(NT, P, 2, HD).transpose(1, 0, 2, 3)

    perm = np.concatenate([np.arange(0, S, 2), np.arange(1, S, 2)])
    t = np.linspace(0.0, 1.0, S, dtype=np.float32)[:, None]
    bands = (EMB - 1) // 2
    w = (np.float32(2.0 * math.pi) * np.arange(S, dtype=np.float32)[:, None] / np.float32(S)).astype(np.float32)
    fr = np.linspace(1e-4, bands - 1, bands, dtype=np.float32)[None, :]
    arg = (fr * w).astype(np.float32).astype(np.float64)
    z = np.concatenate([t, np.cos(arg), -np.sin(arg)], -1)[perm].T
    zt = np.zeros((P, HALF))
    zt[0:EMB], zt[64:64 + EMB] = z[:, :HALF], z[:, HALF:]
    deltas = np.linspace(math.log(1e-2) / 1.5, math.log(1e-2) / 0.3, HYW, dtype=np.float32)
    decay = np.exp((-t * np.abs(deltas)).astype(np.float64))
    decay = np.concatenate([decay, decay], 1)
    decay[0, HYW:] = 0.0
    decay = decay[perm].reshape(NT, P, 2 * HYW).transpose(1, 0, 2)

    n = np.arange(S)[:, None]
    k = np.arange(HALF)[None, :]
    theta = np.pi * ((n * (2 * k + 1)) % 4096) / 2048.0
    cs = np.stack([np.cos(theta), np.sin(theta)], 1)[perm]
    fwd = cs.reshape(NT, P, 2, 4, P).transpose(3, 1, 0, 2, 4)
    inv_t = cs.transpose(2, 1, 0).reshape(4, P, 2, S)

    w_ = np.arange(P) % GRID_W
    wk = np.arange(GRID_W)
    first = np.clip(w_ - KW // 2, 0, GRID_W - KW)[:, None]
    cmask = np.where((wk >= first) & (wk < first + KW), 0.0, NEG)
    rmask = np.zeros((P, 5, 10))
    for n_, tile in enumerate([0, 1, 3, 6, 7]):
        for p in range(P):
            r = 2 * tile + p // GRID_W
            rs = min(max(r - KH // 2, 0), ROWS - KH)
            for i in range(10):
                kr = 2 * window(tile) + i
                rmask[p, n_, i] = 0.0 if rs <= kr < rs + KH else NEG
    out = dict(ident=np.eye(P), rope=rope, zt=zt, decay=decay, fwd=fwd, inv=inv_t, cmask=cmask, rmask=rmask)
    return {"cst_" + n_: np.ascontiguousarray(a, np.float32) for n_, a in out.items()}


def window(t):
    return min(max(t - 2, 0), 3)


def bias_kind(t):
    return {0: 0, 1: 1, 6: 3, 7: 4}.get(t, 2)


def bias_shift(kind):
    return [8, 6, 4, 2, 0][kind]


class Unit:

    def __init__(self, v, it=0):
        self.v, self.it, self.par, self.na = v, it, v % 2, v < HN * NT
        self.n = v + 8 * it
        w = v if self.na else v - HN * NT
        self.blk, self.j = w // 8 + it, w % 8
        self.kv = None if self.na else self.j // (HQ // HKV)
        self.n_gqa = self.n - HN * NT
        self.banks = [range(0, 4), range(4, 7)] if self.na else [range(0, 4), range(4, 8), range(8, 10)]

    def turned(self, bank):
        return 2 * self.n + bank + 1 if self.na else 2 * HN * NT + 3 * self.n_gqa + bank + 1

    def ahead(self, d):
        return Unit(self.v + d, self.it)


class Chain:

    def __init__(self, eng, sem):
        self.eng, self.sem, self.n = eng, sem, 0

    def step(self, ins):
        ins.then_inc(self.sem, 1)
        self.n = self.n + 1

    def wait(self):
        self.eng.wait_ge(self.sem, self.n)

    def enter(self, it, per):
        self.base = self.n
        self.per = per
        self.n = it * per + self.base

    def leave(self, count):
        self.n = self.base + count * self.per


def build(nc, io, cst, out):
    ctx = ExitStack()
    with ctx:
        sem = lambda name: ctx.enter_context(nc.semaphore(name))
        arena = ctx.enter_context(nc.sbuf_tensor("arena", [P, 207 * 256], F32))
        PS = ctx.enter_context(nc.psum_tensor("PS", [P, 8, 512], F32))
        skew = nc.dram_tensor("skewed_bias_rows", (HN, 19, 64, P), F32, kind="Internal")

        def f32(kb, *shape):
            n = int(np.prod(shape))
            o = int(kb * 256)
            v = arena[:, o:o + n]
            names = "abcd"[:len(shape)]
            if len(shape) > 1:
                v = v.rearrange(f"p ({' '.join(names)}) -> p {' '.join(names)}",
                                **{c: s for c, s in zip(names, shape)})
            return v

        def f16(kb, *shape):
            n = int(np.prod(shape))
            o = int(kb * 256)
            v = arena[:, o:o + n // 2].bitcast(F16)
            names = "abcd"[:len(shape)]
            if len(shape) > 1:
                v = v.rearrange(f"p ({' '.join(names)}) -> p {' '.join(names)}",
                                **{c: s for c, s in zip(names, shape)})
            return v

        ident = f32(0, P)
        ident16 = f16(0.5, P)
        cols = f32(0.75, P)
        mod = f32(1.25, 48, 2)
        am = f32(1.625, 8, 2)
        af = f32(1.6875, 8, 2)
        silu_c = f32(1.75, 8, 2)
        cwb = f32(1.8125, 18)
        fvec = f32(1.9, 4)
        ss = f32(2.0, 16)
        rs = f32(2.0625, 16)
        neghalf = f32(2.125, 16)
        ones1 = f32(2.1875, 1)
        ssq = f32(2.25, 2, 8)
        rsq = f32(2.3125, 2, 8)
        nmax = f32(2.375, 2)
        esum = f32(2.40625, 4)
        rcp = f32(2.4375, 2)
        gq = f32(2.5, 2, HD)
        rmask = f32(3.0, 5, 10)
        cmask = f32(3.25, GRID_W)
        gkc = f32(3.5, HD)

        PSf = PS[:, :, :].rearrange("p a b -> p (a b)")
        RAW = lambda s: 4 + 8 * s
        Z = 108

        def raw(c, *shape):
            return f32(RAW(chunk_slot(c)), *shape)

        def spl(slot, *shape):
            return f16(36 + 8 * slot, 2, *shape)

        hT = f16(68, 2, KD, S)
        hcT = f16(100, 2, KD, C)
        yT = f16(Z, 2, 2, S)
        x2T = f32(Z + 8, 2, S)
        uvT = f32(Z + 16, 2, S)
        vtok = f32(Z + 24, NT, HYW)
        Fc = f32(Z + 32, 4, 2 * HYW)
        Fs = f32(Z + 40, 4, 2 * HYW)
        zt = f32(Z + 8, HALF)
        fu = f32(Z + 12, HALF)
        fk = f32(Z + 16, HALF)
        fh = f32(Z + 20, HALF)
        mrow = f32(Z, 2, GW)
        macc = f32(Z, 2, GW)
        decay = f32(Z + 24, NT, 2 * HYW)
        fw = f32(Z + 40, 4, P)
        fwo = f32(Z + 42, 2 * HYW)
        fbd = f32(Z + 44, 2, 2, HYW)
        filt_a = f32(52, NT, HYW)
        filt_b = f32(60, NT, HYW)
        rows = f32(Z + 48, P)
        accx = f32(Z + 48, 2, S)
        htmp = f32(Z + 48, 2, 512)
        tE = f32(Z + 56, 2, 2, HYW)
        tE0 = f32(Z + 52, 2, 2, HYW)
        xs = f32(Z + 59, 10, D)
        V2c = f32(Z + 60, 512)
        V2s = f32(Z + 62, 512)
        t1 = f32(Z + 64, 512)
        t2 = f32(Z + 66, 512)
        Yc = f32(Z + 68, 512)
        Ys = f32(Z + 70, 512)
        G = f32(Z + 72, 2, 4, HYW)
        yo = f32(Z + 80, 2, 512)
        t3 = f32(Z + 84, 512)
        t4 = f32(Z + 48, 512)
        qT = f16(Z + 8, HQ, S)
        kT = f16(Z + 24, HKV, 2, S + C)
        V = f32(Z + 34, NT + NC, 6, HD)
        nqT = f16(Z + 59, HN, S)
        nkT = f16(Z + 67, HN, 2, S + C)
        nT = [f32(Z + 49, 512), f32(Z + 51, 512)]
        bT = [f32(Z + 53, 512), f32(Z + 55, 512)]
        stk = [f16(Z + 57, 1024), f16(Z + 95, 1024)]
        skrow = f32(Z + 97, P)
        gc = f32(Z + 87, NT, 2, HD)
        gk = f32(Z + 91, NT, 2, HD)
        Pb = f32(Z + 49, 2, 10, P)
        J = f32(20, 2, 18, GRID_W)
        bias = f32(36, 2, 5, 10, GRID_W)
        mixtok = f32(68, NT, 768)
        PT = f32(92, 2, 10, P)
        woS = [f16(Z + 59 + 8 * i, 2, 4, 512) for i in range(4)]
        mixT = f16(Z + 8, 2, 6, S)
        gate1 = f32(Z + 95, D)
        gate2 = f32(Z + 91, D)
        x1 = f32(20, NT, D)
        ones = f32(Z + 32, P)
        diag = f32(Z + 33, 8, P)
        xn1 = f32(Z + 32, 4, D)
        wtmp = f32(Z + 49, 2, D)
        h2tmp = f32(100, 2, 512)
        fiS = [f16(52, 2, 8, 256), f16(60, 2, 8, 256)]
        foS = [f16(52, 2, 2, 1024), f16(60, 2, 2, 1024)]
        prodT = f16(Z, 2, KF, S)
        sg = f32(100, S)
        pr = f32(104, S)
        gfin = f32(68, D)
        otmp = f32(72, 4, D)
        osq = f32(88, D)

        first_in = sem("first_small_in")
        small_in = sem("filter_network_in")
        rest_in = sem("rest_in")
        x_in = [sem(f"x_in{i}") for i in range(3)]
        raw_in = [sem(f"raw_in{i}") for i in range(4)]
        split_hi = sem("split_hi")
        split_lo = sem("split_lo")
        wo_split = sem("w_out_split")
        id16_rdy = sem("ident16_ready")
        cols_rdy = sem("columns_ready")
        silu_rdy = sem("silu_of_c_ready")
        mlp_mm = sem("filter_layer_product")
        mlp_arg = sem("filter_layer_argument")
        mlp_h = sem("filter_layer_value")
        taps_mm = sem("filter_taps_product")
        taps_rdy = sem("filter_taps_ready")
        spec_mm = sem("spectrum_product")
        even_part = sem("even_part_copied")
        spec_rdy = sem("spectrum_ready")
        cols_mm = sem("columns_transposed")
        mod_used = sem("modulation_chunk_used")
        mrow_rdy = sem("modulation_row_copied")
        mcol_mm = sem("modulation_by_feature")
        late_used = sem("late_product_added")
        late_mm = sem("late_group_by_feature")
        late_rdy = sem("late_groups_ready")
        mod_rdy = sem("modulation_ready")
        sq_done = sem("squares_summed")
        ms_rdy = sem("mean_square_ready")
        rs_rdy = sem("inverse_root_ready")
        xn_rdy = sem("x_normalised")
        hT_mm = sem("h_transposed")
        hT_f = sem("h_modulated")
        hT_rdy = sem("h_split")
        hy_mm = sem("hyena_projection")
        hy_mid = sem("middle_tap")
        hy_rdy = sem("short_convolution")
        vt_mm = sem("v_transposed")
        vt_rdy = sem("v_by_token")
        G_rdy = sem("folded_spectrum")
        inv_mm = sem("inverse_products")
        y_f = sem("hyena_output")
        y_hi = sem("hyena_output_hi")
        y_rdy = sem("hyena_output_split")
        gn_in = sem("gains_in")
        gt_rdy = sem("rope_tables_ready")
        pr_mm = sem("qkv_projection")
        pr_sq = sem("qk_squares")
        pr_n = sem("qk_scaled")
        pr_ms = sem("qk_mean_square")
        pr_rs = sem("qk_inverse_root")
        pr_r = sem("qk_rotated")
        pr_hi = sem("qk_hi")
        pr_lo = sem("qk_lo")
        pr_v = sem("values_copied")
        pr_tm = sem("qk_transposed")
        pr_tc = sem("qk_transposed_copied")
        skew_rows = sem("bias_rows_in")
        skew_set = sem("bias_rows_cleared")
        skew_out = sem("bias_rows_out")
        J_in = [sem("bias_table_in0"), sem("bias_table_in1")]
        bias_add = sem("bias_added")
        bias_rdy = sem("bias_ready")
        s_mm = sem("scores")
        s_max = sem("score_maximum")
        s_exp = sem("exponentials")
        pt_mm = sem("probabilities_transposed")
        pt_d = sem("probabilities_copied_by_vector")
        pt_a = sem("probabilities_copied_by_scalar")
        o_mm = sem("values_weighted")
        o_rdy = sem("attention_output")
        gate_d = sem("gate_diagonal")
        gate_mm = sem("gate_spread")
        gate_rdy = sem("gate_ready")
        mx_mm = sem("mix_transposed")
        mx_hi = sem("mix_hi")
        mx_lo = sem("mix_lo")
        wo_mm = sem("output_projection")
        x1_rdy = sem("x1_ready")
        x1_sum = sem("x1_summed")
        x1_in = sem("x_again_in")
        sq1 = sem("x1_squares")
        ms1 = sem("x1_mean_square")
        rs1 = sem("x1_inverse_root")
        xn1_rdy = sem("x1_normalised")
        fi_mm = sem("ffn_in_product")
        fi_s = sem("silu_done")
        fi_p = sem("gated")
        fi_hi = sem("gated_hi")
        fi_lo = sem("gated_lo")
        fo_used = sem("ffn_out_chunk_used")
        fo_x = sem("x2_summed")
        fo_mm = sem("ffn_out_product")
        fo_r = sem("x2_ready")
        fo_sq = sem("x2_squares")
        fo_ms = sem("x2_mean_square")
        fo_rs = sem("x2_inverse_root")
        fo_y = sem("output_row_ready")
        gf_in = sem("g_final_in")
        out_done = sem("output_stored")
        dve_own = sem("vector_steps")
        pool_own = sem("pool_steps")

        block = ctx.enter_context(nc.Block())
        x_rows = io["x"].rearrange("b (t p) d -> p (b t) d", p=P)
        ctx_rows = io["ctx"].rearrange("b (t p) d -> p (b t) d", p=P)
        out_rows = out.rearrange("b (t p) d -> p (b t) d", p=P)
        w_mod = io["w_mod"][0].rearrange("(k p) n -> p k n", p=P)
        w_in = io["w_in"][0].rearrange("(k p) n -> p k n", p=P)
        w_out = io["w_out"][0].rearrange("(k p) n -> p k n", p=P)
        w_fi = io["w_ffn_in"][0].rearrange("(k p) n -> p k n", p=P)
        w_fo = io["w_ffn_out"][0].rearrange("(k p) n -> p k n", p=P)
        first = [
            (rows[V_C:V_C + 8], io["c"][0].rearrange("(t p) -> t p", p=P)),
            (rows[V_CC:V_CC + 8], io["c_ctx"].rearrange("(t p) -> t p", p=P)),
            (ident, cst["ident"]),
            (rows[V_BMOD:V_BMOD + 48], io["b_mod"][0].rearrange("(t p) -> t p", p=P)),
            (rows[V_GMIX:V_GMIX + 8], io["g_mix"][0].rearrange("(t p) -> t p", p=P)),
            (rows[V_GFFN:V_GFFN + 8], io["g_ffn"][0].rearrange("(t p) -> t p", p=P)),
            (rows[V_CW:V_CW + 18], io["hy_conv_w"][0].rearrange("i (t p) -> (i t) p", p=P)),
            (rows[V_CB:V_CB + 6], io["hy_conv_b"][0].rearrange("(t p) -> t p", p=P)),
            (rows[V_SKIP:V_SKIP + 2], io["hy_skip"][0].rearrange("(t p) -> t p", p=P)),
        ]
        small = [(zt, cst["zt"])]
        for h in range(2):
            small.append((fw[64 * h:64 * h + EMB, 0, 0:FW], io["hy_f_w1"][0]))
            small += [(fvec[64 * h:64 * h + FW, n:n + 1], io[v].rearrange("a f -> f a"))
                      for n, v in enumerate(("hy_f_b1", "hy_f_b2", "hy_f_b3", "hy_f_freq"))]
            small += [(fw[64 * h:64 * h + FW, n, 0:FW], io[v][0]) for n, v in ((1, "hy_f_w2"), (2, "hy_f_w3"))]
            small.append((fwo[64 * h:64 * h + FW], io["hy_f_wout"][0]))
        rest = [
            (decay, cst["decay"]),
            (gq[:, 0], io["qk_g_q"][0].partition_broadcast(P)),
            (gq[:, 1], io["qk_g_k"][0].partition_broadcast(P)),
            (rmask, cst["rmask"]),
            (cmask, cst["cmask"]),
        ]
        N_FIRST = len(first) * 16
        N_REST = len(rest) * 16
        N_SMALL = len(small) * 16

        UNITS = [(g, t) for g in (1, 2, 0) for t in range(NT + (NC if g else 0))]
        NU = len(UNITS)
        GROUP0 = {1: 0, 2: NT + NC, 0: 2 * (NT + NC)}

        def n_normed(u):
            return sum(g != 2 for g, _ in UNITS[:u + 1])

        NV = HN * NT + HQ * NT
        NNA = HN * NT

        def arrived(eng, c, more=0):
            eng.wait_ge(raw_in[chunk_slot(c)], more * 16 + 16 * chunk_arrivals(c))

        def stacks(g, t, par):
            out = []
            n_k = {1: HKV, 2: HN, 0: 0}[g]
            if n_k:
                v = stk[par][:, 0:n_k * 256].rearrange("p (h a r d) -> p h a r d", h=n_k, a=2, r=2)
                src = nT[par][:, 0:n_k * HD].rearrange("p (h d) -> p h d", d=HD).unsqueeze(2)\
                    .broadcast_to((P, n_k, 2, HD))
                out.append((v[:, :, 0], v[:, :, 1], src))
            if g == 0 or (g == 1 and t < NT):
                n_q, o, s = (HQ, 0, 0) if g == 0 else (HN, 512, 128)
                v = stk[par][:, o:o + n_q * 128].rearrange("p (h a d) -> p h a d", h=n_q, a=2)
                out.append((v[:, :, 0], v[:, :, 1], nT[par][:, s:s + n_q * HD].rearrange("p (h d) -> p h d", d=HD)))
            return out

        def tok(t):
            return bass.ds(t * P, P)

        @block.sync
        def _(sp):
            def load(c, src, shape):
                before = chunk_before(c)
                if before is not None:
                    kind = CHUNKS[before]
                    if kind in ("ff", "fwd"):
                        sp.wait_ge(spec_mm, n_of_kind(before, "ff", "fwd"))
                    elif kind == "inv":
                        sp.wait_ge(inv_mm, n_of_kind(before, "inv"))
                    elif kind == "mod":
                        sp.wait_ge(mod_used, n_of_kind(before, "mod"))
                    elif kind == "late":
                        sp.wait_ge(late_used, 2 * n_of_kind(before, "late"))
                    elif kind == "wo":
                        sp.wait_ge(wo_split, n_of_kind(before, "wo"))
                    else:
                        sp.wait_ge(split_lo, n_split(before))
                sp.dma_start(raw(c, *shape), src).then_inc(raw_in[chunk_slot(c)], 16)

            for dst, src in first:
                sp.dma_start(dst, src).then_inc(first_in, 16)
            n_of = dict.fromkeys(CHUNKS, 0)
            for c in range(N_EARLY):
                if c == 1:
                    sp.wait_ge(small_in, N_SMALL)
                if c == 3:
                    for dst, src in rest:
                        sp.dma_start(dst, src).then_inc(rest_in, 16)
                if c in (4, 6):
                    i = c // 2 - 2
                    sp.dma_start(xs[:, 4 * i:4 * i + 4], x_rows[:, 4 * i:4 * i + 4]).then_inc(x_in[i], 16)
                if c == 8:
                    sp.dma_start(xs[:, 8:10], ctx_rows).then_inc(x_in[2], 16)
                kind = CHUNKS[c]
                n = n_of[kind]
                n_of[kind] += 1
                if kind in ("mod", "late"):
                    g, kp = n // 4 + (0 if kind == "mod" else 2), n % 4
                    load(c, w_mod[:, 2 * kp:2 * kp + 2, GW * g:GW * g + GW], (2, GW))
                elif kind == "hy":
                    load(c, w_in[:, :, 256 * n:256 * n + 256], (8, 256))
                elif kind in ("ff", "fwd"):
                    load(c, cst["fwd"][n].rearrange("p a b k -> p (a b) k"), (16, P))
                elif kind == "inv":
                    load(c, cst["inv"][n], (2, S))
                else:
                    col, kh = QKV0 + 512 * (1, 2, 0)[n // 2], 4 * (n % 2)
                    load(c, w_in[:, kh:kh + 4, col:col + 512], (4, 512))
                if kind == "hy" and n == 2:
                    sp.wait_ge(hT_mm, 20)
                    for tab in (gc, gk):
                        sp.dma_start(tab, cst["rope"]).then_inc(gn_in, 16)
            sp.wait_ge(skew_out, 16)
            sp.wait_ge(split_lo, n_split(chunk_index("qkv", 5) - 1))
            for h in range(HN):
                if h >= 2:
                    sp.wait_ge(bias_rdy, 5 * (h - 1))
                for a in range(2):
                    src = bass.AP(tensor=skew, offset=(h * 19 + 1 - a) * 64 * P + 63,
                                  ap=[[P - 1, 64], [64 * P, 18], [1, GRID_W]])
                    sp.dma_start(J[64 * a:64 * a + 64, h % 2], src).then_inc(J_in[h % 2], 16)
                if h == 1:
                    for n in range(2):
                        load(chunk_index("wo", n), w_out[:, 0:4, 512 * n:512 * n + 512], (4, 512))
            for n in range(2, 4):
                load(chunk_index("wo", n), w_out[:, 4:8, 512 * (n % 2):512 * (n % 2) + 512], (4, 512))
            sp.wait_ge(bias_add, NNA)
            for i in range(4):
                sp.dma_start(x1[:, 2 * i:2 * i + 2], x_rows[:, 2 * i:2 * i + 2]).then_inc(x1_in, 16)
            c0 = chunk_index("fi", 0)

            def load_fi(j, b):
                for g in range(2):
                    sp.dma_start(f32(RAW(b), KD, 2, P)[:, :, g], w_fi[:, :, bass.ds(j * P + g * FH, P)])\
                        .then_inc(raw_in[b], 16)

            for b in range(2):
                sp.wait_ge(wo_split, 3 + b)
                load_fi(b, b)
            with sp.Fori(0, KF // 2 - 1) as it:
                for b in range(2):
                    sp.wait_ge(split_lo, it * 2 + n_split(c0 + b))
                    load_fi(it * 2 + 2 + b, b)
            c1 = chunk_index("fo", 0)
            for grp in range(2):
                with sp.Fori(0, 5) as it:
                    for b in range(2):
                        s = (grp + b) % 2
                        sp.wait_ge(split_lo, it * 2 + n_split(c1 + grp * 11 + b - 2))
                        sp.dma_start(f32(RAW(s), 2, D), w_fo[:, bass.ds(it * 4 + 2 * b, 2), :]).then_inc(raw_in[s], 16)
                sp.wait_ge(split_lo, n_split(c1 + grp * 11 + 8))
                sp.dma_start(f32(RAW(grp), 2, D), w_fo[:, 20:22, :]).then_inc(raw_in[grp], 16)
            for t in range(NT):
                sp.wait_ge(fo_y, t + 1)
                sp.dma_start(out_rows[:, t], x1[:, t]).then_inc(out_done, 16)
            sp.wait_ge(out_done, 16 * NT)

        @block.gpsimd
        def _(pool):
            own = Chain(pool, pool_own)
            own.step(pool.memset(neghalf, -0.5))
            own.step(pool.memset(ones1, 1.0))
            own.wait()
            for i, (a, b) in enumerate(((0, 4), (4, 8), (8, 10))):
                pool.wait_ge(ms_rdy, i + 1)
                pool.tensor_tensor(rs[:, a:b], ss[:, a:b], neghalf[:, a:b], ALU.pow).then_inc(rs_rdy, 1)
            pool.wait_ge(hT_mm, 20)
            pool.memset(skrow[0:HN * 19], NEG).then_inc(skew_set, 1)
            for u, (g, t) in enumerate(UNITS):
                if g == 2:
                    continue
                n, w = n_normed(u), HQ if g == 0 else HKV
                pool.wait_ge(pr_ms, n)
                pool.tensor_tensor(rsq[:, u % 2, 0:w], ssq[:, u % 2, 0:w], neghalf[:, 0:w], ALU.pow)\
                    .then_inc(pr_rs, 1)
            for h in range(HN):
                pool.wait_ge(J_in[h % 2], 32 * (h // 2 + 1))
                own.step(pool.tensor_tensor(J[:, h % 2], J[:, h % 2],
                                            cmask.unsqueeze(1).broadcast_to((P, 18, GRID_W)), ALU.add))
                own.wait()
                if h < 2:
                    pool.wait_ge(pr_mm, (GROUP0[0], NU)[h])
                else:
                    pool.wait_ge(bias_add, NT * (h - 1))
                for kind in range(5):
                    o = bias_shift(kind)
                    last = pool.tensor_tensor(bias[:, h % 2, kind], J[:, h % 2, o:o + 10],
                                              rmask[:, kind, :].unsqueeze(2).broadcast_to((P, 10, GRID_W)), ALU.add)
                    last.then_inc(bias_rdy, 1)
            for n in range(4):
                c = chunk_index("wo", n)
                arrived(pool, c)
                if n == 0:
                    pool.wait_ge(s_mm, NNA)
                r, (k0, hy) = raw(c, 4, 512), (4 * (n // 2), 2 if n < 2 else 0)
                if hy:
                    own.step(pool.tensor_scalar(r[:, 0:2], r[:, 0:2], WS / HS, None, ALU.mult))
                own.step(pool.tensor_scalar(r[:, hy:4], r[:, hy:4], WS, None, ALU.mult))
                own.wait()
                own.step(pool.tensor_copy(woS[n][:, 0], r))
                own.wait()
                pool.tensor_tensor(woS[n][:, 1], r, woS[n][:, 0], ALU.subtract).then_inc(wo_split, 1)
            for half in range(2):
                pool.wait_ge(ms1, half + 1)
                pool.tensor_tensor(rs[:, 4 * half:4 * half + 4], ss[:, 4 * half:4 * half + 4],
                                   neghalf[:, 0:4], ALU.pow).then_inc(rs1, 1)
            for t in range(NT):
                pool.wait_ge(fo_ms, t + 1)
                pool.tensor_tensor(rs[:, t:t + 1], ss[:, t:t + 1], neghalf[:, 0:1], ALU.pow).then_inc(fo_rs, 1)

        @block.tensor
        def _(pe):
            def mm(out, lhsT, rhs, start, stop):
                return pe.matmul(out, lhsT, rhs, start=start, stop=stop, skip_group_check=True)

            pe.wait_ge(first_in, N_FIRST)
            pe.transpose(PS[:, 5, 0:N_ROWS], rows[0:N_ROWS], ident[0:N_ROWS, 0:N_ROWS]).then_inc(cols_mm, 1)

            def filter_layer(layer):
                if layer:
                    pe.wait_ge(mlp_h, layer)
                k = FW if layer else EMB
                for o in (0, FW):
                    ins = mm(PS[o:o + FW, 4, :], fw[o:o + k, layer, 0:FW], (fh if layer else zt)[o:o + k], True, True)
                ins.then_inc(mlp_mm, 1)

            def taps(nt):
                if nt >= 2:
                    pe.wait_ge(taps_rdy, nt - 1)
                o, t = FW * (nt // 4), nt % 4
                mm(PS[:, 6 + nt % 2, :], fh[o:o + FW, t * P:t * P + P], fwo[o:o + FW], True, True).then_inc(taps_mm, 1)

            def modulation(c):
                w = raw(c, 2, GW)
                arrived(pe, c)
                for i in range(2):
                    k = 2 * (c % 4) + i
                    for half in range(2):
                        ins = mm(PS[0:2, 2 * (c // 4) + half, :], silu_c[:, k], w[:, i, half * 512:half * 512 + 512],
                                 k == 0, k == KD - 1)
                ins.then_inc(mod_used, 1)

            pe.wait_ge(small_in, N_SMALL)
            filter_layer(0)
            pe.wait_ge(silu_rdy, 1)
            modulation(0)
            modulation(1)
            filter_layer(1)
            modulation(2)
            modulation(3)
            filter_layer(2)
            modulation(4)
            for nt in range(NT):
                if nt == 0:
                    pe.wait_ge(mlp_h, 3)
                taps(nt)
                if nt in (3, 5, 7):
                    modulation(4 + nt // 2)
            for g in range(2):
                pe.wait_ge(mrow_rdy, g + 1)
                for i in range(8):
                    o = 16 * g + 2 * i
                    ins = pe.transpose(PS[:, 5, o:o + 2], mrow[0:2, g, i * P:i * P + P], ident[0:2, 0:2])
            ins.then_inc(mcol_mm, 1)

            def spectrum(c, bank, cos_of, sin_of, part):
                w = raw(c, NT, 2, P)
                trig, odd = part // 2, part % 2
                if part == 0:
                    arrived(pe, c)
                for i in range(4):
                    nt = 4 * odd + i
                    ins = mm(PS[:, bank + trig, 256 * odd:256 * odd + 256], w[:, nt, trig],
                             (sin_of if trig else cos_of)[:, nt], i == 0, i == 3)
                if part == 3:
                    ins.then_inc(spec_mm, 1)

            def turn_x(src, tiles, bank, f):
                for i, t in enumerate(tiles):
                    ins = pe.transpose(PS[:, bank, i * P:i * P + P], src[:, t, f * P:f * P + P], ident)
                ins.then_inc(hT_mm, 1)

            pe.wait_ge(mod_rdy, 1)
            pe.wait_ge(taps_rdy, NT)
            for step in range(16):
                for n in (2 * step, 2 * step + 1):
                    if n >= 20:
                        continue
                    if n % 8 == 0:
                        pe.wait_ge(xn_rdy, (4, 8, 10)[n // 8])
                    if n >= 4:
                        pe.wait_ge(hT_f, n - 3)
                    if n < 16:
                        turn_x(xs, range(4 * (n // KD), 4 * (n // KD) + 4), n % 4, n % KD)
                    else:
                        for i in range(4):
                            f, t = 2 * (n - 16) + i // 2, NT + i % 2
                            ins = pe.transpose(PS[:, n % 4, i * P:i * P + P], xs[:, t, f * P:f * P + P], ident)
                        ins.then_inc(hT_mm, 1)
                kt = step // 4
                if kt >= 2 and step % 4 == 0:
                    pe.wait_ge(spec_rdy, kt - 1)
                spectrum(chunk_index("ff", kt), 4 + 2 * (kt % 2), filt_a, filt_b, step % 4)

            def late_columns(g, bank):
                pe.wait_ge(late_used, 8 * g + 8)
                for i in range(8):
                    ins = mm(PS[:, bank, 8 * (g % 2) + i:8 * (g % 2) + i + 1], macc[:, g % 2, i * P:i * P + P], ones1,
                             True, True)
                ins.then_inc(late_mm, 1)

            pe.wait_ge(hT_rdy, 16)
            for i in range(3):
                slot = i % 2
                w = spl(slot, KD, 256)
                pe.wait_ge(split_lo, i + 1)
                for b in range(2):
                    ct = 2 * i + b
                    if ct >= 2:
                        pe.wait_ge(hy_rdy, ct - 1)
                    else:
                        pe.wait_ge(hT_f, 18 + 2 * ct)
                    for k in range(KD):
                        for part, others in ((0, (0, 1)), (1, (0,))):
                            for o in others:
                                for half in range(2):
                                    ins = mm(PS[:, 2 * b + half, :], w[:, part, k, b * P:b * P + P],
                                             hT[:, o, k, half * 512:half * 512 + 512],
                                             k == 0 and part + o == 0, k == KD - 1 and part == 1)
                    ins.then_inc(hy_mm, 1)
                if i:
                    if i == 1:
                        pe.wait_ge(spec_rdy, 4)
                    late_columns(i - 1, 6)

            pe.wait_ge(hy_rdy, 4)
            for q in range(4):
                if q >= 2:
                    pe.wait_ge(vt_rdy, q - 1)
                for i in range(2):
                    nt = 2 * q + i
                    o = nt * 256 if nt < 4 else (nt - 4) * 256 + 1
                    for c2 in range(2):
                        ins = pe.transpose(PS[:, 4 + q % 2, 256 * i + P * c2:256 * i + P * c2 + P],
                                           uvT[:, c2, o:o + 255:2], ident)
                ins.then_inc(vt_mm, 1)
            pe.wait_ge(vt_rdy, 4)
            pe.wait_ge(hy_rdy, 6)
            pe.wait_ge(late_rdy, 1)

            def inverse(c, kt):
                w = raw(c, 2, S)
                arrived(pe, c)
                pe.wait_ge(G_rdy, kt + 1)
                for trig in range(2):
                    for odd in range(2):
                        for c2 in range(2):
                            ins = mm(PS[:, 4 + 2 * c2 + odd, :], G[:, kt % 2, 2 * odd + trig, c2 * P:c2 * P + P],
                                     w[:, trig, 512 * odd:512 * odd + 512], kt == 0 and trig == 0,
                                     kt == 3 and trig == 1)
                ins.then_inc(inv_mm, 1)

            for kt in range(5):
                if kt < 4:
                    if kt >= 2:
                        pe.wait_ge(spec_rdy, 4 + kt - 1)
                    for part in range(4):
                        spectrum(chunk_index("fwd", kt), 2 * (kt % 2), vtok, vtok, part)
                else:
                    pe.wait_ge(spec_rdy, 8)
                    late_columns(2, 3)
                    late_columns(3, 3)
                if kt:
                    inverse(chunk_index("inv", kt - 1), kt - 1)

            def project(u, par, g, t, is_ctx, it=None):
                more = 0 if it is None else it * 2
                if u >= 2:
                    if UNITS[u - 2][0] != 0:
                        pe.wait_ge(pr_v, more + u - 1)
                    if UNITS[u - 2][0] != 2:
                        pe.wait_ge(pr_n, more + n_normed(u - 2))
                pair = 2 if g != 2 else 0
                width = 256 if (is_ctx and g == 1) else 512
                for k in range(KD):
                    w = spl(pair + k // 4, 4, 512)
                    src = hcT if is_ctx else hT
                    for part, others in ((0, (0, 1)), (1, (0,))):
                        for o in others:
                            ins = mm(PS[:, par, 0:width], src[:, part, k, tok(t)], w[:, o, k % 4, 0:width],
                                     k == 0 and part + o == 0, k == KD - 1 and part == 1)
                ins.then_inc(pr_mm, 1)

            def turn_qk(u, par, n, it=None):
                more = 0 if it is None else it * 2
                pe.wait_ge(pr_lo, more + u + 1)
                if u >= 2:
                    pe.wait_ge(pr_tc, more + u - 1)
                out16 = PS[:, 2 + par, :].bitcast(F16)
                for j in range(n):
                    ins = pe.transpose(out16[:, j * P:j * P + P], stk[par][:, j * P:j * P + P], ident16)
                ins.then_inc(pr_tm, 1)

            for gi, g in enumerate((1, 2, 0)):
                u0 = GROUP0[g]
                pe.wait_ge(split_lo, 3 + 2 * gi + 2)
                for b in range(2):
                    project(u0 + b, b, g, b, False)
                    if gi:
                        turn_qk(u0 + b - 2, b, 4 if g == 2 else 8)
                with pe.Fori(0, 3) as it:
                    for b in range(2):
                        project(u0 + 2 + b, b, g, it * 2 + 2 + b, False, it)
                        turn_qk(u0 + b, b, 8, it)
                if g:
                    for b in range(2):
                        project(u0 + 8 + b, b, g, b, True)
                        turn_qk(u0 + 6 + b, b, 8)
            for b in range(2):
                turn_qk(NU - 2 + b, b, 8)

            def copied(u, bank):
                if bank < 2:
                    pe.wait_ge(pt_a, 2 * u.n + bank + 1)
                elif not u.na:
                    pe.wait_ge(pt_d, u.n_gqa + 1)

            def scores(u):
                if u.na:
                    q, k = nqT[:, u.blk, u.j * P:u.j * P + P], nkT[:, u.blk]
                    k0 = window(u.j) * P
                    pieces = ((0, 512, k0), (512, 128, k0 + 512), (640, 256, S))
                else:
                    q, k = qT[:, u.j, tok(u.blk)], kT[:, u.kv]
                    pieces = ((0, 512, 0), (512, 512, 512), (1024, 256, 1024))
                for o, w, s0 in pieces:
                    if u.v >= 2 and o % 512 == 0:
                        copied(u.ahead(-2), o // 512)
                    for part in range(2):
                        ins = mm(PSf[:, 1536 * u.par + o:1536 * u.par + o + w], q, k[:, part, s0:s0 + w],
                                 part == 0, part == 1)
                ins.then_inc(s_mm, 1)

            def turn_p(u):
                pe.wait_ge(s_exp, u.n + 1)
                for bank in u.banks:
                    for i in bank:
                        o = 1536 * u.par + i * P
                        ins = pe.transpose(PSf[:, o:o + P], Pb[:, u.par, i], ident)
                    ins.then_inc(pt_mm, 1)

            def weigh(u):
                if u.v >= 2:
                    pe.wait_ge(o_rdy, u.n - 1)
                tiles = [window(u.j) + i for i in range(5)] + [NT, NT + 1] if u.na else range(10)
                for i, kt in enumerate(tiles):
                    if i % 4 == 0:
                        copied(u, i // 4)
                    ins = mm(PS[:, 6 + u.par, 0:HD], PT[:, u.par, i], V[:, kt, HKV + u.blk if u.na else u.kv],
                             i == 0, i == len(tiles) - 1)
                ins.then_inc(o_mm, 1)

            def attend(u):
                if u.v < NV - 1:
                    scores(u.ahead(1))
                turn_p(u)
                if u.v:
                    weigh(u.ahead(-1))

            pe.wait_ge(pr_tc, NU)
            scores(Unit(0))
            for v in range(3):
                attend(Unit(v))
            with pe.Fori(0, HN - 1) as it:
                for v in range(3, 11):
                    attend(Unit(v, it))
            for v in range(27, 33):
                attend(Unit(v))
            with pe.Fori(0, NT - 1) as it:
                for v in range(33, 41):
                    attend(Unit(v, it))
            for v in range(89, NV):
                attend(Unit(v))
            weigh(Unit(NV - 1))

            for n in range(2):
                pe.wait_ge(gate_d, n + 1)
                for i in range(2):
                    ins = mm(PS[:, 2 * n + i, :], ones, diag[:, 4 * i:4 * i + 4].rearrange("p a b -> p (a b)"),
                             True, True)
                ins.then_inc(gate_mm, 1)
            pe.wait_ge(o_rdy, NV)
            for t in range(NT):
                if t >= 2:
                    pe.wait_ge(mx_lo, t - 1)
                for f in range(6):
                    ins = pe.transpose(PS[:, 4 + 2 * (t % 2) + f // 4, (f % 4) * P:(f % 4) * P + P],
                                       mixtok[:, t, f * P:f * P + P], ident)
                ins.then_inc(mx_mm, 1)

            def project_out(t, b):
                for k in range(KD):
                    for part, others in ((0, (0, 1)), (1, (0,))):
                        lhs = yT[:, part, k, tok(t)] if k < 2 else mixT[:, part, k - 2, tok(t)]
                        for o in others:
                            for half in range(2):
                                ins = mm(PS[:, 2 * b + half, :], lhs, woS[2 * (k // 4) + half][:, o, k % 4, :],
                                         k == 0 and part + o == 0, k == KD - 1 and part == 1)
                ins.then_inc(wo_mm, 1)

            pe.wait_ge(mx_lo, NT)
            pe.wait_ge(gate_rdy, 2)
            pe.wait_ge(wo_split, 4)
            pe.wait_ge(y_rdy, 4)
            for b in range(2):
                project_out(b, b)
            with pe.Fori(0, 3) as it:
                for b in range(2):
                    pe.wait_ge(x1_rdy, it * 2 + b + 1)
                    project_out(it * 2 + 2 + b, b)
            for half in range(2):
                pe.wait_ge(xn1_rdy, half + 1)
                for f in range(KD):
                    n = 8 * half + f
                    if n >= 4:
                        pe.wait_ge(hT_f, 20 + n - 3)
                    turn_x(xn1, range(4), 4 + n % 4, f)

            def hidden(b):
                w = fiS[b]
                for gu in range(2):
                    for k in range(KD):
                        for part, others in ((0, (0, 1)), (1, (0,))):
                            for o in others:
                                for half in range(2):
                                    ins = mm(PS[:, 4 * b + 2 * gu + half, :], w[:, part, k, gu * P:gu * P + P],
                                             hT[:, o, k, half * 512:half * 512 + 512],
                                             k == 0 and part + o == 0, k == KD - 1 and part == 1)
                ins.then_inc(fi_mm, 1)

            pe.wait_ge(hT_rdy, 20 + 16)
            base = n_split(chunk_index("fi", 0))
            for b in range(2):
                pe.wait_ge(split_lo, base + b)
                hidden(b)
            with pe.Fori(0, KF // 2 - 1) as it:
                for b in range(2):
                    pe.wait_ge(split_lo, it * 2 + base + 2 + b)
                    pe.wait_ge(fi_p, it * 2 + b + 1)
                    hidden(b)

            def down(k0, s, grp, start, stop):
                for t in range(4):
                    if start and grp:
                        pe.wait_ge(fo_r, t + 1)
                    for kk in range(2):
                        for part, others in ((0, (0, 1)), (1, (0,))):
                            for o in others:
                                for half in range(2):
                                    ins = mm(PS[:, 2 * t + half, :], prodT[:, part, k0 + kk, tok(4 * grp + t)],
                                             foS[s][:, o, kk, half * 512:half * 512 + 512],
                                             start and kk == 0 and part + o == 0, stop and kk == 1 and part == 1)
                    if stop:
                        ins.then_inc(fo_mm, 1)
                if not stop:
                    ins.then_inc(fo_used, 1)

            pe.wait_ge(fi_lo, KF)
            base = n_split(chunk_index("fo", 0))
            for grp in range(2):
                n0 = base + 11 * grp
                pe.wait_ge(split_lo, n0)
                down(0, grp % 2, grp, True, False)
                with pe.Fori(0, 4) as it:
                    for b in range(2):
                        pe.wait_ge(split_lo, it * 2 + n0 + 1 + b)
                        down(it * 4 + 2 + 2 * b, (grp + 1 + b) % 2, grp, False, False)
                for b in range(2):
                    pe.wait_ge(split_lo, n0 + 9 + b)
                    down(18 + 2 * b, (grp + 1 + b) % 2, grp, False, b == 1)

        @block.scalar
        def _(act):
            for dst, src in small:
                act.dma_start(dst, src).then_inc(small_in, 16)

            def hi_of(c, dst):
                arrived(act, c)
                n = int(np.prod(dst.shape[2:]))
                src = f32(RAW(chunk_slot(c)), n)
                act.activation(flat(dst[:, 0]), src, ACT.Copy, scale=WS).then_inc(split_hi, 1)

            act.wait_ge(cols_rdy, 1)
            act.activation(silu_c.rearrange("p k n -> p n k"),
                           cols[:, V_C:V_C + 16].rearrange("p (n k) -> p n k", n=2), ACT.Silu).then_inc(silu_rdy, 1)
            for layer in range(3):
                act.wait_ge(mlp_arg, layer + 1)
                act.activation(fh, fu, ACT.Sin).then_inc(mlp_h, 1)
            for t in range(10):
                if t == 8:
                    act.wait_ge(mod_used, 4)
                    act.copy(mrow[0:2, 0], PSf[0:2, 0:GW]).then_inc(mrow_rdy, 1)
                act.wait_ge(x_in[t // 4], 16)
                act.activation(f32(68 + 4 * t, D), xs[:, t], ACT.Square, accum_out=ss[:, t:t + 1]).then_inc(sq_done, 1)
            act.wait_ge(mod_used, 8)
            act.copy(mrow[0:2, 1], PSf[0:2, GW:2 * GW]).then_inc(mrow_rdy, 1)

            def even_filter(kt):
                act.wait_ge(spec_mm, kt + 1)
                if kt >= 2:
                    act.wait_ge(spec_rdy, kt - 1)
                b = 4 + 2 * (kt % 2)
                act.activation(tE0[:, kt % 2], PS[:, b:b + 2, 0:256], ACT.Copy, scale=1.0 / 1024).then_inc(even_part, 1)

            act.wait_ge(mod_rdy, 1)
            for n in range(20):
                act.wait_ge(hT_mm, n + 1)
                if n >= 2:
                    act.wait_ge(hT_rdy, n - 1)
                if n < 16:
                    f = n % KD
                    act.activation(htmp[:, n % 2], PS[:, n % 4], ACT.Identity, scale=am[:, f, 0:1],
                                   bias=mod[:, f, 0:1]).then_inc(hT_f, 1)
                else:
                    for i in range(2):
                        f = 2 * (n - 16) + i
                        ins = act.activation(htmp[:, n % 2, 256 * i:256 * i + 256], PS[:, n % 4, 256 * i:256 * i + 256],
                                             ACT.Identity, scale=am[:, f, 1:2], bias=mod[:, f, 1:2])
                    ins.then_inc(hT_f, 1)
                if n % 8 == 7:
                    even_filter(n // 8)
                if n == 15:
                    hi_of(chunk_index("hy", 0), spl(0, KD, 256))
            even_filter(2)
            even_filter(3)
            hi_of(chunk_index("hy", 1), spl(1, KD, 256))
            for ct in range(6):
                act.wait_ge(hy_mm, ct + 1)
                if ct == 2:
                    act.wait_ge(hT_rdy, 20)
                dst = (uvT, accx, x2T)[ct // 2][:, ct % 2]
                act.activation(dst, PSf[:, 1024 * (ct % 2):1024 * (ct % 2) + 1024], ACT.Identity,
                               scale=cwb[:, 6 + ct:7 + ct], bias=cols[:, V_CB + ct:V_CB + ct + 1]).then_inc(hy_mid, 1)
                if ct == 1:
                    hi_of(chunk_index("hy", 2), spl(0, KD, 256))
            for q in range(4):
                act.wait_ge(vt_mm, q + 1)
                act.copy(flat(vtok[:, 2 * q:2 * q + 2]), PS[:, 4 + q % 2]).then_inc(vt_rdy, 1)
            for kt in range(4):
                act.wait_ge(spec_mm, 4 + kt + 1)
                if kt >= 2:
                    act.wait_ge(spec_rdy, 4 + kt - 1)
                act.copy(tE[:, kt % 2], PS[:, 2 * (kt % 2):2 * (kt % 2) + 2, 0:256]).then_inc(even_part, 1)
            for i in range(2):
                hi_of(chunk_index("qkv", i), spl(2 + i, 4, 512))
            for n in range(4):
                c2, odd = n // 2, n % 2
                act.wait_ge(y_f, n + 1)
                act.copy(yT[:, 0, c2, odd::2], yo[:, n % 2]).then_inc(y_hi, 1)
            for i in range(2, 4):
                hi_of(chunk_index("qkv", i), spl(i - 2, 4, 512))

            def from_psum(u, it=0):
                (g, t), par, m = UNITS[u], u % 2, it * 2
                act.wait_ge(pr_mm, m + u + 1)
                if u >= 2:
                    act.wait_ge(pr_lo, m + u - 1)
                    if UNITS[u - 2][0] != 2:
                        act.wait_ge(pr_r, m + n_normed(u - 2))
                ps, tt = PS[:, par], t + m
                if g == 0:
                    act.activation(bT[par], ps, ACT.Square).then_inc(pr_sq, 1)
                elif g == 1:
                    act.activation(bT[par][:, 0:128], ps[:, 0:128], ACT.Square).then_inc(pr_sq, 1)
                    if t < NT:
                        act.activation(nT[par][:, 128:384], ps[:, 256:512], ACT.Copy, scale=0.125 / WS)
                    act.activation(V[:, tt, 0:2], ps[:, 128:256].rearrange("p (h d) -> p h d", h=2), ACT.Copy,
                                   scale=1 / WS).then_inc(pr_v, 1)
                else:
                    act.activation(nT[par][:, 0:256], ps[:, 0:256], ACT.Copy, scale=1 / WS)
                    act.activation(V[:, tt, 2:6], ps[:, 256:512].rearrange("p (h d) -> p h d", h=4), ACT.Copy,
                                   scale=1 / WS).then_inc(pr_v, 1)

            def hi_parts(u, it=0):
                (g, t), par, m = UNITS[u], u % 2, it * 2
                if g != 2:
                    act.wait_ge(pr_r, m + n_normed(u))
                if g != 0:
                    act.wait_ge(pr_v, m + u + 1)
                if u >= 2:
                    act.wait_ge(pr_tm, m + u - 1)
                for out, _, src in stacks(g, t, par):
                    ins = act.copy(out, src)
                ins.then_inc(pr_hi, 1)

            def turned(u, it=0):
                (g, t), par, m = UNITS[u], u % 2, it * 2
                act.wait_ge(pr_tm, m + u + 1)
                ps = PS[:, 2 + par, :].bitcast(F16).rearrange("p (j t) -> p j t", t=P)
                if g == 0:
                    ins = act.copy(qT[:, :, tok(t + m)], ps)
                elif g == 2:
                    ins = act.copy(nkT.rearrange("p h a s -> p (h a) s")[:, :, tok(t + m)], ps)
                else:
                    ins = act.copy(kT.rearrange("p h a s -> p (h a) s")[:, :, tok(t + m)], ps[:, 0:4])
                    if t < NT:
                        ins = act.copy(nqT[:, :, tok(t + m)], ps[:, 4:8])
                ins.then_inc(pr_tc, 1)

            def slot(u, it=0):
                if u < NU:
                    from_psum(u, it)
                if 1 <= u <= NU:
                    hi_parts(u - 1, it)
                if u >= 2:
                    turned(u - 2, it)

            for g in (1, 2, 0):
                u0 = GROUP0[g]
                slot(u0)
                if g == 2:
                    for i in range(4, 6):
                        hi_of(chunk_index("qkv", i), spl(i - 2, 4, 512))
                slot(u0 + 1)
                with act.Fori(0, 3) as it:
                    for b in range(2):
                        slot(u0 + 2 + b, it)
                if g:
                    slot(u0 + 8)
                    slot(u0 + 9)
                if g == 1:
                    act.wait_ge(skew_set, 1)
                    for h in range(HN):
                        act.dma_start(skrow[19 * h + 2:19 * h + 17, 48:79], io["na_rpb"][0, h])\
                            .then_inc(skew_rows, 16)
                    act.wait_ge(skew_rows, 16 * HN)
                    act.dma_start(skew.ap().rearrange("h r c x -> (h r) c x"),
                                  skrow[0:19 * HN].unsqueeze(1).broadcast_to((19 * HN, 64, P))).then_inc(skew_out, 16)
            slot(NU)
            slot(NU + 1)

            def exponentials(u):
                act.wait_ge(s_max, u.n + 1)
                w = 7 if u.na else 10
                act.activation(flat(Pb[:, u.par, 0:w]), PSf[:, 1536 * u.par:1536 * u.par + w * P], ACT.Exp,
                               bias=nmax[:, u.par:u.par + 1], accum_out=esum[:, u.v % 4:u.v % 4 + 1]).then_inc(s_exp, 1)

            def copy_p(u):
                if u.v >= 2:
                    act.wait_ge(o_mm, u.n - 1)
                for b in range(2):
                    act.wait_ge(pt_mm, u.turned(b))
                    t = u.banks[b]
                    o = 1536 * u.par
                    act.copy(flat(PT[:, u.par, t.start:t.stop]), PSf[:, o + t.start * P:o + t.stop * P])\
                        .then_inc(pt_a, 1)

            def attend(u):
                copy_p(u)
                if u.v < NV - 1:
                    exponentials(u.ahead(1))

            act.wait_ge(pr_mm, NU)
            exponentials(Unit(0))
            for v in range(3):
                attend(Unit(v))
            with act.Fori(0, HN - 1) as it:
                for v in range(3, 11):
                    attend(Unit(v, it))
            for v in range(27, 33):
                attend(Unit(v))
            with act.Fori(0, NT - 1) as it:
                for v in range(33, 41):
                    attend(Unit(v, it))
            for v in range(89, NV):
                attend(Unit(v))

            for n in range(2):
                act.wait_ge(gate_mm, n + 1)
                act.copy((gate1, gate2)[n], PSf[:, 1024 * n:1024 * n + 1024]).then_inc(gate_rdy, 1)
            for t in range(NT):
                act.wait_ge(mx_mm, t + 1)
                o = 2048 + 1024 * (t % 2)
                act.copy(mixT[:, 0, :, t * P:t * P + P], PSf[:, o:o + 768].rearrange("p (f t) -> p f t", f=6))\
                    .then_inc(mx_hi, 1)
            act.wait_ge(bias_add, NNA)
            for b in range(2):
                hi_of(chunk_index("fi", b), fiS[b])
            for t in range(NT):
                act.wait_ge(x1_sum, t + 1)
                if t:
                    act.wait_ge(sq1, t)
                act.activation(f32(104, D), x1[:, t], ACT.Square, accum_out=ss[:, t:t + 1]).then_inc(sq1, 1)
            for n in range(16):
                act.wait_ge(hT_mm, 20 + n + 1)
                if n >= 2:
                    act.wait_ge(hT_rdy, 20 + n - 1)
                f = n % KD
                act.activation(h2tmp[:, n % 2], PS[:, 4 + n % 4], ACT.Identity, scale=af[:, f, 0:1],
                               bias=mod[:, 24 + f, 0:1]).then_inc(hT_f, 1)

            def silu(b, j, first=False):
                act.wait_ge(fi_mm, j + 1)
                if not first:
                    act.wait_ge(fi_p, j)
                act.activation(sg, PSf[:, 2048 * b:2048 * b + 1024], ACT.Silu, scale=1 / WS).then_inc(fi_s, 1)

            def gated_hi(j):
                act.wait_ge(fi_p, j + 1)
                act.copy(prodT[:, 0, j, :], pr).then_inc(fi_hi, 1)

            act.wait_ge(hT_rdy, 36)
            c0 = chunk_index("fi", 0)
            for b in range(2):
                silu(b, b, b == 0)
                hi_of(c0 + 2 + b, fiS[b])
                gated_hi(b)
            with act.Fori(0, KF // 2 - 2) as it:
                for b in range(2):
                    silu(b, it * 2 + 2 + b)
                    act.wait_ge(raw_in[b], it * 32 + 16 * chunk_arrivals(c0 + 4 + b))
                    act.activation(flat(fiS[b][:, 0]), f32(RAW(b), 2048), ACT.Copy, scale=WS).then_inc(split_hi, 1)
                    gated_hi(it * 2 + 2 + b)
            for b in range(2):
                silu(b, KF - 2 + b)
                hi_of(chunk_index("fo", b), foS[b])
                gated_hi(KF - 2 + b)
            act.wait_ge(fi_mm, KF)
            act.dma_start(gfin, io["g_final"].partition_broadcast(P)).then_inc(gf_in, 16)

            c1 = chunk_index("fo", 0)

            def fo_hi(s, base_c, it=0):
                act.wait_ge(raw_in[s], it * 16 + 16 * chunk_arrivals(base_c))
                act.activation(flat(foS[s][:, 0]), f32(RAW(s), 2048), ACT.Copy, scale=WS).then_inc(split_hi, 1)

            def x2_square(t):
                act.wait_ge(fo_x, t + 1)
                if t:
                    act.wait_ge(fo_sq, t)
                act.activation(osq, x1[:, t], ACT.Square, accum_out=ss[:, t:t + 1]).then_inc(fo_sq, 1)

            with act.Fori(0, 4) as it:
                for b in range(2):
                    act.wait_ge(fo_used, it * 2 + b + 1)
                    fo_hi(b, c1 + 2 + b, it)
            for m in (10, 11):
                act.wait_ge(fo_used, m - 1)
                fo_hi(m % 2, c1 + m)
            act.wait_ge(fo_mm, 4)
            fo_hi(0, c1 + 12)
            for t in range(4):
                x2_square(t)
            with act.Fori(0, 4) as it:
                for b in range(2):
                    act.wait_ge(fo_used, it * 2 + b + 11)
                    fo_hi(1 - b, c1 + 13 + b, it)
            act.wait_ge(fo_used, 19)
            fo_hi(1, c1 + 21)
            for t in range(4, NT):
                x2_square(t)

        @block.vector
        def _(dve):
            own = Chain(dve, dve_own)

            def lo_of(c, dst):
                n = int(np.prod(dst.shape[2:]))
                dve.wait_ge(split_hi, n_split(c))
                dve.scalar_tensor_tensor(flat(dst[:, 1]), f32(RAW(chunk_slot(c)), n), WS, flat(dst[:, 0]),
                                         ALU.mult, ALU.subtract).then_inc(split_lo, 1)

            dve.wait_ge(cols_mm, 1)
            dve.tensor_copy(cols[:, 0:N_ROWS], PS[:, 5, 0:N_ROWS]).then_inc(cols_rdy, 1)
            dve.tensor_copy(ident16, ident).then_inc(id16_rdy, 1)
            dve.wait_ge(cols_rdy, 1)
            own.step(dve.tensor_scalar(cwb, cols[:, V_CW:V_CW + 18], 1 / WS, None, ALU.mult))
            u, k = fu, fk
            for layer in range(3):
                dve.wait_ge(mlp_mm, layer + 1)
                own.step(dve.tensor_scalar(u, PS[:, 4], fvec[:, layer:layer + 1], fvec[:, 3:4],
                                           ALU.add, ALU.mult))
                own.wait()
                own.step(dve.tensor_scalar(k, u, 1 / (2 * math.pi), MAGIC, ALU.mult, ALU.add))
                own.wait()
                own.step(dve.tensor_scalar(k, k, MAGIC, None, ALU.subtract))
                own.wait()
                for part in (TWO_PI_1, TWO_PI_2, TWO_PI_3):
                    own.step(dve.scalar_tensor_tensor(u, k, -part, u, ALU.mult, ALU.add))
                    own.wait()
                dve.tensor_scalar(u, u, PI_IN, -PI_IN, ALU.min, ALU.max).then_inc(mlp_arg, 1)
            dve.wait_ge(rest_in, N_REST)
            own.step(dve.tensor_scalar(gkc, gq[:, 1], 1 / WS, None, ALU.mult))
            for nt in range(NT):
                dve.wait_ge(taps_mm, nt + 1)
                own.step(dve.tensor_tensor(flat(fbd[:, nt % 2]), PS[:, 6 + nt % 2], decay[:, nt], ALU.mult))
                own.wait()
                own.step(dve.tensor_tensor(filt_a[:, nt], fbd[:, nt % 2, 0], fbd[:, nt % 2, 1], ALU.add))
                dve.tensor_tensor(filt_b[:, nt], fbd[:, nt % 2, 0], fbd[:, nt % 2, 1], ALU.subtract)\
                    .then_inc(taps_rdy, 1)
            for i, (ta, tb) in enumerate(((0, 4), (4, 8), (8, 10))):
                dve.wait_ge(sq_done, tb)
                dve.tensor_scalar(ss[:, ta:tb], ss[:, ta:tb], 1.0 / D, EPS, ALU.mult, ALU.add).then_inc(ms_rdy, 1)
                dve.wait_ge(rs_rdy, i + 1)
                for t in range(ta, tb):
                    dve.tensor_scalar(xs[:, t], xs[:, t], rs[:, t:t + 1], None, ALU.mult).then_inc(xn_rdy, 1)

            def filter_spectrum(kt):
                par = kt % 2
                dve.wait_ge(even_part, kt + 1)
                oc, os = PS[:, 4 + 2 * par, 256:512], PS[:, 5 + 2 * par, 256:512]
                ec, es = tE0[:, par, 0], tE0[:, par, 1]
                a = 1.0 / 1024
                dve.scalar_tensor_tensor(Fc[:, kt, 0:256], oc, a, ec, ALU.mult, ALU.add)
                dve.scalar_tensor_tensor(Fc[:, kt, 256:512], oc, -a, ec, ALU.mult, ALU.add)
                dve.scalar_tensor_tensor(Fs[:, kt, 0:256], os, a, es, ALU.mult, ALU.add)
                dve.scalar_tensor_tensor(Fs[:, kt, 256:512], os, a, es, ALU.mult, ALU.subtract).then_inc(spec_rdy, 1)

            def modulation_gain(a, scale0, gain0, n):
                dve.scalar_tensor_tensor(a[:, :, 0:n], mod[:, scale0:scale0 + 8, 0:n], 1.0,
                                         cols[:, gain0:gain0 + 8].unsqueeze(2).broadcast_to((P, 8, n)),
                                         ALU.add, ALU.mult).then_inc(mod_rdy, 1)

            dve.wait_ge(mcol_mm, 1)
            own.step(dve.tensor_tensor(mod[:, 0:16], PS[:, 5, 0:32].rearrange("p (t n) -> p t n", n=2),
                                       cols[:, V_BMOD:V_BMOD + 16].unsqueeze(2).broadcast_to((P, 16, 2)), ALU.add))
            own.wait()
            modulation_gain(am, 8, V_GMIX, 2)

            def split_h(n, f, hi, lo):
                dve.wait_ge(hT_f, n + 1)
                own.step(dve.tensor_copy(hi, f))
                own.wait()
                dve.tensor_tensor(lo, f, hi, ALU.subtract).then_inc(hT_rdy, 1)

            for n in range(20):
                if n < 16:
                    f, o = n % KD, 512 * (n // KD)
                    split_h(n, htmp[:, n % 2], hT[:, 0, f, o:o + 512], hT[:, 1, f, o:o + 512])
                else:
                    f = 2 * (n - 16)
                    split_h(n, htmp[:, n % 2].rearrange("p (f t) -> p f t", f=2), hcT[:, 0, f:f + 2], hcT[:, 1, f:f + 2])
                if n % 8 == 7:
                    filter_spectrum(n // 8)
                if n == 15:
                    lo_of(chunk_index("hy", 0), spl(0, KD, 256))
            filter_spectrum(2)
            filter_spectrum(3)
            lo_of(chunk_index("hy", 1), spl(1, KD, 256))

            def late(n):
                c = chunk_index("late", n)
                w, g, kp = raw(c, 2, GW), n // 4, n % 4
                acc = macc[:, g % 2]
                arrived(dve, c)
                if kp == 0 and g >= 2:
                    dve.wait_ge(late_mm, g - 1)
                for i in range(2):
                    s = silu_c[:, 2 * kp + i, 0:1]
                    if kp + i:
                        dve.wait_ge(late_used, 2 * n + i)
                        ins = dve.scalar_tensor_tensor(acc, w[:, i], s, acc, ALU.mult, ALU.add)
                    else:
                        ins = dve.tensor_scalar(acc, w[:, i], s, None, ALU.mult)
                    ins.then_inc(late_used, 1)

            for ct in range(6):
                dst = (uvT, accx, x2T)[ct // 2][:, ct % 2]
                ps = PSf[:, 1024 * (ct % 2):1024 * (ct % 2) + 1024]
                dve.wait_ge(hy_mid, ct + 1)
                own.step(dve.scalar_tensor_tensor(dst[:, 1:S], ps[:, 0:S - 1], cwb[:, ct:ct + 1], dst[:, 1:S],
                                                  ALU.mult, ALU.add))
                own.wait()
                ins = dve.scalar_tensor_tensor(dst[:, 0:S - 1], ps[:, 1:S], cwb[:, 12 + ct:13 + ct], dst[:, 0:S - 1],
                                               ALU.mult, ALU.add)
                if ct // 2 == 1:
                    own.step(ins)
                    own.wait()
                    ins = dve.tensor_tensor(uvT[:, ct % 2], uvT[:, ct % 2], dst, ALU.mult)
                ins.then_inc(hy_rdy, 1)
                if ct == 1:
                    lo_of(chunk_index("hy", 2), spl(0, KD, 256))
                late(2 * ct)
                late(2 * ct + 1)

            dve.wait_ge(late_mm, 2)
            dve.tensor_tensor(mod[:, 16:32, 0], PS[:, 6, 0:16], cols[:, V_BMOD + 16:V_BMOD + 32], ALU.add)                .then_inc(late_rdy, 1)
            for kt in range(4):
                par = kt % 2
                dve.wait_ge(even_part, 4 + kt + 1)
                oc, os = PS[:, 2 * par, 256:512], PS[:, 2 * par + 1, 256:512]
                ec, es = tE[:, par, 0], tE[:, par, 1]
                own.step(dve.tensor_tensor(V2c[:, 0:256], oc, ec, ALU.add))
                own.step(dve.tensor_tensor(V2c[:, 256:512], ec, oc, ALU.subtract))
                own.step(dve.tensor_tensor(V2s[:, 0:256], os, es, ALU.add))
                dve.tensor_tensor(V2s[:, 256:512], os, es, ALU.subtract).then_inc(spec_rdy, 1)
                dve.wait_ge(spec_rdy, 4 + kt + 1)
                own.step(dve.tensor_tensor(t1, V2c, Fc[:, kt], ALU.mult))
                own.step(dve.tensor_tensor(t2, V2s, Fs[:, kt], ALU.mult))
                own.step(dve.tensor_tensor(t3, V2c, Fs[:, kt], ALU.mult))
                own.step(dve.tensor_tensor(t4, V2s, Fc[:, kt], ALU.mult))
                own.wait()
                own.step(dve.tensor_tensor(Yc, t1, t2, ALU.subtract))
                own.step(dve.tensor_tensor(Ys, t3, t4, ALU.add))
                own.wait()
                if kt >= 2:
                    dve.wait_ge(inv_mm, kt - 1)
                dve.tensor_tensor(G[:, par, 0], Yc[:, 0:256], Yc[:, 256:512], ALU.add)
                dve.tensor_tensor(G[:, par, 1], Ys[:, 0:256], Ys[:, 256:512], ALU.subtract)
                dve.tensor_tensor(G[:, par, 2], Yc[:, 0:256], Yc[:, 256:512], ALU.subtract)
                dve.tensor_tensor(G[:, par, 3], Ys[:, 0:256], Ys[:, 256:512], ALU.add).then_inc(G_rdy, 1)
                late(12 + kt)
            for i in range(2):
                lo_of(chunk_index("qkv", i), spl(2 + i, 4, 512))
            dve.wait_ge(late_mm, 4)
            dve.tensor_tensor(mod[:, 32:48, 0], PS[:, 3, 0:16], cols[:, V_BMOD + 32:V_BMOD + 48], ALU.add)                .then_inc(late_rdy, 1)
            dve.wait_ge(late_rdy, 2)
            modulation_gain(af, 32, V_GFFN, 1)
            dve.wait_ge(inv_mm, 4)
            for n in range(4):
                c2, odd = n // 2, n % 2
                if n >= 2:
                    dve.wait_ge(y_rdy, n - 1)
                own.step(dve.scalar_tensor_tensor(yo[:, n % 2], uvT[:, c2, odd::2], cols[:, V_SKIP + c2:V_SKIP + c2 + 1],
                                                  PS[:, 4 + n], ALU.mult, ALU.add))
                own.wait()
                dve.scalar_tensor_tensor(yo[:, n % 2], yo[:, n % 2], HS, x2T[:, c2, odd::2], ALU.mult, ALU.mult)\
                    .then_inc(y_f, 1)
                dve.wait_ge(y_hi, n + 1)
                dve.tensor_tensor(yT[:, 1, c2, odd::2], yo[:, n % 2], yT[:, 0, c2, odd::2], ALU.subtract)\
                    .then_inc(y_rdy, 1)
            for i in range(2, 4):
                lo_of(chunk_index("qkv", i), spl(i - 2, 4, 512))
            dve.wait_ge(gn_in, 32)
            for n, tab in enumerate((gc, gk)):
                s = (0.125 / WS, 1 / WS)[n]
                for o, w, g0 in ((0, 64, 0), (64, 32, 32), (96, 32, 0)):
                    v = tab.rearrange("p t a d -> p t (a d)")[:, :, o:o + w]
                    own.step(dve.scalar_tensor_tensor(v, v, s, gq[:, n, g0:g0 + w].unsqueeze(1).broadcast_to((P, NT, w)),
                                                      ALU.mult, ALU.mult))
            own.wait()

            def mean_square(u, it=0):
                (g, t), par, m = UNITS[u], u % 2, it * 2
                if g == 2:
                    return
                w = HQ if g == 0 else HKV
                dve.wait_ge(pr_sq, m + n_normed(u))
                own.step(dve.tensor_reduce(ssq[:, par, 0:w], bT[par][:, 0:w * HD].rearrange("p (h d) -> p h d", d=HD),
                                           AX, ALU.add))
                own.wait()
                dve.tensor_scalar(ssq[:, par, 0:w], ssq[:, par, 0:w], 1.0 / (HD * WS * WS), EPS, ALU.mult, ALU.add)\
                    .then_inc(pr_ms, 1)

            def rotate(u, it=0):
                (g, t), par, m = UNITS[u], u % 2, it * 2
                if g == 2:
                    return
                w = HQ if g == 0 else HKV
                dve.wait_ge(pr_rs, m + n_normed(u))
                if g == 1:
                    dve.wait_ge(pr_v, m + u + 1)
                if u >= 2:
                    dve.wait_ge(pr_hi, m + u - 1)
                n = nT[par][:, 0:w * HD].rearrange("p (h d) -> p h d", d=HD)
                b = bT[par][:, 0:w * HD].rearrange("p (h d) -> p h d", d=HD)
                dve.tensor_tensor(n, PS[:, par, 0:w * HD].rearrange("p (h d) -> p h d", d=HD),
                                  rsq[:, par, 0:w].unsqueeze(2).broadcast_to((P, w, HD)), ALU.mult).then_inc(pr_n, 1)
                dve.wait_ge(pr_n, m + n_normed(u))
                if t >= NT:
                    dve.tensor_tensor(n, n, gkc.unsqueeze(1).broadcast_to((P, w, HD)), ALU.mult).then_inc(pr_r, 1)
                    return
                tab = (gc if g == 0 else gk)[:, t + m]

                def of(a, o, k):
                    return tab[:, a, o:o + k].unsqueeze(1).broadcast_to((P, w, k))

                own.step(dve.tensor_tensor(b[:, :, 0:32], n[:, :, 32:64], of(1, 0, 32), ALU.mult))
                own.step(dve.tensor_tensor(b[:, :, 32:64], n[:, :, 0:32], of(1, 32, 32), ALU.mult))
                own.wait()
                own.step(dve.tensor_tensor(n, n, of(0, 0, 64), ALU.mult))
                own.wait()
                dve.tensor_tensor(n, n, b, ALU.add).then_inc(pr_r, 1)

            def lo_parts(u, it=0):
                (g, t), par, m = UNITS[u], u % 2, it * 2
                dve.wait_ge(pr_hi, m + u + 1)
                for hi, lo, src in stacks(g, t, par):
                    ins = dve.tensor_tensor(lo, src, hi, ALU.subtract)
                ins.then_inc(pr_lo, 1)

            def slot(u, it=0):
                if u < NU:
                    mean_square(u, it)
                if 1 <= u <= NU:
                    lo_parts(u - 1, it)
                if u < NU:
                    rotate(u, it)

            for g in (1, 2, 0):
                u0 = GROUP0[g]
                slot(u0)
                if g == 2:
                    for i in range(4, 6):
                        lo_of(chunk_index("qkv", i), spl(i - 2, 4, 512))
                slot(u0 + 1)
                with dve.Fori(0, 3) as it:
                    own.enter(it, {1: 8, 2: 0, 0: 8}[g])
                    for b in range(2):
                        slot(u0 + 2 + b, it)
                    own.leave(3)
                if g:
                    slot(u0 + 8)
                    slot(u0 + 9)
            slot(NU)

            def maximum(u):
                dve.wait_ge(s_mm, u.n + 1)
                o, w = 1536 * u.par, (7 if u.na else 10) * P
                if u.na:
                    dve.wait_ge(bias_rdy, u.blk * 5 + 5)
                    b = bias[:, u.blk % 2, bias_kind(u.j)].rearrange("p i w -> p (i w)")
                    dve.tensor_tensor(PSf[:, o:o + 640], PSf[:, o:o + 640], b, ALU.add).then_inc(bias_add, 1)
                    dve.wait_ge(bias_add, u.n + 1)
                dve.tensor_reduce(nmax[:, u.par:u.par + 1], PSf[:, o:o + w], AX, ALU.max, negate=True)\
                    .then_inc(s_max, 1)

            def copy_p(u):
                if u.na:
                    return
                dve.wait_ge(pt_mm, u.turned(2))
                dve.wait_ge(o_mm, u.n - 1)
                o = 1536 * u.par + 1024
                dve.tensor_copy(flat(PT[:, u.par, 8:10]), PSf[:, o:o + 256]).then_inc(pt_d, 1)

            def normalise(u):
                dve.wait_ge(o_mm, u.n + 1)
                own.step(dve.reciprocal(rcp[:, u.par:u.par + 1], esum[:, u.v % 4:u.v % 4 + 1]))
                own.wait()
                if u.na:
                    dst = mixtok[:, u.j, bass.ds(u.blk * HD + HQ * HD, HD)]
                else:
                    dst = mixtok[:, u.blk, u.j * HD:u.j * HD + HD]
                dve.tensor_scalar(dst, PS[:, 6 + u.par, 0:HD], rcp[:, u.par:u.par + 1], None, ALU.mult)\
                    .then_inc(o_rdy, 1)

            def attend(u):
                if u.v < NV - 1:
                    maximum(u.ahead(1))
                copy_p(u)
                if u.v:
                    normalise(u.ahead(-1))

            maximum(Unit(0))
            for v in range(3):
                attend(Unit(v))
            with dve.Fori(0, HN - 1) as it:
                own.enter(it, 8)
                for v in range(3, 11):
                    attend(Unit(v, it))
                own.leave(HN - 1)
            for v in range(27, 33):
                attend(Unit(v))
            with dve.Fori(0, NT - 1) as it:
                own.enter(it, 8)
                for v in range(33, 41):
                    attend(Unit(v, it))
                own.leave(NT - 1)
            for v in range(89, NV):
                attend(Unit(v))
            normalise(Unit(NV - 1))

            own.step(dve.memset(ones, 1.0))
            own.wait()
            for n in range(2):
                if n:
                    dve.wait_ge(gate_mm, 1)
                g0 = (16, 40)[n]
                dve.tensor_tensor(diag, ident.unsqueeze(1).broadcast_to((P, 8, P)),
                                  mod[:, g0:g0 + 8, 0:1].broadcast_to((P, 8, P)), ALU.mult).then_inc(gate_d, 1)
            for t in range(NT):
                dve.wait_ge(mx_hi, t + 1)
                o, cut = 2048 + 1024 * (t % 2), slice(t * P, t * P + P)
                dve.tensor_tensor(mixT[:, 1, :, cut], PSf[:, o:o + 768].rearrange("p (f t) -> p f t", f=6),
                                  mixT[:, 0, :, cut], ALU.subtract).then_inc(mx_lo, 1)
            for b in range(2):
                lo_of(chunk_index("fi", b), fiS[b])

            def residual(t):
                dve.wait_ge(wo_mm, t + 1)
                dve.scalar_tensor_tensor(wtmp[:, t % 2], PSf[:, 1024 * (t % 2):1024 * (t % 2) + 1024], 1 / WS, gate1,
                                         ALU.mult, ALU.mult).then_inc(x1_rdy, 1)
                dve.wait_ge(x1_rdy, t + 1)
                dve.tensor_tensor(x1[:, t], x1[:, t], wtmp[:, t % 2], ALU.add).then_inc(x1_sum, 1)

            def mean1(half):
                dve.wait_ge(sq1, 4 * half + 4)
                dve.tensor_scalar(ss[:, 4 * half:4 * half + 4], ss[:, 4 * half:4 * half + 4], 1.0 / D, EPS,
                                  ALU.mult, ALU.add).then_inc(ms1, 1)

            def normalise1(half):
                dve.wait_ge(rs1, half + 1)
                if half:
                    dve.wait_ge(hT_mm, 20 + KD)
                for i in range(4):
                    ins = dve.tensor_scalar(xn1[:, i], x1[:, 4 * half + i], rs[:, 4 * half + i:4 * half + i + 1], None,
                                            ALU.mult)
                ins.then_inc(xn1_rdy, 1)

            dve.wait_ge(gate_rdy, 2)
            dve.wait_ge(x1_in, 64)
            for t in range(NT):
                residual(t)
                if t == 4:
                    mean1(0)
                if t == 6:
                    normalise1(0)
            mean1(1)

            for n in range(16):
                if n == 8:
                    normalise1(1)
                f, o = n % KD, 512 * (n // KD)
                split_h(20 + n, h2tmp[:, n % 2], hT[:, 0, f, o:o + 512], hT[:, 1, f, o:o + 512])

            def gated(b, j, first=False):
                dve.wait_ge(fi_s, j + 1)
                if not first:
                    dve.wait_ge(fi_lo, j)
                dve.scalar_tensor_tensor(pr, PSf[:, 2048 * b + 1024:2048 * b + 2048], GS / WS, sg, ALU.mult, ALU.mult)\
                    .then_inc(fi_p, 1)

            def gated_lo(j):
                dve.wait_ge(fi_hi, j + 1)
                dve.tensor_tensor(prodT[:, 1, j, :], pr, prodT[:, 0, j, :], ALU.subtract).then_inc(fi_lo, 1)

            c0 = chunk_index("fi", 0)
            for b in range(2):
                gated(b, b, b == 0)
                lo_of(c0 + 2 + b, fiS[b])
                gated_lo(b)
            with dve.Fori(0, KF // 2 - 2) as it:
                for b in range(2):
                    gated(b, it * 2 + 2 + b)
                    dve.wait_ge(split_hi, it * 2 + n_split(c0 + 4 + b))
                    dve.scalar_tensor_tensor(flat(fiS[b][:, 1]), f32(RAW(b), 2048), WS, flat(fiS[b][:, 0]),
                                             ALU.mult, ALU.subtract).then_inc(split_lo, 1)
                    gated_lo(it * 2 + 2 + b)
            for b in range(2):
                gated(b, KF - 2 + b)
                lo_of(chunk_index("fo", b), foS[b])
                gated_lo(KF - 2 + b)

            c1 = chunk_index("fo", 0)

            def fo_lo(s, base_c, it=0):
                dve.wait_ge(split_hi, it + n_split(base_c))
                dve.scalar_tensor_tensor(flat(foS[s][:, 1]), f32(RAW(s), 2048), WS, flat(foS[s][:, 0]),
                                         ALU.mult, ALU.subtract).then_inc(split_lo, 1)

            def gate_out(t):
                dve.wait_ge(fo_mm, t + 1)
                dve.tensor_tensor(otmp[:, t % 4], PSf[:, 1024 * (t % 4):1024 * (t % 4) + 1024], gate2, ALU.mult)\
                    .then_inc(fo_r, 1)
                dve.wait_ge(fo_r, t + 1)
                dve.tensor_tensor(x1[:, t], x1[:, t], otmp[:, t % 4], ALU.add).then_inc(fo_x, 1)

            def mean_out(t):
                dve.wait_ge(fo_sq, t + 1)
                dve.tensor_scalar(ss[:, t:t + 1], ss[:, t:t + 1], 1.0 / D, EPS, ALU.mult, ALU.add).then_inc(fo_ms, 1)

            def norm_out(t):
                dve.wait_ge(fo_rs, t + 1)
                dve.scalar_tensor_tensor(x1[:, t], x1[:, t], rs[:, t:t + 1], gfin, ALU.mult, ALU.mult).then_inc(fo_y, 1)

            with dve.Fori(0, 4) as it:
                for b in range(2):
                    fo_lo(b, c1 + 2 + b, it * 2)
            for m in (10, 11):
                fo_lo(m % 2, c1 + m)
            gate_out(0)
            gate_out(1)
            fo_lo(0, c1 + 12)
            gate_out(2)
            gate_out(3)
            dve.wait_ge(gf_in, 16)
            for t in range(4):
                mean_out(t)
                if t:
                    norm_out(t - 1)
            norm_out(3)
            with dve.Fori(0, 4) as it:
                for b in range(2):
                    fo_lo(1 - b, c1 + 13 + b, it * 2)
            fo_lo(1, c1 + 21)
            for t in range(4, NT):
                gate_out(t)
                if t > 4:
                    mean_out(t - 1)
                if t > 5:
                    norm_out(t - 2)
            mean_out(NT - 1)
            norm_out(NT - 2)
            norm_out(NT - 1)


INPUTS = ["x", "c", "ctx", "c_ctx", "w_mod", "b_mod", "g_mix", "g_ffn", "w_in", "w_out", "hy_conv_w", "hy_conv_b",
          "hy_f_w1", "hy_f_b1", "hy_f_w2", "hy_f_b2", "hy_f_w3", "hy_f_b3", "hy_f_wout", "hy_f_freq", "hy_skip",
          "qk_g_q", "qk_g_k", "na_rpb", "w_ffn_in", "w_ffn_out", "g_final"]


def kernel(**inputs):
    import concourse.bacc as bacc
    from concourse.bass_utils import run_bass_kernel_spmd

    nc = bacc.Bacc("TRN2", target_bir_lowering=False, num_devices=1)
    tables = constants()
    arrays = {"in_" + n: np.ascontiguousarray(inputs[n]) for n in INPUTS} | tables
    dram = {n: nc.dram_tensor(n, a.shape, mybir.dt.from_np(a.dtype), kind="ExternalInput").ap()
            for n, a in arrays.items()}
    out = nc.dram_tensor("out", (1, S, D), F32, kind="ExternalOutput").ap()
    build(nc, {n: dram["in_" + n] for n in INPUTS}, {n[4:]: dram[n] for n in tables}, out)
    return run_bass_kernel_spmd(nc, [arrays], core_ids=[0]).results[0]["out"]
```

```python
import math
from contextlib import ExitStack

import numpy as np

import concourse.bass as bass
import concourse.mybir as mybir

F32 = mybir.dt.float32
F16 = mybir.dt.float16
ACT = mybir.ActivationFunctionType
ALU = mybir.AluOpType
AX = mybir.AxisListType.X

P = 128
S, C, D = 1024, 256, 1024
NT, NC, KD = S // P, C // P, D // P
HD = 64
HQ, HKV, HN = 8, 2, 4
HYW = 256
GRID_W, ROWS, KH, KW = 64, 16, 8, 16
FH = 2816
KF = FH // P
QKV0 = 3 * HYW
FW, EMB = 64, 33
EPS = 1e-6
NEG = -1e30
HALF = S // 2

WS = 2.0 ** 8
HS = 2.0 ** -6
PSC = 2.0 ** 12
VS = 2.0 ** 4
GS = 2.0 ** -8
MAGIC = 1.5 * 2.0 ** 23
TWO_PI_1 = 6.28125
TWO_PI_2 = float(np.float32(np.round((2 * math.pi - TWO_PI_1) * 2 ** 21) / 2 ** 21))
TWO_PI_3 = float(np.float32(2 * math.pi - TWO_PI_1 - TWO_PI_2))
PI_IN = 3.1415925

V_BMOD, V_GMIX, V_GFFN, V_C, V_CC, V_CW, V_CB, V_SKIP = 0, 48, 56, 64, 72, 80, 98, 104
N_ROWS = 106

CHUNKS = (["mod"] * 8 + ["ff", "ff", "hy", "ff", "ff", "hy"] + ["late"] * 3 + ["hy"] + ["late"] * 9
          + ["fwd", "fwd", "late", "inv", "fwd", "late", "inv", "fwd", "late", "inv", "late", "inv"]
          + ["qkv"] * 6 + ["wo"] * 4 + ["fi"] * KF + ["fo"] * KF)
N_EARLY = CHUNKS.index("wo")
AS_IS = ("ff", "mod", "late", "fwd", "inv")
GW = 1024


def chunk_slot(c):
    return c % 4 if c < N_EARLY else (c - N_EARLY) % 2


def chunk_arrivals(c):
    return sum(1 + (CHUNKS[i] == "fi") for i in range(c + 1) if chunk_slot(i) == chunk_slot(c))


def chunk_before(c):
    return next((i for i in range(c - 1, -1, -1) if chunk_slot(i) == chunk_slot(c)), None)


def n_of_kind(c, *kinds):
    return sum(k in kinds for k in CHUNKS[:c + 1])


def n_split(c):
    return sum(k not in AS_IS and k != "wo" for k in CHUNKS[:c + 1])


def chunk_index(kind, n):
    return [i for i, k in enumerate(CHUNKS) if k == kind][n]


def flat(v):
    names = "abcd"[:len(v.shape) - 1]
    return v if len(names) == 1 else v.rearrange(f"p {' '.join(names)} -> p ({' '.join(names)})")


def constants():
    pos = np.arange(S)
    inv = (10000.0 ** (-np.arange(HD // 4, dtype=np.float32) / (HD // 4))).astype(np.float32)
    ang = np.concatenate([(pos // GRID_W).astype(np.float32)[:, None] * inv,
                          (pos % GRID_W).astype(np.float32)[:, None] * inv], -1).astype(np.float32)
    cos, sin = np.cos(ang.astype(np.float64)), np.sin(ang.astype(np.float64))
    rope = np.stack([np.concatenate([cos, cos], 1), np.concatenate([-sin, sin], 1)], 1)
    rope = rope.reshape(NT, P, 2, HD).transpose(1, 0, 2, 3)

    perm = np.concatenate([np.arange(0, S, 2), np.arange(1, S, 2)])
    t = np.linspace(0.0, 1.0, S, dtype=np.float32)[:, None]
    bands = (EMB - 1) // 2
    w = (np.float32(2.0 * math.pi) * np.arange(S, dtype=np.float32)[:, None] / np.float32(S)).astype(np.float32)
    fr = np.linspace(1e-4, bands - 1, bands, dtype=np.float32)[None, :]
    arg = (fr * w).astype(np.float32).astype(np.float64)
    z = np.concatenate([t, np.cos(arg), -np.sin(arg)], -1)[perm].T
    zt = np.zeros((P, HALF))
    zt[0:EMB], zt[64:64 + EMB] = z[:, :HALF], z[:, HALF:]
    deltas = np.linspace(math.log(1e-2) / 1.5, math.log(1e-2) / 0.3, HYW, dtype=np.float32)
    decay = np.exp((-t * np.abs(deltas)).astype(np.float64))
    decay = np.concatenate([decay, decay], 1)
    decay[0, HYW:] = 0.0
    decay = decay[perm].reshape(NT, P, 2 * HYW).transpose(1, 0, 2)

    n = np.arange(S)[:, None]
    k = np.arange(HALF)[None, :]
    theta = np.pi * ((n * (2 * k + 1)) % 4096) / 2048.0
    cs = np.stack([np.cos(theta), np.sin(theta)], 1)[perm]
    fwd = cs.reshape(NT, P, 2, 4, P).transpose(3, 1, 0, 2, 4)
    inv_t = cs.transpose(2, 1, 0).reshape(4, P, 2, S)

    w_ = np.arange(P) % GRID_W
    wk = np.arange(GRID_W)
    first = np.clip(w_ - KW // 2, 0, GRID_W - KW)[:, None]
    cmask = np.where((wk >= first) & (wk < first + KW), 0.0, NEG)
    rmask = np.zeros((P, 5, 10))
    for n_, tile in enumerate([0, 1, 3, 6, 7]):
        for p in range(P):
            r = 2 * tile + p // GRID_W
            rs = min(max(r - KH // 2, 0), ROWS - KH)
            for i in range(10):
                kr = 2 * window(tile) + i
                rmask[p, n_, i] = 0.0 if rs <= kr < rs + KH else NEG
    out = dict(ident=np.eye(P), rope=rope, zt=zt, decay=decay, fwd=fwd, inv=inv_t, cmask=cmask, rmask=rmask)
    return {"cst_" + n_: np.ascontiguousarray(a, np.float32) for n_, a in out.items()}


def window(t):
    return min(max(t - 2, 0), 3)


def bias_kind(t):
    return {0: 0, 1: 1, 6: 3, 7: 4}.get(t, 2)


def bias_shift(kind):
    return [8, 6, 4, 2, 0][kind]


class Unit:

    def __init__(self, v, it=0):
        self.v, self.it, self.par, self.na = v, it, v % 2, v < HN * NT
        self.n = v + 8 * it
        w = v if self.na else v - HN * NT
        self.blk, self.j = w // 8 + it, w % 8
        self.kv = None if self.na else self.j // (HQ // HKV)
        self.n_gqa = self.n - HN * NT
        self.banks = [range(0, 4), range(4, 7)] if self.na else [range(0, 4), range(4, 8), range(8, 10)]

    def turned(self, bank):
        return 2 * self.n + bank + 1 if self.na else 2 * HN * NT + 3 * self.n_gqa + bank + 1

    def turned_at(self, bank):
        if bank == 2:
            return 512 * (6 + self.par) + 256
        return 1536 * self.par + 512 * (bank + (self.na and bank == 1))

    def ahead(self, d):
        return Unit(self.v + d, self.it)


class Chain:

    def __init__(self, eng, sem):
        self.eng, self.sem, self.n = eng, sem, 0

    def step(self, ins):
        ins.then_inc(self.sem, 1)
        self.n = self.n + 1

    def wait(self):
        self.eng.wait_ge(self.sem, self.n)

    def enter(self, it, per):
        self.base = self.n
        self.per = per
        self.n = it * per + self.base

    def leave(self, count):
        self.n = self.base + count * self.per


def build(nc, io, cst, out):
    ctx = ExitStack()
    with ctx:
        sem = lambda name: ctx.enter_context(nc.semaphore(name))
        arena = ctx.enter_context(nc.sbuf_tensor("arena", [P, 207 * 256], F32))
        PS = ctx.enter_context(nc.psum_tensor("PS", [P, 8, 512], F32))
        skew = nc.dram_tensor("skewed_bias_rows", (HN, 19, 64, P), F32, kind="Internal")
        gates = nc.dram_tensor("gates", (2, D), F32, kind="Internal").ap()

        def f32(kb, *shape):
            n = int(np.prod(shape))
            o = int(kb * 256)
            v = arena[:, o:o + n]
            names = "abcd"[:len(shape)]
            if len(shape) > 1:
                v = v.rearrange(f"p ({' '.join(names)}) -> p {' '.join(names)}",
                                **{c: s for c, s in zip(names, shape)})
            return v

        def f16(kb, *shape):
            n = int(np.prod(shape))
            o = int(kb * 256)
            v = arena[:, o:o + n // 2].bitcast(F16)
            names = "abcd"[:len(shape)]
            if len(shape) > 1:
                v = v.rearrange(f"p ({' '.join(names)}) -> p {' '.join(names)}",
                                **{c: s for c, s in zip(names, shape)})
            return v

        ident = f32(0, P)
        ident16 = f16(0.5, P)
        cols = f32(0.75, P)
        mod = f32(1.25, 48, 2)
        am = f32(1.625, 8, 2)
        af = f32(1.6875, 8, 2)
        silu_c = f32(1.75, 8, 2)
        cwb = f32(1.8125, 18)
        fvec = f32(1.9, 4)
        ss = f32(2.0, 16)
        rs = f32(2.0625, 16)
        neghalf = f32(2.125, 16)
        ones1 = f32(2.1875, 1)
        warm = f32(2.19921875, 1)
        ssq = f32(2.25, 2, 8)
        rsq = f32(2.3125, 2, 8)
        nmax = f32(2.375, 2)
        cmax = f32(2.390625, 2)
        esum = f32(2.40625, 4)
        rcp = f32(2.4375, 2)
        gq = f32(2.5, 2, HD)
        rmask = f32(3.0, 5, 10)
        cmask = f32(3.25, GRID_W)
        gkc = f32(3.5, HD)

        PSf = PS[:, :, :].rearrange("p a b -> p (a b)")
        RAW = lambda s: 4 + 8 * s
        Z = 108

        def raw(c, *shape):
            return f32(RAW(chunk_slot(c)), *shape)

        def spl(slot, *shape):
            return f16(36 + 8 * slot, 2, *shape)

        hT = f16(68, 2, KD, S)
        hcT = f16(100, 2, KD, C)
        yT = f16(Z, 2, 2, S)
        x2T = f32(Z + 8, 2, S)
        uvT = f32(Z + 16, 2, S)
        vtok = f32(Z + 24, NT, HYW)
        Fc = f32(Z + 32, 4, 2 * HYW)
        Fs = f32(Z + 40, 4, 2 * HYW)
        zt = f32(Z + 8, HALF)
        fu = f32(Z + 12, HALF)
        fk = f32(Z + 16, HALF)
        fh = f32(Z + 20, HALF)
        mrow = f32(Z, 2, GW)
        macc = f32(Z, 2, GW)
        decay = f32(Z + 24, NT, 2 * HYW)
        fw = f32(Z + 40, 4, P)
        fwo = f32(Z + 42, 2 * HYW)
        fbd = f32(Z + 44, 2, 2, HYW)
        filt_a = f32(52, NT, HYW)
        filt_b = f32(60, NT, HYW)
        rows = f32(Z + 48, P)
        accx = f32(Z + 48, 2, S)
        htmp = f32(Z + 48, 2, 512)
        tE = f32(Z + 56, 2, 2, HYW)
        tE0 = f32(Z + 52, 2, 2, HYW)
        xs = f32(Z + 59, 10, D)
        V2c = f32(Z + 60, 512)
        V2s = f32(Z + 62, 512)
        t1 = f32(Z + 64, 512)
        t2 = f32(Z + 66, 512)
        Yc = f32(Z + 68, 512)
        Ys = f32(Z + 70, 512)
        G = f32(Z + 72, 2, 4, HYW)
        yo = f32(Z + 80, 2, 512)
        t3 = f32(Z + 84, 512)
        t4 = f32(Z + 48, 512)
        qT = f16(Z + 8, HQ, S)
        kT = f16(Z + 24, HKV, 2, S + C)
        V = f16(Z + 34, NT + NC, 6, 2, HD)
        nqT = f16(Z + 59, HN, S)
        nkT = f16(Z + 67, HN, 2, S + C)
        nT = [f32(Z + 49, 512), f32(Z + 51, 512)]
        bT = [f32(Z + 53, 512), f32(Z + 55, 512)]
        stk = [f16(Z + 57, 1024), f16(Z + 95, 1024)]
        skrow = f32(Z + 97, P)
        gc = f32(Z + 87, NT, 2, HD)
        gk = f32(Z + 91, NT, 2, HD)
        Pb = f32(Z + 49, 2, 10, P)
        J = f32(20, 2, 18, GRID_W)
        bias = f32(36, 2, 5, 10, GRID_W)
        mixtok = f32(68, NT, 768)
        PT = f16(92, 2, 2, 10, P)
        oab = f32(36, NT, HQ, 2, HD)
        woS = [f16(Z + 59 + 8 * i, 2, 4, 512) for i in range(4)]
        mixT = f16(Z + 8, 2, 6, S)
        gate1 = f32(Z + 95, D)
        gate2 = f32(Z + 91, D)
        x1 = f32(20, NT, D)
        xn1 = f32(Z + 32, 4, D)
        wtmp = f32(Z + 49, 2, D)
        h2tmp = f32(100, 2, 512)
        fiS = [f16(52, 2, 8, 256), f16(60, 2, 8, 256)]
        foS = [f16(52, 2, 2, 1024), f16(60, 2, 2, 1024)]
        prodT = f16(Z, 2, KF, S)
        sg = f32(100, S)
        pr = f32(104, S)
        gfin = f32(68, D)
        osq = f32(88, D)

        first_in = sem("first_small_in")
        small_in = sem("filter_network_in")
        rest_in = sem("rest_in")
        x_in = [sem(f"x_in{i}") for i in range(3)]
        raw_in = [sem(f"raw_in{i}") for i in range(4)]
        split_hi = sem("split_hi")
        split_lo = sem("split_lo")
        wo_split = sem("w_out_split")
        id16_rdy = sem("ident16_ready")
        cols_rdy = sem("columns_ready")
        silu_rdy = sem("silu_of_c_ready")
        mlp_mm = sem("filter_layer_product")
        mlp_arg = sem("filter_layer_argument")
        mlp_h = sem("filter_layer_value")
        taps_mm = sem("filter_taps_product")
        taps_rdy = sem("filter_taps_ready")
        spec_mm = sem("spectrum_product")
        even_part = sem("even_part_copied")
        spec_rdy = sem("spectrum_ready")
        cols_mm = sem("columns_transposed")
        mod_used = sem("modulation_chunk_used")
        mrow_rdy = sem("modulation_row_copied")
        mcol_mm = sem("modulation_by_feature")
        late_used = sem("late_product_added")
        late_mm = sem("late_group_by_feature")
        late_rdy = sem("late_groups_ready")
        mod_rdy = sem("modulation_ready")
        sq_done = sem("squares_summed")
        ms_rdy = sem("mean_square_ready")
        rs_rdy = sem("inverse_root_ready")
        xn_rdy = sem("x_normalised")
        hT_mm = sem("h_transposed")
        hT_f = sem("h_modulated")
        hT_rdy = sem("h_split")
        hy_mm = sem("hyena_projection")
        hy_mid = sem("middle_tap")
        hy_rdy = sem("short_convolution")
        vt_mm = sem("v_transposed")
        vt_rdy = sem("v_by_token")
        G_rdy = sem("folded_spectrum")
        inv_mm = sem("inverse_products")
        y_f = sem("hyena_output")
        y_hi = sem("hyena_output_hi")
        y_rdy = sem("hyena_output_split")
        gn_in = sem("gains_in")
        pr_mm = sem("qkv_projection")
        pr_sq = sem("qk_squares")
        pr_n = sem("qk_scaled")
        pr_ms = sem("qk_mean_square")
        pr_rs = sem("qk_inverse_root")
        pr_r = sem("qk_rotated")
        pr_hi = sem("qk_hi")
        pr_lo = sem("qk_lo")
        pr_v = sem("values_hi")
        pr_vl = sem("values_lo")
        pr_tm = sem("qk_transposed")
        pr_tc = sem("qk_transposed_copied")
        skew_rows = sem("bias_rows_in")
        skew_set = sem("bias_rows_cleared")
        skew_out = sem("bias_rows_out")
        J_in = [sem("bias_table_in0"), sem("bias_table_in1")]
        bias_add = sem("bias_added")
        bias_rdy = sem("bias_ready")
        s_mm = sem("scores")
        s_max = sem("score_maximum")
        s_neg = sem("maximum_negated")
        s_exp = sem("exponentials")
        pt_mm = sem("probabilities_transposed")
        pt_hi = sem("probabilities_hi")
        pt_lo = sem("probabilities_lo")
        o_mm = sem("values_weighted")
        o_rdy = sem("attention_output")
        rcp_rdy = sem("inverse_sum_ready")
        oab_sum = sem("outputs_added")
        gates_out = sem("gates_out")
        gates_in = sem("gates_in")
        mx_mm = sem("mix_transposed")
        mx_hi = sem("mix_hi")
        mx_lo = sem("mix_lo")
        wo_mm = sem("output_projection")
        x1_rdy = sem("x1_ready")
        x1_sum = sem("x1_summed")
        x1_in = sem("x_again_in")
        sq1 = sem("x1_squares")
        ms1 = sem("x1_mean_square")
        rs1 = sem("x1_inverse_root")
        xn1_rdy = sem("x1_normalised")
        fi_mm = sem("ffn_in_product")
        fi_s = sem("silu_done")
        fi_p = sem("gated")
        fi_hi = sem("gated_hi")
        fi_lo = sem("gated_lo")
        fo_used = sem("ffn_out_chunk_used")
        fo_x = sem("x2_summed")
        fo_gated = sem("ffn_out_chunk_gated")
        fo_mm = sem("ffn_out_product")
        fo_sq = sem("x2_squares")
        fo_ms = sem("x2_mean_square")
        fo_rs = sem("x2_inverse_root")
        fo_y = sem("output_row_ready")
        gf_in = sem("g_final_in")
        out_done = sem("output_stored")
        dve_own = sem("vector_steps")
        pool_own = sem("pool_steps")

        block = ctx.enter_context(nc.Block())
        x_rows = io["x"].rearrange("b (t p) d -> p (b t) d", p=P)
        ctx_rows = io["ctx"].rearrange("b (t p) d -> p (b t) d", p=P)
        out_rows = out.rearrange("b (t p) d -> p (b t) d", p=P)
        w_mod = io["w_mod"][0].rearrange("(k p) n -> p k n", p=P)
        w_in = io["w_in"][0].rearrange("(k p) n -> p k n", p=P)
        w_out = io["w_out"][0].rearrange("(k p) n -> p k n", p=P)
        w_fi = io["w_ffn_in"][0].rearrange("(k p) n -> p k n", p=P)
        w_fo = io["w_ffn_out"][0].rearrange("(k p) n -> p k n", p=P)
        first = [
            (rows[V_C:V_C + 8], io["c"][0].rearrange("(t p) -> t p", p=P)),
            (rows[V_CC:V_CC + 8], io["c_ctx"].rearrange("(t p) -> t p", p=P)),
            (ident, cst["ident"]),
            (rows[V_BMOD:V_BMOD + 48], io["b_mod"][0].rearrange("(t p) -> t p", p=P)),
            (rows[V_GMIX:V_GMIX + 8], io["g_mix"][0].rearrange("(t p) -> t p", p=P)),
            (rows[V_GFFN:V_GFFN + 8], io["g_ffn"][0].rearrange("(t p) -> t p", p=P)),
            (rows[V_CW:V_CW + 18], io["hy_conv_w"][0].rearrange("i (t p) -> (i t) p", p=P)),
            (rows[V_CB:V_CB + 6], io["hy_conv_b"][0].rearrange("(t p) -> t p", p=P)),
            (rows[V_SKIP:V_SKIP + 2], io["hy_skip"][0].rearrange("(t p) -> t p", p=P)),
        ]
        def twice(v):
            return bass.AP(tensor=v.tensor, offset=v.offset, ap=[[0, 2]] + [list(d) for d in v.ap])

        small = [(zt, cst["zt"])]
        small += [(fw[64 * h:64 * h + EMB, 0, 0:FW], io["hy_f_w1"][0]) for h in range(2)]
        small += [(fvec[:, n:n + 1], twice(io[v].rearrange("a f -> f a")))
                  for n, v in enumerate(("hy_f_b1", "hy_f_b2", "hy_f_b3", "hy_f_freq"))]
        small += [(fw[:, n, 0:FW], twice(io[v][0])) for n, v in ((1, "hy_f_w2"), (2, "hy_f_w3"))]
        small.append((fwo, twice(io["hy_f_wout"][0])))
        rest = [
            (decay, cst["decay"]),
            (gq[:, 0], io["qk_g_q"][0].partition_broadcast(P)),
            (gq[:, 1], io["qk_g_k"][0].partition_broadcast(P)),
            (rmask, cst["rmask"]),
            (cmask, cst["cmask"]),
        ]
        N_FIRST = len(first) * 16
        N_REST = len(rest) * 16
        N_SMALL = len(small) * 16

        X1_PARTS = ((0, 4), (4, 7), (7, 8))
        GROUPS = (1, 0, 2)
        UNITS = [(g, t) for g in GROUPS for t in range(NT + (NC if g else 0))]
        NU = len(UNITS)
        GROUP0 = {g: UNITS.index((g, 0)) for g in GROUPS}

        def n_normed(u):
            return sum(g != 2 for g, _ in UNITS[:u + 1])

        def n_valued(u):
            return sum(g != 0 for g, _ in UNITS[:u + 1])

        NV = HN * NT + HQ * NT
        NNA = HN * NT

        def arrived(eng, c, more=0):
            eng.wait_ge(raw_in[chunk_slot(c)], more * 16 + 16 * chunk_arrivals(c))

        def stacks(g, t, par):
            out = []
            n_k = {1: HKV, 2: HN, 0: 0}[g]
            if n_k:
                v = stk[par][:, 0:n_k * 256].rearrange("p (h a r d) -> p h a r d", h=n_k, a=2, r=2)
                src = nT[par][:, 0:n_k * HD].rearrange("p (h d) -> p h d", d=HD).unsqueeze(2)\
                    .broadcast_to((P, n_k, 2, HD))
                out.append((v[:, :, 0], v[:, :, 1], src))
            if g == 0 or (g == 1 and t < NT):
                n_q, o, s = (HQ, 0, 0) if g == 0 else (HN, 512, 128)
                v = stk[par][:, o:o + n_q * 128].rearrange("p (h a d) -> p h a d", h=n_q, a=2)
                out.append((v[:, :, 0], v[:, :, 1], nT[par][:, s:s + n_q * HD].rearrange("p (h d) -> p h d", d=HD)))
            return out

        def tok(t):
            return bass.ds(t * P, P)

        @block.sync
        def _(sp):
            def load(c, src, shape):
                before = chunk_before(c)
                if before is not None:
                    kind = CHUNKS[before]
                    if kind in ("ff", "fwd"):
                        sp.wait_ge(spec_mm, n_of_kind(before, "ff", "fwd"))
                    elif kind == "inv":
                        sp.wait_ge(inv_mm, n_of_kind(before, "inv"))
                    elif kind == "mod":
                        sp.wait_ge(mod_used, n_of_kind(before, "mod"))
                    elif kind == "late":
                        sp.wait_ge(late_used, 2 * n_of_kind(before, "late"))
                    elif kind == "wo":
                        sp.wait_ge(wo_split, n_of_kind(before, "wo"))
                    else:
                        sp.wait_ge(split_lo, n_split(before))
                sp.dma_start(raw(c, *shape), src).then_inc(raw_in[chunk_slot(c)], 16)

            for dst, src in first:
                sp.dma_start(dst, src).then_inc(first_in, 16)
            n_of = dict.fromkeys(CHUNKS, 0)
            for c in range(N_EARLY):
                if c == 1:
                    sp.wait_ge(small_in, N_SMALL)
                if c == 6:
                    for dst, src in rest:
                        sp.dma_start(dst, src).then_inc(rest_in, 16)
                if c in (6, 8):
                    i = c // 2 - 3
                    sp.dma_start(xs[:, 4 * i:4 * i + 4], x_rows[:, 4 * i:4 * i + 4]).then_inc(x_in[i], 16)
                if c == 8:
                    sp.dma_start(xs[:, 8:10], ctx_rows).then_inc(x_in[2], 16)
                kind = CHUNKS[c]
                n = n_of[kind]
                n_of[kind] += 1
                if kind in ("mod", "late"):
                    g, kp = n // 4 + (0 if kind == "mod" else 2), n % 4
                    load(c, w_mod[:, 2 * kp:2 * kp + 2, GW * g:GW * g + GW], (2, GW))
                elif kind == "hy":
                    load(c, w_in[:, :, 256 * n:256 * n + 256], (8, 256))
                elif kind in ("ff", "fwd"):
                    load(c, cst["fwd"][n].rearrange("p a b k -> p (a b) k"), (16, P))
                elif kind == "inv":
                    load(c, cst["inv"][n], (2, S))
                else:
                    col, kh = QKV0 + 512 * GROUPS[n // 2], 4 * (n % 2)
                    load(c, w_in[:, kh:kh + 4, col:col + 512], (4, 512))
                if kind == "hy" and n == 2:
                    sp.wait_ge(hT_mm, 20)
                    for tab in (gc, gk):
                        sp.dma_start(tab, cst["rope"]).then_inc(gn_in, 16)
            sp.wait_ge(late_rdy, 2)
            for n in range(2):
                t0 = (16, 40)[n]
                sp.dma_start(gates[n].rearrange("(t p) -> p t", p=P), mod[:, t0:t0 + 8, 0],
                             allow_slow_non_contiguous=True).then_inc(gates_out, 16)
            sp.wait_ge(gates_out, 32)
            sp.wait_ge(skew_out, 16)
            sp.wait_ge(split_lo, n_split(chunk_index("qkv", 5) - 1))
            for h in range(HN):
                if h >= 2:
                    sp.wait_ge(bias_rdy, 5 * (h - 1))
                for a in range(2):
                    src = bass.AP(tensor=skew, offset=(h * 19 + 1 - a) * 64 * P + 63,
                                  ap=[[P - 1, 64], [64 * P, 18], [1, GRID_W]])
                    sp.dma_start(J[64 * a:64 * a + 64, h % 2], src).then_inc(J_in[h % 2], 16)
                if h == 1:
                    sp.wait_ge(pr_tc, NU)
                    for n in range(2):
                        sp.dma_start((gate1, gate2)[n], gates[n].partition_broadcast(P)).then_inc(gates_in, 16)
                    for n in range(2):
                        load(chunk_index("wo", n), w_out[:, 0:4, 512 * n:512 * n + 512], (4, 512))
            for n in range(2, 4):
                load(chunk_index("wo", n), w_out[:, 4:8, 512 * (n % 2):512 * (n % 2) + 512], (4, 512))
            sp.wait_ge(bias_add, NNA)
            for i in range(4):
                if i >= 2:
                    sp.wait_ge(oab_sum, 2 * i - 2)
                sp.dma_start(x1[:, 2 * i:2 * i + 2], x_rows[:, 2 * i:2 * i + 2]).then_inc(x1_in, 16)
            c0 = chunk_index("fi", 0)

            def load_fi(j, b):
                for g in range(2):
                    sp.dma_start(f32(RAW(b), KD, 2, P)[:, :, g], w_fi[:, :, bass.ds(j * P + g * FH, P)])\
                        .then_inc(raw_in[b], 16)

            for b in range(2):
                sp.wait_ge(wo_split, 3 + b)
                load_fi(b, b)
            with sp.Fori(0, KF // 2 - 1) as it:
                for b in range(2):
                    sp.wait_ge(split_lo, it * 2 + n_split(c0 + b))
                    load_fi(it * 2 + 2 + b, b)
            c1 = chunk_index("fo", 0)
            for grp in range(2):
                with sp.Fori(0, 5) as it:
                    for b in range(2):
                        s = (grp + b) % 2
                        sp.wait_ge(split_lo, it * 2 + n_split(c1 + grp * 11 + b - 2))
                        sp.dma_start(f32(RAW(s), 2, D), w_fo[:, bass.ds(it * 4 + 2 * b, 2), :]).then_inc(raw_in[s], 16)
                sp.wait_ge(split_lo, n_split(c1 + grp * 11 + 8))
                sp.dma_start(f32(RAW(grp), 2, D), w_fo[:, 20:22, :]).then_inc(raw_in[grp], 16)
            for t in range(NT):
                sp.wait_ge(fo_y, t + 1)
                sp.dma_start(out_rows[:, t], x1[:, t]).then_inc(out_done, 16)
            sp.wait_ge(out_done, 16 * NT)

        @block.gpsimd
        def _(pool):
            own = Chain(pool, pool_own)
            own.step(pool.memset(neghalf, -0.5))
            own.step(pool.memset(ones1, 1.0))
            own.wait()
            for i, (a, b) in enumerate(((0, 4), (4, 8), (8, 10))):
                pool.wait_ge(ms_rdy, i + 1)
                pool.tensor_tensor(rs[:, a:b], ss[:, a:b], neghalf[:, a:b], ALU.pow).then_inc(rs_rdy, 1)
            pool.wait_ge(hT_mm, 20)
            pool.memset(skrow[0:HN * 19], NEG).then_inc(skew_set, 1)
            for u, (g, t) in enumerate(UNITS):
                if g == 2:
                    continue
                n, w = n_normed(u), HQ if g == 0 else HKV
                pool.wait_ge(pr_ms, n)
                pool.tensor_tensor(rsq[:, u % 2, 0:w], ssq[:, u % 2, 0:w], neghalf[:, 0:w], ALU.pow)\
                    .then_inc(pr_rs, 1)
            for h in range(HN):
                pool.wait_ge(J_in[h % 2], 32 * (h // 2 + 1))
                own.step(pool.tensor_tensor(J[:, h % 2], J[:, h % 2],
                                            cmask.unsqueeze(1).broadcast_to((P, 18, GRID_W)), ALU.add))
                own.wait()
                if h < 2:
                    pool.wait_ge(pr_mm, (GROUP0[2], NU)[h])
                else:
                    pool.wait_ge(bias_add, NT * (h - 1))
                for kind in range(5):
                    o = bias_shift(kind)
                    last = pool.tensor_tensor(bias[:, h % 2, kind], J[:, h % 2, o:o + 10],
                                              rmask[:, kind, :].unsqueeze(2).broadcast_to((P, 10, GRID_W)), ALU.add)
                    last.then_inc(bias_rdy, 1)
            for n in range(4):
                c = chunk_index("wo", n)
                arrived(pool, c)
                if n == 0:
                    pool.wait_ge(s_mm, NNA)
                r, (k0, hy) = raw(c, 4, 512), (4 * (n // 2), 2 if n < 2 else 0)
                if hy:
                    own.step(pool.tensor_scalar(r[:, 0:2], r[:, 0:2], WS / HS, None, ALU.mult))
                own.step(pool.tensor_scalar(r[:, hy:4], r[:, hy:4], WS, None, ALU.mult))
                own.wait()
                own.step(pool.tensor_copy(woS[n][:, 0], r))
                own.wait()
                pool.tensor_tensor(woS[n][:, 1], r, woS[n][:, 0], ALU.subtract).then_inc(wo_split, 1)
            for t in range(NT):
                pool.wait_ge(o_rdy, NNA + HQ * (t + 1))
                pool.tensor_tensor(mixtok[:, t, 0:HQ * HD].rearrange("p (h d) -> p h d", h=HQ), oab[:, t, :, 0],
                                   oab[:, t, :, 1], ALU.add).then_inc(oab_sum, 1)
            for n, (a, b) in enumerate(X1_PARTS):
                pool.wait_ge(ms1, n + 1)
                pool.tensor_tensor(rs[:, a:b], ss[:, a:b], neghalf[:, a:b], ALU.pow).then_inc(rs1, 1)
            for t in range(NT):
                pool.wait_ge(fo_ms, t + 1)
                pool.tensor_tensor(rs[:, t:t + 1], ss[:, t:t + 1], neghalf[:, 0:1], ALU.pow).then_inc(fo_rs, 1)

        @block.tensor
        def _(pe):
            def mm(out, lhsT, rhs, start, stop):
                return pe.matmul(out, lhsT, rhs, start=start, stop=stop, skip_group_check=True)

            pe.wait_ge(first_in, N_FIRST)
            pe.transpose(PS[:, 5, 0:N_ROWS], rows[0:N_ROWS], ident[0:N_ROWS, 0:N_ROWS]).then_inc(cols_mm, 1)

            def filter_layer(layer):
                if layer:
                    pe.wait_ge(mlp_h, layer)
                k = FW if layer else EMB
                for o in (0, FW):
                    ins = mm(PS[o:o + FW, 4, :], fw[o:o + k, layer, 0:FW], (fh if layer else zt)[o:o + k], True, True)
                ins.then_inc(mlp_mm, 1)

            def taps(nt):
                if nt >= 2:
                    pe.wait_ge(taps_rdy, nt - 1)
                o, t = FW * (nt // 4), nt % 4
                mm(PS[:, 6 + nt % 2, :], fh[o:o + FW, t * P:t * P + P], fwo[o:o + FW], True, True).then_inc(taps_mm, 1)

            def modulation(c):
                w = raw(c, 2, GW)
                arrived(pe, c)
                for i in range(2):
                    k = 2 * (c % 4) + i
                    for half in range(2):
                        ins = mm(PS[0:2, 2 * (c // 4) + half, :], silu_c[:, k], w[:, i, half * 512:half * 512 + 512],
                                 k == 0, k == KD - 1)
                ins.then_inc(mod_used, 1)

            pe.wait_ge(small_in, N_SMALL)
            filter_layer(0)
            pe.wait_ge(silu_rdy, 1)
            modulation(0)
            modulation(1)
            filter_layer(1)
            modulation(2)
            modulation(3)
            filter_layer(2)
            modulation(4)
            modulation(5)
            pe.wait_ge(mlp_h, 3)
            for nt in range(NT):
                taps(nt)
                if nt % 4 == 3:
                    modulation(6 + nt // 4)
            for g in range(2):
                pe.wait_ge(mrow_rdy, g + 1)
                for i in range(8):
                    o = 16 * g + 2 * i
                    ins = pe.transpose(PS[:, 5, o:o + 2], mrow[0:2, g, i * P:i * P + P], ident[0:2, 0:2])
            ins.then_inc(mcol_mm, 1)

            def spectrum(c, bank, cos_of, sin_of, part):
                w = raw(c, NT, 2, P)
                trig, odd = part // 2, part % 2
                if part == 0:
                    arrived(pe, c)
                for i in range(4):
                    nt = 4 * odd + i
                    ins = mm(PS[:, bank + trig, 256 * odd:256 * odd + 256], w[:, nt, trig],
                             (sin_of if trig else cos_of)[:, nt], i == 0, i == 3)
                if part == 3:
                    ins.then_inc(spec_mm, 1)

            def turn_x(src, tiles, bank, f):
                for i, t in enumerate(tiles):
                    ins = pe.transpose(PS[:, bank, i * P:i * P + P], src[:, t, f * P:f * P + P], ident)
                ins.then_inc(hT_mm, 1)

            for step in range(16):
                for n in (2 * step, 2 * step + 1):
                    if n >= 20:
                        continue
                    if n % 8 == 0:
                        pe.wait_ge(xn_rdy, (4, 8, 10)[n // 8])
                    if n >= 4:
                        pe.wait_ge(hT_f, n - 3)
                    if n < 16:
                        turn_x(xs, range(4 * (n // KD), 4 * (n // KD) + 4), n % 4, n % KD)
                    else:
                        for i in range(4):
                            f, t = 2 * (n - 16) + i // 2, NT + i % 2
                            ins = pe.transpose(PS[:, n % 4, i * P:i * P + P], xs[:, t, f * P:f * P + P], ident)
                        ins.then_inc(hT_mm, 1)
                kt = step // 4
                if step == 0:
                    pe.wait_ge(mod_rdy, 1)
                    pe.wait_ge(taps_rdy, NT)
                if kt >= 2 and step % 4 == 0:
                    pe.wait_ge(spec_rdy, kt - 1)
                spectrum(chunk_index("ff", kt), 4 + 2 * (kt % 2), filt_a, filt_b, step % 4)

            def late_columns(g, bank):
                pe.wait_ge(late_used, 8 * g + 8)
                for i in range(8):
                    ins = mm(PS[:, bank, 8 * (g % 2) + i:8 * (g % 2) + i + 1], macc[:, g % 2, i * P:i * P + P], ones1,
                             True, True)
                ins.then_inc(late_mm, 1)

            pe.wait_ge(hT_rdy, 16)
            for i in range(3):
                slot = i % 2
                w = spl(slot, KD, 256)
                pe.wait_ge(split_lo, i + 1)
                for b in range(2):
                    ct = 2 * i + b
                    if ct >= 2:
                        pe.wait_ge(hy_rdy, ct - 1)
                    else:
                        pe.wait_ge(hT_f, 18 + 2 * ct)
                    for k in range(KD):
                        for part, others in ((0, (0, 1)), (1, (0,))):
                            for o in others:
                                for half in range(2):
                                    ins = mm(PS[:, 2 * b + half, :], w[:, part, k, b * P:b * P + P],
                                             hT[:, o, k, half * 512:half * 512 + 512],
                                             k == 0 and part + o == 0, k == KD - 1 and part == 1)
                    ins.then_inc(hy_mm, 1)
                if i:
                    if i == 1:
                        pe.wait_ge(spec_rdy, 4)
                    late_columns(i - 1, 6)

            pe.wait_ge(hy_rdy, 4)
            for q in range(4):
                if q >= 2:
                    pe.wait_ge(vt_rdy, q - 1)
                for i in range(2):
                    nt = 2 * q + i
                    o = nt * 256 if nt < 4 else (nt - 4) * 256 + 1
                    for c2 in range(2):
                        ins = pe.transpose(PS[:, 4 + q % 2, 256 * i + P * c2:256 * i + P * c2 + P],
                                           uvT[:, c2, o:o + 255:2], ident)
                ins.then_inc(vt_mm, 1)
            pe.wait_ge(vt_rdy, 4)
            pe.wait_ge(hy_rdy, 6)
            pe.wait_ge(late_rdy, 1)

            def inverse(c, kt):
                w = raw(c, 2, S)
                arrived(pe, c)
                pe.wait_ge(G_rdy, kt + 1)
                for trig in range(2):
                    for odd in range(2):
                        for c2 in range(2):
                            ins = mm(PS[:, 4 + 2 * c2 + odd, :], G[:, kt % 2, 2 * odd + trig, c2 * P:c2 * P + P],
                                     w[:, trig, 512 * odd:512 * odd + 512], kt == 0 and trig == 0,
                                     kt == 3 and trig == 1)
                ins.then_inc(inv_mm, 1)

            for kt in range(5):
                if kt < 4:
                    if kt >= 2:
                        pe.wait_ge(spec_rdy, 4 + kt - 1)
                    for part in range(4):
                        spectrum(chunk_index("fwd", kt), 2 * (kt % 2), vtok, vtok, part)
                else:
                    pe.wait_ge(spec_rdy, 8)
                    late_columns(2, 3)
                    late_columns(3, 3)
                if kt:
                    inverse(chunk_index("inv", kt - 1), kt - 1)

            def project(u, par, g, t, is_ctx, it=None):
                more = 0 if it is None else it * 2
                if u >= 2:
                    if UNITS[u - 2][0] != 0:
                        pe.wait_ge(pr_vl, more + n_valued(u - 2))
                    if UNITS[u - 2][0] != 2:
                        pe.wait_ge(pr_n, more + n_normed(u - 2))
                pair = 0 if g == 0 else 2
                width = 256 if (is_ctx and g == 1) else 512
                for k in range(KD):
                    w = spl(pair + k // 4, 4, 512)
                    src = hcT if is_ctx else hT
                    for part, others in ((0, (0, 1)), (1, (0,))):
                        for o in others:
                            ins = mm(PS[:, par, 0:width], src[:, part, k, tok(t)], w[:, o, k % 4, 0:width],
                                     k == 0 and part + o == 0, k == KD - 1 and part == 1)
                ins.then_inc(pr_mm, 1)

            def turn_qk(u, par, n, it=None):
                more = 0 if it is None else it * 2
                pe.wait_ge(pr_lo, more + u + 1)
                if u >= 2:
                    pe.wait_ge(pr_tc, more + u - 1)
                out16 = PS[:, 2 + par, :].bitcast(F16)
                for j in range(n):
                    ins = pe.transpose(out16[:, j * P:j * P + P], stk[par][:, j * P:j * P + P], ident16)
                ins.then_inc(pr_tm, 1)

            pe.wait_ge(id16_rdy, 1)
            for gi, g in enumerate(GROUPS):
                u0 = GROUP0[g]
                pe.wait_ge(split_lo, 3 + 2 * gi + 2)
                for b in range(2):
                    project(u0 + b, b, g, b, False)
                    if gi:
                        turn_qk(u0 + b - 2, b, 4 if g == 0 else 8)
                with pe.Fori(0, 3) as it:
                    for b in range(2):
                        project(u0 + 2 + b, b, g, it * 2 + 2 + b, False, it)
                        turn_qk(u0 + b, b, 8, it)
                if g:
                    for b in range(2):
                        project(u0 + 8 + b, b, g, b, True)
                        turn_qk(u0 + 6 + b, b, 8)
            for b in range(2):
                turn_qk(NU - 2 + b, b, 8)

            def copied(u, bank):
                if bank < len(u.banks):
                    pe.wait_ge(pt_lo, u.turned(bank))

            def scores(u):
                if u.na:
                    q, k = nqT[:, u.blk, u.j * P:u.j * P + P], nkT[:, u.blk]
                    k0 = window(u.j) * P
                    pieces = ((512, 128, k0 + 512), (640, 256, S), (0, 512, k0))
                else:
                    q, k = qT[:, u.j, tok(u.blk)], kT[:, u.kv]
                    pieces = ((1024, 256, 1024), (0, 512, 0), (512, 512, 512))
                for o, w, s0 in pieces:
                    if u.v >= 2 and o == 0:
                        copied(u.ahead(-2), 0)
                    elif u.v >= 2 and o == (1024 if u.ahead(-2).na else 512):
                        copied(u.ahead(-2), 1)
                    for part in range(2):
                        ins = mm(PSf[:, 1536 * u.par + o:1536 * u.par + o + w], q, k[:, part, s0:s0 + w],
                                 part == 0, part == 1)
                ins.then_inc(s_mm, 1)

            def turn_p(u):
                pe.wait_ge(s_exp, u.n + 1)
                for b, bank in enumerate(u.banks):
                    if u.na and b == 1 and u.v >= 2:
                        copied(u.ahead(-2), 1)
                    if b == 2:
                        pe.wait_ge(o_rdy, u.n - 1)
                    for i in bank:
                        o = u.turned_at(b) + (i - bank.start) * P
                        ins = pe.transpose(PSf[:, o:o + P], Pb[:, u.par, i], ident)
                    ins.then_inc(pt_mm, 1)

            def weigh(u):
                if u.v >= 2:
                    pe.wait_ge(o_rdy, u.n - 1)
                tiles = [window(u.j) + i for i in range(5)] + [NT, NT + 1] if u.na else range(10)
                for i, kt in enumerate(tiles):
                    if i == 0 and not u.na:
                        copied(u, 2)
                    elif i % 4 == 0 and u.na:
                        copied(u, i // 4)
                    first, last = i == 0, i == len(tiles) - 1
                    if u.na:
                        for part, vp in ((0, 0), (1, 0), (0, 1)):
                            ins = mm(PS[:, 6 + u.par, 0:HD], PT[:, u.par, part, i], V[:, kt, HKV + u.blk, vp],
                                     first and part + vp == 0, last and vp == 1)
                    else:
                        for part in range(2):
                            ins = mm(PS[:, 6 + u.par, 0:2 * HD], PT[:, u.par, part, i],
                                     V[:, kt, u.kv].rearrange("p a d -> p (a d)"), first and part == 0,
                                     last and part == 1)
                ins.then_inc(o_mm, 1)

            def attend(u):
                if u.v < NV - 1:
                    scores(u.ahead(1))
                turn_p(u)
                if u.v:
                    weigh(u.ahead(-1))

            pe.wait_ge(pr_tc, NU)
            scores(Unit(0))
            for v in range(3):
                attend(Unit(v))
            with pe.Fori(0, HN - 1) as it:
                for v in range(3, 11):
                    attend(Unit(v, it))
            for v in range(27, 33):
                attend(Unit(v))
            with pe.Fori(0, NT - 1) as it:
                for v in range(33, 41):
                    attend(Unit(v, it))
            for v in range(89, NV):
                attend(Unit(v))
            weigh(Unit(NV - 1))

            def turn_mix(t):
                pe.wait_ge(oab_sum, t + 1)
                if t >= 2:
                    pe.wait_ge(mx_lo, t - 1)
                for f in range(6):
                    ins = pe.transpose(PS[:, 4 + 2 * (t % 2) + f // 4, (f % 4) * P:(f % 4) * P + P],
                                       mixtok[:, t, f * P:f * P + P], ident)
                ins.then_inc(mx_mm, 1)

            def project_out(t, b, between={}):
                for k in range(KD):
                    for part, others in ((0, (0, 1)), (1, (0,))):
                        lhs = yT[:, part, k, tok(t)] if k < 2 else mixT[:, part, k - 2, tok(t)]
                        for o in others:
                            for half in range(2):
                                ins = mm(PS[:, 2 * b + half, :], lhs, woS[2 * (k // 4) + half][:, o, k % 4, :],
                                         k == 0 and part + o == 0, k == KD - 1 and part == 1)
                    if k == KD - 1:
                        ins.then_inc(wo_mm, 1)
                    if k in between:
                        between[k]()

            pe.wait_ge(o_rdy, NV)
            turn_mix(0)
            turn_mix(1)
            pe.wait_ge(wo_split, 4)
            pe.wait_ge(y_rdy, 4)
            pe.wait_ge(mx_lo, 1)
            project_out(0, 0, {3: lambda: turn_mix(2), 6: lambda: turn_mix(3)})
            pe.wait_ge(mx_lo, 2)
            project_out(1, 1, {k: (lambda t=t: turn_mix(t)) for k, t in ((0, 4), (1, 5), (3, 6), (5, 7))})
            pe.wait_ge(mx_lo, NT)
            with pe.Fori(0, 2) as it:
                for b in range(2):
                    pe.wait_ge(x1_rdy, it * 2 + b + 1)
                    project_out(it * 2 + 2 + b, b)

            def turn_x1(n):
                if n % KD == 0:
                    pe.wait_ge(xn1_rdy, (1, len(X1_PARTS))[n // KD])
                if n >= 4:
                    pe.wait_ge(hT_f, 20 + n - 3)
                turn_x(xn1, range(4), 4 + n % 4, n % KD)

            pe.wait_ge(x1_rdy, 5)
            project_out(6, 0, {6: lambda: turn_x1(0), 7: lambda: [turn_x1(n) for n in (1, 2, 3)]})
            pe.wait_ge(x1_rdy, 6)
            project_out(7, 1, {k: (lambda n=n: turn_x1(n)) for k, n in ((2, 4), (3, 5), (4, 6), (5, 7))})

            def hidden(b, halves=(0, 1), before=None):
                w = fiS[b]
                for gu in range(2):
                    for k in range(KD):
                        if before:
                            before(gu, k)
                        for part, others in ((0, (0, 1)), (1, (0,))):
                            for o in others:
                                for half in halves:
                                    ins = mm(PS[:, 4 * b + 2 * gu + half, :], w[:, part, k, gu * P:gu * P + P],
                                             hT[:, o, k, half * 512:half * 512 + 512],
                                             k == 0 and part + o == 0, k == KD - 1 and part == 1)
                if 1 in halves:
                    ins.then_inc(fi_mm, 1)

            def beside_second_half(gu, k):
                if k == 0:
                    pe.wait_ge(x1_rdy, NT - 1 + gu)
                if gu == 0:
                    pe.wait_ge(hT_rdy, 20 + k + 1)
                else:
                    turn_x1(8 + k)

            base = n_split(chunk_index("fi", 0))
            pe.wait_ge(split_lo, base + 1)
            hidden(0, (0,), beside_second_half)
            pe.wait_ge(hT_f, 36)
            hidden(1, (0,))
            hidden(0, (1,), lambda gu, k: pe.wait_ge(hT_rdy, 28 + k + 1) if gu == 0 else None)
            hidden(1, (1,))
            with pe.Fori(0, KF // 2 - 1) as it:
                for b in range(2):
                    pe.wait_ge(split_lo, it * 2 + base + 2 + b)
                    pe.wait_ge(fi_p, it * 2 + b + 1)
                    hidden(b)

            def down(k0, s, grp, start, stop):
                for t in range(4):
                    if start and grp:
                        pe.wait_ge(fo_x, t + 1)
                    elif start and t == 2:
                        pe.wait_ge(fi_p, KF)
                    for kk in range(2):
                        for part, others in ((0, (0, 1)), (1, (0,))):
                            for o in others:
                                for half in range(2):
                                    ins = mm(PS[:, 2 * t + half, :], prodT[:, part, k0 + kk, tok(4 * grp + t)],
                                             foS[s][:, o, kk, half * 512:half * 512 + 512],
                                             start and kk == 0 and part + o == 0, stop and kk == 1 and part == 1)
                    if stop:
                        ins.then_inc(fo_mm, 1)
                if not stop:
                    ins.then_inc(fo_used, 1)

            pe.wait_ge(fi_lo, KF - 1)
            base = n_split(chunk_index("fo", 0))
            for grp in range(2):
                n0 = base + 11 * grp
                pe.wait_ge(split_lo, n0)
                down(0, grp % 2, grp, True, False)
                with pe.Fori(0, 4) as it:
                    for b in range(2):
                        pe.wait_ge(split_lo, it * 2 + n0 + 1 + b)
                        down(it * 4 + 2 + 2 * b, (grp + 1 + b) % 2, grp, False, False)
                pe.wait_ge(fi_lo, KF)
                for b in range(2):
                    pe.wait_ge(split_lo, n0 + 9 + b)
                    down(18 + 2 * b, (grp + 1 + b) % 2, grp, False, b == 1)

        @block.scalar
        def _(act):
            for dst, src in small:
                act.dma_start(dst, src).then_inc(small_in, 16)

            def hi_of(c, dst):
                arrived(act, c)
                n = int(np.prod(dst.shape[2:]))
                src = f32(RAW(chunk_slot(c)), n)
                act.activation(flat(dst[:, 0]), src, ACT.Copy, scale=WS).then_inc(split_hi, 1)

            act.wait_ge(cols_rdy, 1)
            act.activation(silu_c.rearrange("p k n -> p n k"),
                           cols[:, V_C:V_C + 16].rearrange("p (n k) -> p n k", n=2), ACT.Silu).then_inc(silu_rdy, 1)
            for layer in range(3):
                act.wait_ge(mlp_arg, layer + 1)
                act.activation(fh, fu, ACT.Sin).then_inc(mlp_h, 1)
            for t in range(10):
                if t == 8:
                    act.wait_ge(mod_used, 4)
                    act.copy(mrow[0:2, 0], PSf[0:2, 0:GW]).then_inc(mrow_rdy, 1)
                act.wait_ge(x_in[t // 4], 16)
                act.activation(f32(68 + 4 * t, D), xs[:, t], ACT.Square, accum_out=ss[:, t:t + 1]).then_inc(sq_done, 1)
            act.wait_ge(mod_used, 8)
            act.copy(mrow[0:2, 1], PSf[0:2, GW:2 * GW]).then_inc(mrow_rdy, 1)

            def even_filter(kt):
                act.wait_ge(spec_mm, kt + 1)
                if kt >= 2:
                    act.wait_ge(spec_rdy, kt - 1)
                b = 4 + 2 * (kt % 2)
                act.activation(tE0[:, kt % 2], PS[:, b:b + 2, 0:256], ACT.Copy, scale=1.0 / 1024).then_inc(even_part, 1)

            act.wait_ge(mod_rdy, 1)
            for n in range(20):
                act.wait_ge(hT_mm, n + 1)
                if n >= 2:
                    act.wait_ge(hT_rdy, n - 1)
                if n < 16:
                    f = n % KD
                    act.activation(htmp[:, n % 2], PS[:, n % 4], ACT.Identity, scale=am[:, f, 0:1],
                                   bias=mod[:, f, 0:1]).then_inc(hT_f, 1)
                else:
                    for i in range(2):
                        f = 2 * (n - 16) + i
                        ins = act.activation(htmp[:, n % 2, 256 * i:256 * i + 256], PS[:, n % 4, 256 * i:256 * i + 256],
                                             ACT.Identity, scale=am[:, f, 1:2], bias=mod[:, f, 1:2])
                    ins.then_inc(hT_f, 1)
                if n % 8 == 7:
                    even_filter(n // 8)
                if n == 15:
                    hi_of(chunk_index("hy", 0), spl(0, KD, 256))
            even_filter(2)
            even_filter(3)
            hi_of(chunk_index("hy", 1), spl(1, KD, 256))
            for ct in range(6):
                act.wait_ge(hy_mm, ct + 1)
                if ct == 2:
                    act.wait_ge(hT_rdy, 20)
                dst = (uvT, accx, x2T)[ct // 2][:, ct % 2]
                act.activation(dst, PSf[:, 1024 * (ct % 2):1024 * (ct % 2) + 1024], ACT.Identity,
                               scale=cwb[:, 6 + ct:7 + ct], bias=cols[:, V_CB + ct:V_CB + ct + 1]).then_inc(hy_mid, 1)
                if ct == 1:
                    hi_of(chunk_index("hy", 2), spl(0, KD, 256))
            for q in range(4):
                act.wait_ge(vt_mm, q + 1)
                act.copy(flat(vtok[:, 2 * q:2 * q + 2]), PS[:, 4 + q % 2]).then_inc(vt_rdy, 1)
            for kt in range(4):
                act.wait_ge(spec_mm, 4 + kt + 1)
                if kt >= 2:
                    act.wait_ge(spec_rdy, 4 + kt - 1)
                act.copy(tE[:, kt % 2], PS[:, 2 * (kt % 2):2 * (kt % 2) + 2, 0:256]).then_inc(even_part, 1)
            for i in range(2):
                hi_of(chunk_index("qkv", i), spl(2 + i, 4, 512))
            for n in range(4):
                c2, odd = n // 2, n % 2
                act.wait_ge(y_f, n + 1)
                act.copy(yT[:, 0, c2, odd::2], yo[:, n % 2]).then_inc(y_hi, 1)

            def from_psum(u, it=0):
                (g, t), par, m = UNITS[u], u % 2, it * 2
                act.wait_ge(pr_mm, m + u + 1)
                if u >= 2:
                    act.wait_ge(pr_lo, m + u - 1)
                    if UNITS[u - 2][0] != 2:
                        act.wait_ge(pr_r, m + n_normed(u - 2))
                ps, tt = PS[:, par], t + m
                if g == 0:
                    act.activation(bT[par], ps, ACT.Square).then_inc(pr_sq, 1)
                elif g == 1:
                    act.activation(bT[par][:, 0:128], ps[:, 0:128], ACT.Square).then_inc(pr_sq, 1)
                    if t < NT:
                        act.activation(nT[par][:, 128:384], ps[:, 256:512], ACT.Copy, scale=0.125 / WS)
                    act.activation(V[:, tt, 0:2, 0], ps[:, 128:256].rearrange("p (h d) -> p h d", h=2), ACT.Copy,
                                   scale=VS / WS).then_inc(pr_v, 1)
                else:
                    act.activation(nT[par][:, 0:256], ps[:, 0:256], ACT.Copy, scale=1 / WS)
                    act.activation(V[:, tt, 2:6, 0], ps[:, 256:512].rearrange("p (h d) -> p h d", h=4), ACT.Copy,
                                   scale=VS / WS).then_inc(pr_v, 1)

            def hi_parts(u, it=0):
                (g, t), par, m = UNITS[u], u % 2, it * 2
                if g != 2:
                    act.wait_ge(pr_r, m + n_normed(u))
                if g != 0:
                    act.wait_ge(pr_v, m + n_valued(u))
                if u >= 2:
                    act.wait_ge(pr_tm, m + u - 1)
                for out, _, src in stacks(g, t, par):
                    ins = act.copy(out, src)
                ins.then_inc(pr_hi, 1)

            def turned(u, it=0):
                (g, t), par, m = UNITS[u], u % 2, it * 2
                act.wait_ge(pr_tm, m + u + 1)
                ps = PS[:, 2 + par, :].bitcast(F16).rearrange("p (j t) -> p j t", t=P)
                if g == 0:
                    ins = act.copy(qT[:, :, tok(t + m)], ps)
                elif g == 2:
                    ins = act.copy(nkT.rearrange("p h a s -> p (h a) s")[:, :, tok(t + m)], ps)
                else:
                    ins = act.copy(kT.rearrange("p h a s -> p (h a) s")[:, :, tok(t + m)], ps[:, 0:4])
                    if t < NT:
                        ins = act.copy(nqT[:, :, tok(t + m)], ps[:, 4:8])
                ins.then_inc(pr_tc, 1)

            def slot(u, it=0):
                if u < NU:
                    from_psum(u, it)
                if 1 <= u <= NU:
                    hi_parts(u - 1, it)
                if u >= 2:
                    turned(u - 2, it)

            for g in GROUPS:
                u0 = GROUP0[g]
                slot(u0)
                for b in range(2):
                    if b:
                        slot(u0 + 1)
                    if g == 1:
                        hi_of(chunk_index("qkv", 2 + b), spl(b, 4, 512))
                    elif g == 0:
                        hi_of(chunk_index("qkv", 4 + b), spl(2 + b, 4, 512))
                with act.Fori(0, 3) as it:
                    for b in range(2):
                        slot(u0 + 2 + b, it)
                if g:
                    slot(u0 + 8)
                    slot(u0 + 9)
                if g == 1:
                    act.wait_ge(skew_set, 1)
                    for h in range(HN):
                        act.dma_start(skrow[19 * h + 2:19 * h + 17, 48:79], io["na_rpb"][0, h])\
                            .then_inc(skew_rows, 16)
                    act.wait_ge(skew_rows, 16 * HN)
                    act.dma_start(skew.ap().rearrange("h r c x -> (h r) c x"),
                                  skrow[0:19 * HN].unsqueeze(1).broadcast_to((19 * HN, 64, P))).then_inc(skew_out, 16)
            slot(NU)
            slot(NU + 1)

            def exponentials(u):
                if u.na:
                    act.wait_ge(bias_add, u.n + 1)
                    act.activation(nmax[:, u.par:u.par + 1], cmax[:, u.par:u.par + 1], ACT.Copy, scale=-1.0)\
                        .then_inc(s_neg, 1)
                    act.wait_ge(s_neg, u.n + 1)
                else:
                    act.wait_ge(s_max, u.n_gqa + 1)
                w = 7 if u.na else 10
                act.activation(flat(Pb[:, u.par, 0:w]), PSf[:, 1536 * u.par:1536 * u.par + w * P], ACT.Exp,
                               bias=nmax[:, u.par:u.par + 1], accum_out=esum[:, u.v % 4:u.v % 4 + 1]).then_inc(s_exp, 1)

            def copy_p(u):
                if u.v >= 2:
                    act.wait_ge(o_mm, u.n - 1)
                for b, t in enumerate(u.banks):
                    act.wait_ge(pt_mm, u.turned(b))
                    o = u.turned_at(b)
                    act.activation(flat(PT[:, u.par, 0, t.start:t.stop]), PSf[:, o:o + len(t) * P],
                                   ACT.Copy, scale=PSC).then_inc(pt_hi, 1)

            def scaled(u):
                act.wait_ge(rcp_rdy, u.n + 1)
                act.wait_ge(o_mm, u.n + 1)
                if u.na:
                    w, dst = HD, mixtok[:, u.j, bass.ds(u.blk * HD + HQ * HD, HD)]
                else:
                    w, dst = 2 * HD, oab[:, u.blk, u.j].rearrange("p a d -> p (a d)")
                act.activation(dst, PS[:, 6 + u.par, 0:w], ACT.Copy, scale=rcp[:, u.par:u.par + 1]).then_inc(o_rdy, 1)

            def attend(u):
                copy_p(u)
                if u.v < NV - 1:
                    exponentials(u.ahead(1))
                if u.v:
                    scaled(u.ahead(-1))

            act.activation(warm, neghalf[:, 0:1], ACT.Exp)
            act.wait_ge(pr_mm, NU)
            exponentials(Unit(0))
            for v in range(3):
                attend(Unit(v))
            with act.Fori(0, HN - 1) as it:
                for v in range(3, 11):
                    attend(Unit(v, it))
            for v in range(27, 33):
                attend(Unit(v))
            with act.Fori(0, NT - 1) as it:
                for v in range(33, 41):
                    attend(Unit(v, it))
            for v in range(89, NV):
                attend(Unit(v))
            scaled(Unit(NV - 1))

            for t in range(NT):
                act.wait_ge(mx_mm, t + 1)
                o = 2048 + 1024 * (t % 2)
                act.activation(mixT[:, 0, :, t * P:t * P + P], PSf[:, o:o + 768].rearrange("p (f t) -> p f t", f=6),
                               ACT.Copy, scale=1 / (PSC * VS)).then_inc(mx_hi, 1)
            act.wait_ge(bias_add, NNA)
            for b in range(2):
                hi_of(chunk_index("fi", b), fiS[b])
            def x1_square(t):
                act.wait_ge(x1_sum, t + 1)
                if t:
                    act.wait_ge(sq1, t)
                act.activation(f32(104, D), x1[:, t], ACT.Square, accum_out=ss[:, t:t + 1]).then_inc(sq1, 1)

            def modulate1(n):
                act.wait_ge(hT_mm, 20 + n + 1)
                if n >= 2:
                    act.wait_ge(hT_rdy, 20 + n - 1)
                f = n % KD
                act.activation(h2tmp[:, n % 2], PS[:, 4 + n % 4], ACT.Identity, scale=af[:, f, 0:1],
                               bias=mod[:, 24 + f, 0:1]).then_inc(hT_f, 1)

            for t in range(NT):
                x1_square(t)
                if t in (5, 6):
                    for n in range(4 * (t - 5), 4 * (t - 5) + 4):
                        modulate1(n)
            for n in range(8, 16):
                modulate1(n)

            def silu(b, j, first=False):
                act.wait_ge(fi_mm, j + 1)
                if not first:
                    act.wait_ge(fi_p, j)
                act.activation(sg, PSf[:, 2048 * b:2048 * b + 1024], ACT.Silu, scale=1 / WS).then_inc(fi_s, 1)

            def gated_hi(j):
                act.wait_ge(fi_p, j + 1)
                act.copy(prodT[:, 0, j, :], pr).then_inc(fi_hi, 1)

            act.wait_ge(hT_rdy, 36)
            c0 = chunk_index("fi", 0)
            for b in range(2):
                silu(b, b, b == 0)
                hi_of(c0 + 2 + b, fiS[b])
                gated_hi(b)
            with act.Fori(0, KF // 2 - 2) as it:
                for b in range(2):
                    silu(b, it * 2 + 2 + b)
                    act.wait_ge(raw_in[b], it * 32 + 16 * chunk_arrivals(c0 + 4 + b))
                    act.activation(flat(fiS[b][:, 0]), f32(RAW(b), 2048), ACT.Copy, scale=WS).then_inc(split_hi, 1)
                    gated_hi(it * 2 + 2 + b)
            for b in range(2):
                silu(b, KF - 2 + b)
                act.wait_ge(fo_gated, b + 1)
                hi_of(chunk_index("fo", b), foS[b])
                gated_hi(KF - 2 + b)
            act.wait_ge(fi_mm, KF)
            act.dma_start(gfin, io["g_final"].partition_broadcast(P)).then_inc(gf_in, 16)

            c1 = chunk_index("fo", 0)

            def fo_hi(s, base_c, it=0):
                act.wait_ge(fo_gated, it + base_c - c1 + 1)
                act.activation(flat(foS[s][:, 0]), f32(RAW(s), 2048), ACT.Copy, scale=WS).then_inc(split_hi, 1)

            def x2_square(t):
                act.wait_ge(fo_x, t + 1)
                if t:
                    act.wait_ge(fo_sq, t)
                act.activation(osq, x1[:, t], ACT.Square, accum_out=ss[:, t:t + 1]).then_inc(fo_sq, 1)

            with act.Fori(0, 4) as it:
                for b in range(2):
                    act.wait_ge(fo_used, it * 2 + b + 1)
                    fo_hi(b, c1 + 2 + b, it * 2)
            for m in (10, 11):
                act.wait_ge(fo_used, m - 1)
                fo_hi(m % 2, c1 + m)
            act.wait_ge(fo_mm, 4)
            fo_hi(0, c1 + 12)
            for t in range(4):
                x2_square(t)
            with act.Fori(0, 4) as it:
                for b in range(2):
                    act.wait_ge(fo_used, it * 2 + b + 11)
                    fo_hi(1 - b, c1 + 13 + b, it * 2)
            act.wait_ge(fo_used, 19)
            fo_hi(1, c1 + 21)
            for t in range(4, NT):
                x2_square(t)

        @block.vector
        def _(dve):
            own = Chain(dve, dve_own)

            def lo_of(c, dst):
                n = int(np.prod(dst.shape[2:]))
                dve.wait_ge(split_hi, n_split(c))
                dve.scalar_tensor_tensor(flat(dst[:, 1]), f32(RAW(chunk_slot(c)), n), WS, flat(dst[:, 0]),
                                         ALU.mult, ALU.subtract).then_inc(split_lo, 1)

            dve.wait_ge(cols_mm, 1)
            dve.tensor_copy(cols[:, 0:N_ROWS], PS[:, 5, 0:N_ROWS]).then_inc(cols_rdy, 1)
            dve.tensor_copy(ident16, ident).then_inc(id16_rdy, 1)
            dve.wait_ge(cols_rdy, 1)
            own.step(dve.tensor_scalar(cwb, cols[:, V_CW:V_CW + 18], 1 / WS, None, ALU.mult))
            u, k = fu, fk
            for layer in range(3):
                dve.wait_ge(mlp_mm, layer + 1)
                own.step(dve.tensor_scalar(u, PS[:, 4], fvec[:, layer:layer + 1], fvec[:, 3:4],
                                           ALU.add, ALU.mult))
                own.wait()
                own.step(dve.tensor_scalar(k, u, 1 / (2 * math.pi), MAGIC, ALU.mult, ALU.add))
                own.wait()
                own.step(dve.tensor_scalar(k, k, MAGIC, None, ALU.subtract))
                own.wait()
                for part in (TWO_PI_1, TWO_PI_2, TWO_PI_3):
                    own.step(dve.scalar_tensor_tensor(u, k, -part, u, ALU.mult, ALU.add))
                    own.wait()
                dve.tensor_scalar(u, u, PI_IN, -PI_IN, ALU.min, ALU.max).then_inc(mlp_arg, 1)
            dve.wait_ge(rest_in, N_REST)
            own.step(dve.tensor_scalar(gkc, gq[:, 1], 1 / WS, None, ALU.mult))
            def mean_x(ta, tb):
                dve.wait_ge(sq_done, tb)
                dve.tensor_scalar(ss[:, ta:tb], ss[:, ta:tb], 1.0 / D, EPS, ALU.mult, ALU.add).then_inc(ms_rdy, 1)

            def normalise_x(i, ta, tb):
                dve.wait_ge(rs_rdy, i + 1)
                for t in range(ta, tb):
                    dve.tensor_scalar(xs[:, t], xs[:, t], rs[:, t:t + 1], None, ALU.mult).then_inc(xn_rdy, 1)

            for nt in range(NT):
                dve.wait_ge(taps_mm, nt + 1)
                own.step(dve.tensor_tensor(flat(fbd[:, nt % 2]), PS[:, 6 + nt % 2], decay[:, nt], ALU.mult))
                own.wait()
                own.step(dve.tensor_tensor(filt_a[:, nt], fbd[:, nt % 2, 0], fbd[:, nt % 2, 1], ALU.add))
                dve.tensor_tensor(filt_b[:, nt], fbd[:, nt % 2, 0], fbd[:, nt % 2, 1], ALU.subtract)\
                    .then_inc(taps_rdy, 1)
                if nt == 4:
                    mean_x(0, 4)
                if nt == 5:
                    normalise_x(0, 0, 4)
            mean_x(4, 8)
            mean_x(8, 10)

            def filter_spectrum(kt):
                par = kt % 2
                dve.wait_ge(even_part, kt + 1)
                oc, os = PS[:, 4 + 2 * par, 256:512], PS[:, 5 + 2 * par, 256:512]
                ec, es = tE0[:, par, 0], tE0[:, par, 1]
                a = 1.0 / 1024
                dve.scalar_tensor_tensor(Fc[:, kt, 0:256], oc, a, ec, ALU.mult, ALU.add)
                dve.scalar_tensor_tensor(Fc[:, kt, 256:512], oc, -a, ec, ALU.mult, ALU.add)
                dve.scalar_tensor_tensor(Fs[:, kt, 0:256], os, a, es, ALU.mult, ALU.add)
                dve.scalar_tensor_tensor(Fs[:, kt, 256:512], os, a, es, ALU.mult, ALU.subtract).then_inc(spec_rdy, 1)

            def modulation_gain(a, scale0, gain0, n):
                dve.scalar_tensor_tensor(a[:, :, 0:n], mod[:, scale0:scale0 + 8, 0:n], 1.0,
                                         cols[:, gain0:gain0 + 8].unsqueeze(2).broadcast_to((P, 8, n)),
                                         ALU.add, ALU.mult).then_inc(mod_rdy, 1)

            dve.wait_ge(mcol_mm, 1)
            own.step(dve.tensor_tensor(mod[:, 0:16], PS[:, 5, 0:32].rearrange("p (t n) -> p t n", n=2),
                                       cols[:, V_BMOD:V_BMOD + 16].unsqueeze(2).broadcast_to((P, 16, 2)), ALU.add))
            own.wait()
            modulation_gain(am, 8, V_GMIX, 2)
            normalise_x(1, 4, 8)
            normalise_x(2, 8, 10)

            def split_h(n, f, hi, lo):
                dve.wait_ge(hT_f, n + 1)
                own.step(dve.tensor_copy(hi, f))
                own.wait()
                dve.tensor_tensor(lo, f, hi, ALU.subtract).then_inc(hT_rdy, 1)

            for n in range(20):
                if n < 16:
                    f, o = n % KD, 512 * (n // KD)
                    split_h(n, htmp[:, n % 2], hT[:, 0, f, o:o + 512], hT[:, 1, f, o:o + 512])
                else:
                    f = 2 * (n - 16)
                    split_h(n, htmp[:, n % 2].rearrange("p (f t) -> p f t", f=2),
                            hcT[:, 0, f:f + 2], hcT[:, 1, f:f + 2])
                if n % 8 == 7:
                    filter_spectrum(n // 8)
                if n == 15:
                    lo_of(chunk_index("hy", 0), spl(0, KD, 256))
            filter_spectrum(2)
            filter_spectrum(3)
            lo_of(chunk_index("hy", 1), spl(1, KD, 256))

            def late(n):
                c = chunk_index("late", n)
                w, g, kp = raw(c, 2, GW), n // 4, n % 4
                acc = macc[:, g % 2]
                arrived(dve, c)
                if kp == 0 and g >= 2:
                    dve.wait_ge(late_mm, g - 1)
                for i in range(2):
                    s = silu_c[:, 2 * kp + i, 0:1]
                    if kp + i:
                        dve.wait_ge(late_used, 2 * n + i)
                        ins = dve.scalar_tensor_tensor(acc, w[:, i], s, acc, ALU.mult, ALU.add)
                    else:
                        ins = dve.tensor_scalar(acc, w[:, i], s, None, ALU.mult)
                    ins.then_inc(late_used, 1)

            for ct in range(6):
                dst = (uvT, accx, x2T)[ct // 2][:, ct % 2]
                ps = PSf[:, 1024 * (ct % 2):1024 * (ct % 2) + 1024]
                dve.wait_ge(hy_mid, ct + 1)
                own.step(dve.scalar_tensor_tensor(dst[:, 1:S], ps[:, 0:S - 1], cwb[:, ct:ct + 1], dst[:, 1:S],
                                                  ALU.mult, ALU.add))
                own.wait()
                ins = dve.scalar_tensor_tensor(dst[:, 0:S - 1], ps[:, 1:S], cwb[:, 12 + ct:13 + ct], dst[:, 0:S - 1],
                                               ALU.mult, ALU.add)
                if ct // 2 == 1:
                    own.step(ins)
                    own.wait()
                    ins = dve.tensor_tensor(uvT[:, ct % 2], uvT[:, ct % 2], dst, ALU.mult)
                ins.then_inc(hy_rdy, 1)
                if ct == 1:
                    lo_of(chunk_index("hy", 2), spl(0, KD, 256))
                if ct == 5:
                    dve.wait_ge(late_mm, 2)
                    dve.tensor_tensor(mod[:, 16:32, 0], PS[:, 6, 0:16], cols[:, V_BMOD + 16:V_BMOD + 32], ALU.add)\
                        .then_inc(late_rdy, 1)
                late(2 * ct)
                late(2 * ct + 1)
                if ct == 4:
                    dve.wait_ge(gn_in, 32)
                    for n, tab in enumerate((gc, gk)):
                        s = (0.125 / WS, 1 / WS)[n]
                        for o, w, g0 in ((0, 64, 0), (64, 32, 32), (96, 32, 0)):
                            v = tab.rearrange("p t a d -> p t (a d)")[:, :, o:o + w]
                            gain = gq[:, n, g0:g0 + w].unsqueeze(1).broadcast_to((P, NT, w))
                            own.step(dve.scalar_tensor_tensor(v, v, s, gain, ALU.mult, ALU.mult))
                    own.wait()
            for kt in range(4):
                par = kt % 2
                dve.wait_ge(even_part, 4 + kt + 1)
                oc, os = PS[:, 2 * par, 256:512], PS[:, 2 * par + 1, 256:512]
                ec, es = tE[:, par, 0], tE[:, par, 1]
                own.step(dve.tensor_tensor(V2c[:, 0:256], oc, ec, ALU.add))
                own.step(dve.tensor_tensor(V2c[:, 256:512], ec, oc, ALU.subtract))
                own.step(dve.tensor_tensor(V2s[:, 0:256], os, es, ALU.add))
                dve.tensor_tensor(V2s[:, 256:512], os, es, ALU.subtract).then_inc(spec_rdy, 1)
                dve.wait_ge(spec_rdy, 4 + kt + 1)
                own.step(dve.tensor_tensor(t1, V2c, Fc[:, kt], ALU.mult))
                own.step(dve.tensor_tensor(t2, V2s, Fs[:, kt], ALU.mult))
                own.step(dve.tensor_tensor(t3, V2c, Fs[:, kt], ALU.mult))
                own.step(dve.tensor_tensor(t4, V2s, Fc[:, kt], ALU.mult))
                own.wait()
                own.step(dve.tensor_tensor(Yc, t1, t2, ALU.subtract))
                own.step(dve.tensor_tensor(Ys, t3, t4, ALU.add))
                own.wait()
                if kt >= 2:
                    dve.wait_ge(inv_mm, kt - 1)
                dve.tensor_tensor(G[:, par, 0], Yc[:, 0:256], Yc[:, 256:512], ALU.add)
                dve.tensor_tensor(G[:, par, 1], Ys[:, 0:256], Ys[:, 256:512], ALU.subtract)
                dve.tensor_tensor(G[:, par, 2], Yc[:, 0:256], Yc[:, 256:512], ALU.subtract)
                dve.tensor_tensor(G[:, par, 3], Ys[:, 0:256], Ys[:, 256:512], ALU.add).then_inc(G_rdy, 1)
                late(12 + kt)
            for i in range(2):
                lo_of(chunk_index("qkv", i), spl(2 + i, 4, 512))
            dve.wait_ge(late_mm, 4)
            dve.tensor_tensor(mod[:, 32:48, 0], PS[:, 3, 0:16], cols[:, V_BMOD + 32:V_BMOD + 48], ALU.add)\
                .then_inc(late_rdy, 1)
            dve.wait_ge(late_rdy, 2)
            modulation_gain(af, 32, V_GFFN, 1)
            dve.wait_ge(inv_mm, 4)
            for n in range(4):
                c2, odd = n // 2, n % 2
                if n >= 2:
                    dve.wait_ge(y_rdy, n - 1)
                skip = cols[:, V_SKIP + c2:V_SKIP + c2 + 1]
                own.step(dve.scalar_tensor_tensor(yo[:, n % 2], uvT[:, c2, odd::2], skip, PS[:, 4 + n],
                                                  ALU.mult, ALU.add))
                own.wait()
                dve.scalar_tensor_tensor(yo[:, n % 2], yo[:, n % 2], HS, x2T[:, c2, odd::2], ALU.mult, ALU.mult)\
                    .then_inc(y_f, 1)
                dve.wait_ge(y_hi, n + 1)
                dve.tensor_tensor(yT[:, 1, c2, odd::2], yo[:, n % 2], yT[:, 0, c2, odd::2], ALU.subtract)\
                    .then_inc(y_rdy, 1)

            def mean_square(u, it=0):
                (g, t), par, m = UNITS[u], u % 2, it * 2
                if g == 2:
                    return
                w = HQ if g == 0 else HKV
                dve.wait_ge(pr_sq, m + n_normed(u))
                own.step(dve.tensor_reduce(ssq[:, par, 0:w], bT[par][:, 0:w * HD].rearrange("p (h d) -> p h d", d=HD),
                                           AX, ALU.add))
                own.wait()
                dve.tensor_scalar(ssq[:, par, 0:w], ssq[:, par, 0:w], 1.0 / (HD * WS * WS), EPS, ALU.mult, ALU.add)\
                    .then_inc(pr_ms, 1)

            def rotate(u, it=0):
                (g, t), par, m = UNITS[u], u % 2, it * 2
                if g:
                    dve.wait_ge(pr_v, m + n_valued(u))
                    h0, nh, o = (0, 2, 128) if g == 1 else (2, 4, 256)
                    v = V[:, t + m, h0:h0 + nh]
                    dve.scalar_tensor_tensor(v[:, :, 1], PS[:, par, o:o + nh * HD].rearrange("p (h d) -> p h d", h=nh),
                                             VS / WS, v[:, :, 0], ALU.mult, ALU.subtract).then_inc(pr_vl, 1)
                if g == 2:
                    return
                w = HQ if g == 0 else HKV
                dve.wait_ge(pr_rs, m + n_normed(u))
                if u >= 2:
                    dve.wait_ge(pr_hi, m + u - 1)
                n = nT[par][:, 0:w * HD].rearrange("p (h d) -> p h d", d=HD)
                b = bT[par][:, 0:w * HD].rearrange("p (h d) -> p h d", d=HD)
                dve.tensor_tensor(n, PS[:, par, 0:w * HD].rearrange("p (h d) -> p h d", d=HD),
                                  rsq[:, par, 0:w].unsqueeze(2).broadcast_to((P, w, HD)), ALU.mult).then_inc(pr_n, 1)
                dve.wait_ge(pr_n, m + n_normed(u))
                if t >= NT:
                    dve.tensor_tensor(n, n, gkc.unsqueeze(1).broadcast_to((P, w, HD)), ALU.mult).then_inc(pr_r, 1)
                    return
                tab = (gc if g == 0 else gk)[:, t + m]

                def of(a, o, k):
                    return tab[:, a, o:o + k].unsqueeze(1).broadcast_to((P, w, k))

                own.step(dve.tensor_tensor(b[:, :, 0:32], n[:, :, 32:64], of(1, 0, 32), ALU.mult))
                own.step(dve.tensor_tensor(b[:, :, 32:64], n[:, :, 0:32], of(1, 32, 32), ALU.mult))
                own.wait()
                own.step(dve.tensor_tensor(n, n, of(0, 0, 64), ALU.mult))
                own.wait()
                dve.tensor_tensor(n, n, b, ALU.add).then_inc(pr_r, 1)

            def lo_parts(u, it=0):
                (g, t), par, m = UNITS[u], u % 2, it * 2
                dve.wait_ge(pr_hi, m + u + 1)
                for hi, lo, src in stacks(g, t, par):
                    ins = dve.tensor_tensor(lo, src, hi, ALU.subtract)
                ins.then_inc(pr_lo, 1)

            def slot(u, it=0):
                if u < NU:
                    mean_square(u, it)
                if 1 <= u <= NU:
                    lo_parts(u - 1, it)
                if u < NU:
                    rotate(u, it)

            for g in GROUPS:
                u0 = GROUP0[g]
                slot(u0)
                for b in range(2):
                    if b:
                        slot(u0 + 1)
                    if g == 1:
                        lo_of(chunk_index("qkv", 2 + b), spl(b, 4, 512))
                    elif g == 0:
                        lo_of(chunk_index("qkv", 4 + b), spl(2 + b, 4, 512))
                with dve.Fori(0, 3) as it:
                    own.enter(it, {1: 8, 2: 0, 0: 8}[g])
                    for b in range(2):
                        slot(u0 + 2 + b, it)
                    own.leave(3)
                if g:
                    slot(u0 + 8)
                    slot(u0 + 9)
            slot(NU)

            def maximum(u):
                dve.wait_ge(s_mm, u.n + 1)
                o, w = 1536 * u.par, (7 if u.na else 10) * P
                if u.na:
                    dve.wait_ge(bias_rdy, u.blk * 5 + 5)
                    b = bias[:, u.blk % 2, bias_kind(u.j)].rearrange("p i w -> p (i w)")
                    cm = cmax[:, u.par:u.par + 1]
                    own.step(dve.tensor_reduce(cm, PSf[:, o + 640:o + w], AX, ALU.max))
                    own.wait()
                    dve.tensor_tensor_reduce(PSf[:, o:o + 640], PSf[:, o:o + 640], b, 1.0, cm, ALU.add, ALU.max,
                                             accum_out=cm).then_inc(bias_add, 1)
                    return
                dve.tensor_reduce(nmax[:, u.par:u.par + 1], PSf[:, o:o + w], AX, ALU.max, negate=True)\
                    .then_inc(s_max, 1)

            def low_p(u):
                for b, t in enumerate(u.banks):
                    dve.wait_ge(pt_hi, u.turned(b))
                    o = u.turned_at(b)
                    dve.scalar_tensor_tensor(flat(PT[:, u.par, 1, t.start:t.stop]), PSf[:, o:o + len(t) * P], PSC,
                                             flat(PT[:, u.par, 0, t.start:t.stop]), ALU.mult, ALU.subtract)\
                        .then_inc(pt_lo, 1)

            def inverse_sum(u):
                dve.wait_ge(s_exp, u.n + 1)
                if u.v >= 2:
                    dve.wait_ge(o_rdy, u.n - 1)
                dve.reciprocal(rcp[:, u.par:u.par + 1], esum[:, u.v % 4:u.v % 4 + 1]).then_inc(rcp_rdy, 1)

            def attend(u):
                if u.v < NV - 1:
                    maximum(u.ahead(1))
                low_p(u)
                inverse_sum(u)

            maximum(Unit(0))
            for v in range(NNA + 1):
                attend(Unit(v))
            with dve.Fori(0, NT - 1) as it:
                for v in range(33, 41):
                    attend(Unit(v, it))
            for v in range(89, NV):
                attend(Unit(v))


            def residual(t):
                dve.wait_ge(wo_mm, t + 1)
                dve.scalar_tensor_tensor(wtmp[:, t % 2], PSf[:, 1024 * (t % 2):1024 * (t % 2) + 1024], 1 / WS, gate1,
                                         ALU.mult, ALU.mult).then_inc(x1_rdy, 1)
                dve.wait_ge(x1_rdy, t + 1)
                dve.tensor_tensor(x1[:, t], x1[:, t], wtmp[:, t % 2], ALU.add).then_inc(x1_sum, 1)

            def mean1(n):
                a, b = X1_PARTS[n]
                dve.wait_ge(sq1, b)
                dve.tensor_scalar(ss[:, a:b], ss[:, a:b], 1.0 / D, EPS, ALU.mult, ALU.add).then_inc(ms1, 1)

            def normalise1(n):
                dve.wait_ge(rs1, n + 1)
                if n:
                    dve.wait_ge(hT_mm, 20 + KD)
                for t in range(*X1_PARTS[n]):
                    ins = dve.tensor_scalar(xn1[:, t % 4], x1[:, t], rs[:, t:t + 1], None, ALU.mult)
                ins.then_inc(xn1_rdy, 1)

            def split_h1(n):
                f, o = n % KD, 512 * (n // KD)
                split_h(20 + n, h2tmp[:, n % 2], hT[:, 0, f, o:o + 512], hT[:, 1, f, o:o + 512])

            def low_mix(t):
                dve.wait_ge(mx_hi, t + 1)
                o, cut = 2048 + 1024 * (t % 2), slice(t * P, t * P + P)
                dve.scalar_tensor_tensor(mixT[:, 1, :, cut], PSf[:, o:o + 768].rearrange("p (f t) -> p f t", f=6),
                                         1 / (PSC * VS), mixT[:, 0, :, cut], ALU.mult, ALU.subtract).then_inc(mx_lo, 1)

            for t in range(4):
                low_mix(t)
            dve.wait_ge(gates_in, 32)
            dve.wait_ge(x1_in, 64)
            for t in range(NT):
                residual(t)
                if t == 0:
                    for i in range(4, NT):
                        low_mix(i)
                if 2 <= t < 4:
                    lo_of(chunk_index("fi", t - 2), fiS[t - 2])
                if t == 4:
                    mean1(0)
                if t == 5:
                    normalise1(0)
                    for n in range(4):
                        split_h1(n)
                if t == 6:
                    mean1(1)
                    for n in range(4, 8):
                        split_h1(n)
                    normalise1(1)
            mean1(2)
            normalise1(2)
            for n in range(8, 16):
                split_h1(n)

            def gated(b, j, first=False):
                dve.wait_ge(fi_s, j + 1)
                if not first:
                    dve.wait_ge(fi_lo, j)
                dve.scalar_tensor_tensor(pr, PSf[:, 2048 * b + 1024:2048 * b + 2048], GS / WS, sg, ALU.mult, ALU.mult)\
                    .then_inc(fi_p, 1)

            def gated_lo(j):
                dve.wait_ge(fi_hi, j + 1)
                dve.tensor_tensor(prodT[:, 1, j, :], pr, prodT[:, 0, j, :], ALU.subtract).then_inc(fi_lo, 1)

            c0 = chunk_index("fi", 0)
            for b in range(2):
                gated(b, b, b == 0)
                lo_of(c0 + 2 + b, fiS[b])
                gated_lo(b)
            with dve.Fori(0, KF // 2 - 2) as it:
                for b in range(2):
                    gated(b, it * 2 + 2 + b)
                    dve.wait_ge(split_hi, it * 2 + n_split(c0 + 4 + b))
                    dve.scalar_tensor_tensor(flat(fiS[b][:, 1]), f32(RAW(b), 2048), WS, flat(fiS[b][:, 0]),
                                             ALU.mult, ALU.subtract).then_inc(split_lo, 1)
                    gated_lo(it * 2 + 2 + b)
            c1 = chunk_index("fo", 0)

            def fo_gate(s, base_c, it=0):
                dve.wait_ge(raw_in[s], it * 8 + 16 * chunk_arrivals(base_c))
                w = f32(RAW(s), 2, D)
                dve.tensor_tensor(w, w, gate2.unsqueeze(1).broadcast_to((P, 2, D)), ALU.mult).then_inc(fo_gated, 1)

            for b in range(2):
                fo_gate(b, c1 + b)
                gated(b, KF - 2 + b)
                lo_of(chunk_index("fo", b), foS[b])
                gated_lo(KF - 2 + b)

            def fo_lo(s, base_c, it=0):
                fo_gate(s, base_c, it)
                dve.wait_ge(split_hi, it + n_split(base_c))
                dve.scalar_tensor_tensor(flat(foS[s][:, 1]), f32(RAW(s), 2048), WS, flat(foS[s][:, 0]),
                                         ALU.mult, ALU.subtract).then_inc(split_lo, 1)

            def gate_out(t):
                dve.wait_ge(fo_mm, t + 1)
                dve.tensor_tensor(x1[:, t], x1[:, t], PSf[:, 1024 * (t % 4):1024 * (t % 4) + 1024], ALU.add)\
                    .then_inc(fo_x, 1)

            def mean_out(t):
                dve.wait_ge(fo_sq, t + 1)
                dve.tensor_scalar(ss[:, t:t + 1], ss[:, t:t + 1], 1.0 / D, EPS, ALU.mult, ALU.add).then_inc(fo_ms, 1)

            def norm_out(t):
                dve.wait_ge(fo_rs, t + 1)
                dve.scalar_tensor_tensor(x1[:, t], x1[:, t], rs[:, t:t + 1], gfin, ALU.mult, ALU.mult).then_inc(fo_y, 1)

            with dve.Fori(0, 4) as it:
                for b in range(2):
                    fo_lo(b, c1 + 2 + b, it * 2)
            for m in (10, 11):
                fo_lo(m % 2, c1 + m)
            gate_out(0)
            gate_out(1)
            fo_lo(0, c1 + 12)
            gate_out(2)
            gate_out(3)
            dve.wait_ge(gf_in, 16)
            for t in range(4):
                mean_out(t)
                if t:
                    norm_out(t - 1)
            norm_out(3)
            with dve.Fori(0, 4) as it:
                for b in range(2):
                    fo_lo(1 - b, c1 + 13 + b, it * 2)
            fo_lo(1, c1 + 21)
            for t in range(4, NT):
                gate_out(t)
                if t > 4:
                    mean_out(t - 1)
                if t > 5:
                    norm_out(t - 2)
            mean_out(NT - 1)
            norm_out(NT - 2)
            norm_out(NT - 1)


INPUTS = ["x", "c", "ctx", "c_ctx", "w_mod", "b_mod", "g_mix", "g_ffn", "w_in", "w_out", "hy_conv_w", "hy_conv_b",
          "hy_f_w1", "hy_f_b1", "hy_f_w2", "hy_f_b2", "hy_f_w3", "hy_f_b3", "hy_f_wout", "hy_f_freq", "hy_skip",
          "qk_g_q", "qk_g_k", "na_rpb", "w_ffn_in", "w_ffn_out", "g_final"]


def kernel(**inputs):
    import concourse.bacc as bacc
    from concourse.bass_utils import run_bass_kernel_spmd

    nc = bacc.Bacc("TRN2", target_bir_lowering=False, num_devices=1)
    tables = constants()
    arrays = {"in_" + n: np.ascontiguousarray(inputs[n]) for n in INPUTS} | tables
    dram = {n: nc.dram_tensor(n, a.shape, mybir.dt.from_np(a.dtype), kind="ExternalInput").ap()
            for n, a in arrays.items()}
    out = nc.dram_tensor("out", (1, S, D), F32, kind="ExternalOutput").ap()
    build(nc, {n: dram["in_" + n] for n in INPUTS}, {n[4:]: dram[n] for n in tables}, out)
    return run_bass_kernel_spmd(nc, [arrays], core_ids=[0]).results[0]["out"]
```
